# Optimizing a Trainium2 kernel written in Bass

```python
import jax, jax.numpy as jnp
from jax import lax
import numpy as np
import math

D_MODEL = 1024
BATCH = 1
SEQ = 256
DEPTH = 2

HEAD_DIM = 64
N_SB = 6
N_DSA = 6
N_IDX = 8
IDX_DIM = 64
TOPK_MAX = 256
N_HG = 4
HG_DK = 128
HG_DV = 64
D_FF = 4 * D_MODEL
ROPE_THETA = 500000.0
ROT_DIM = HEAD_DIM // 4
Q_BLOCK = 128
HG_CHUNK = 64
EPS = 1e-6
F_MIN = 1e-12
NEG = -1e30
W_SB = N_SB * HEAD_DIM
W_DSA = N_DSA * HEAD_DIM
W_HF = N_HG * HG_DK
W_HV = N_HG * HG_DV
IDX_SCALE = (IDX_DIM * N_IDX) ** -0.5
SPLITS = (W_SB, W_SB, W_SB,
          W_DSA, HEAD_DIM, HEAD_DIM,
          N_IDX * IDX_DIM, IDX_DIM, N_IDX,
          W_HF, W_HF, W_HV, W_HV,
          D_MODEL, D_MODEL, D_MODEL)
D_IN = sum(SPLITS)


def _split_points():
    return [int(v) for v in np.cumsum(np.array(SPLITS))[:-1]]

def rms_norm(x, gain):
    xf = x.astype(jnp.float32)
    y = xf * lax.rsqrt(jnp.mean(xf * xf, axis=-1, keepdims=True) + EPS)
    return (y * gain.astype(jnp.float32)).astype(x.dtype)

def partial_rope(x, pos):
    half = ROT_DIM // 2
    inv = ROPE_THETA ** (-(jnp.arange(half, dtype=jnp.float32) * 2.0) / ROT_DIM)
    ang = pos.astype(jnp.float32)[:, None] * inv[None, :]
    cos = jnp.cos(ang)[None, :, None, :]
    sin = jnp.sin(ang)[None, :, None, :]
    xr = x[..., :ROT_DIM].astype(jnp.float32)
    x1, x2 = xr[..., :half], xr[..., half:]
    rot = jnp.concatenate([x1 * cos - x2 * sin, x2 * cos + x1 * sin], axis=-1).astype(x.dtype)
    return jnp.concatenate([rot, x[..., ROT_DIM:]], axis=-1)

def stick_breaking_attention(q, k, v):
    B, T, H, D = q.shape
    scale = D ** -0.5
    outs = []
    for blk in range(T // Q_BLOCK):
        q0, q1 = blk * Q_BLOCK, (blk + 1) * Q_BLOCK
        z = jnp.einsum('bqhd,bkhd->bhqk', q[:, q0:q1], k[:, :q1]).astype(jnp.float32) * scale
        t_pos = q0 + jnp.arange(Q_BLOCK)[:, None]
        s_pos = jnp.arange(q1)[None, :]
        past = s_pos < t_pos
        log_1m = jnp.where(past, jax.nn.log_sigmoid(-z), 0.0)
        later = lax.cumsum(log_1m, axis=3, reverse=True) - log_1m
        log_a = jnp.where(past, jax.nn.log_sigmoid(z) + later, NEG)
        a = jnp.exp(log_a)
        outs.append(jnp.einsum('bhqk,bkhd->bqhd', a.astype(v.dtype), v[:, :q1]))
    return jnp.concatenate(outs, axis=1)

def dsa_attention(q, k, v, q_idx, k_idx, w_idx):
    B, T, H, D = q.shape
    k_top = min(TOPK_MAX, T // 4)
    gather = jax.vmap(lambda arr, idx: arr[idx])
    outs = []
    for blk in range(T // Q_BLOCK):
        q0, q1 = blk * Q_BLOCK, (blk + 1) * Q_BLOCK
        kl = min(T, max(q1, k_top))
        rel = jax.nn.relu(jnp.einsum('bqjd,bkd->bqjk', q_idx[:, q0:q1], k_idx[:, :kl]).astype(jnp.float32))
        score = jnp.einsum('bqj,bqjk->bqk', w_idx[:, q0:q1].astype(jnp.float32) * IDX_SCALE, rel)
        t_pos = q0 + jnp.arange(Q_BLOCK)[:, None]
        s_pos = jnp.arange(kl)[None, :]
        score = jnp.where(s_pos <= t_pos, score, NEG)
        top_score, top_idx = lax.top_k(score, k_top)
        k_sel = gather(k, top_idx)
        v_sel = gather(v, top_idx)
        logits = jnp.einsum('bqhd,bqkd->bhqk', q[:, q0:q1], k_sel).astype(jnp.float32) * (D ** -0.5)
        valid = (top_score > 0.5 * NEG)[:, None]
        logits = jnp.where(valid, logits, NEG)
        p = jax.nn.softmax(logits, axis=-1)
        outs.append(jnp.einsum('bhqk,bqkd->bqhd', p.astype(v.dtype), v_sel))
    return jnp.concatenate(outs, axis=1)

def hgrn2(q, f_pre, inp, lb):
    B, T, H, DK = q.shape
    DV = inp.shape[-1]
    C = HG_CHUNK
    N = T // C
    q = jax.nn.silu(q.astype(jnp.float32))
    lb = lb.astype(jnp.float32)
    f = lb + (1.0 - lb) * jax.nn.sigmoid(f_pre.astype(jnp.float32))
    log_f = jnp.log(jnp.maximum(f, F_MIN))
    k = 1.0 - f

    def to_chunks(a):
        return a.reshape(B, N, C, H, a.shape[-1]).transpose(1, 0, 3, 2, 4)

    qc, kc, vc, gc = (to_chunks(a) for a in (q, k, inp.astype(jnp.float32), log_f))
    causal = jnp.tril(jnp.ones((C, C), dtype=bool))[:, :, None]

    def step(S, xs):
        qt, kt, vt, gt = xs
        b = jnp.cumsum(gt, axis=2)
        diff = b[:, :, :, None, :] - b[:, :, None, :, :]
        decay = jnp.exp(jnp.where(causal, diff, NEG))
        att = jnp.einsum('bhtk,bhsk,bhtsk->bhts', qt, kt, decay)
        o = jnp.einsum('bhts,bhsv->bhtv', att, vt) + jnp.einsum('bhtk,bhkv->bhtv', qt * jnp.exp(b), S)
        b_last = b[:, :, -1:, :]
        S = S * jnp.exp(b_last[:, :, 0, :, None]) + jnp.einsum('bhsk,bhsv->bhkv', kt * jnp.exp(b_last - b), vt)
        return S, o

    S0 = jnp.zeros((B, H, DK, DV), jnp.float32)
    _, o = lax.scan(step, S0, (qc, kc, vc, gc))
    return o.transpose(1, 0, 3, 2, 4).reshape(B, T, H, DV).astype(inp.dtype)

def hybrid_mixer(h, w_in_l, qn, kn, lb, onorm, w_sb_l, w_dsa_l, w_hg_l, w_out_l):
    B, T, _ = h.shape
    pos = jnp.arange(T)
    (sq, sk, sv, dq, dk, dv, iq, ik, iw, hq, hf, hi, hg,
     g_sb, g_dsa, g_hg) = jnp.split(h @ w_in_l, _split_points(), axis=-1)
    heads = lambda a, n: a.reshape(B, T, n, -1)
    y_sb = stick_breaking_attention(heads(sq, N_SB), heads(sk, N_SB), heads(sv, N_SB)).reshape(B, T, W_SB) @ w_sb_l
    q = partial_rope(rms_norm(heads(dq, N_DSA), qn), pos)
    k = partial_rope(rms_norm(dk[:, :, None, :], kn), pos)[:, :, 0]
    q_i = partial_rope(heads(iq, N_IDX), pos)
    k_i = partial_rope(ik[:, :, None, :], pos)[:, :, 0]
    y_dsa = dsa_attention(q, k, dv, q_i, k_i, iw).reshape(B, T, W_DSA) @ w_dsa_l
    o = hgrn2(heads(hq, N_HG), heads(hf, N_HG), heads(hi, N_HG), lb.reshape(N_HG, HG_DK))
    o = rms_norm(o, onorm) * jax.nn.silu(heads(hg, N_HG))
    y_hg = o.reshape(B, T, W_HV) @ w_hg_l
    mixed = jax.nn.sigmoid(g_sb) * y_sb + jax.nn.sigmoid(g_dsa) * y_dsa + jax.nn.sigmoid(g_hg) * y_hg
    return mixed @ w_out_l

def first_inputs(seed: int = 0) -> dict:
    key = jax.random.key(seed)
    ks = jax.random.split(key, 16)
    f32 = jnp.float32
    res = (2 * DEPTH) ** -0.5

    def nrm(k, shape, fan_in, g=1.0):
        return jax.random.normal(k, shape, f32) * (g * fan_in ** -0.5)

    def gain(k, shape):
        return 1.0 + 0.02 * jax.random.normal(k, shape, f32)

    return {
        'x': jax.random.normal(ks[0], (BATCH, SEQ, D_MODEL), f32),
        'norm_mix': gain(ks[1], (DEPTH, D_MODEL)),
        'w_in': nrm(ks[2], (DEPTH, D_MODEL, D_IN), D_MODEL),
        'qn_dsa': gain(ks[3], (DEPTH, HEAD_DIM)),
        'kn_dsa': gain(ks[4], (DEPTH, HEAD_DIM)),
        'hgrn_lb': 0.5 * jax.random.normal(ks[5], (DEPTH, W_HF), f32),
        'hgrn_onorm': gain(ks[6], (DEPTH, HG_DV)),
        'w_br_sb': nrm(ks[7], (DEPTH, W_SB, D_MODEL), W_SB),
        'w_br_dsa': nrm(ks[8], (DEPTH, W_DSA, D_MODEL), W_DSA),
        'w_br_hgrn': nrm(ks[9], (DEPTH, W_HV, D_MODEL), W_HV),
        'w_out': nrm(ks[10], (DEPTH, D_MODEL, D_MODEL), D_MODEL, res),
        'norm_mlp': gain(ks[11], (DEPTH, D_MODEL)),
        'w_up': nrm(ks[12], (DEPTH, D_MODEL, D_FF), D_MODEL),
        'w_down': nrm(ks[13], (DEPTH, D_FF, D_MODEL), D_FF, res),
    }

def first_block(x, norm_mix, w_in, qn_dsa, kn_dsa, hgrn_lb, hgrn_onorm, w_br_sb, w_br_dsa,
              w_br_hgrn, w_out, norm_mlp, w_up, w_down):
    p_lb = jax.nn.softmax(hgrn_lb.astype(jnp.float32), axis=0)
    lbs = jnp.cumsum(p_lb, axis=0) - p_lb[0:1]
    for l in range(DEPTH):
        h = rms_norm(x, norm_mix[l])
        x = x + hybrid_mixer(h, w_in[l], qn_dsa[l], kn_dsa[l], lbs[l], hgrn_onorm[l],
                             w_br_sb[l], w_br_dsa[l], w_br_hgrn[l], w_out[l])
        h2 = rms_norm(x, norm_mlp[l])
        x = x + jnp.square(jax.nn.relu(h2 @ w_up[l])) @ w_down[l]
    return x


N_MIXERS = 2
N_HY_LAYERS = (DEPTH + 1) // 2
N_AT_LAYERS = DEPTH // 2
D_MIX = D_MODEL
MEM_LEN = 256
MEM_HEADS = 4
D_MEM = MEM_HEADS * HEAD_DIM
D_MAIN = D_MIX - D_MEM
N_Q_HEADS = D_MAIN // HEAD_DIM
N_KV_HEADS = 4
GQA_GROUP = N_Q_HEADS // N_KV_HEADS
GRID_W = 64
ROPE_THETA_2 = 10000.0
ROPE_AXIS_DIM = HEAD_DIM // 2
HY_ORDER = 2
HY_SHORT = 3
HY_BANDS = 16
HY_EMB = 1 + 2 * HY_BANDS
HY_FILT = 64
HY_DECAY_TARGET = 1e-2
HY_FAST_PCT = 0.3
HY_SLOW_PCT = 1.5
N_EXPERTS = 16
EC_CAPACITY_FACTOR = 2
EXPERT_FF = 768
NORM_EPS = 1e-6
D_IN_HY = 3 * D_MAIN + D_MEM
D_IN_AT = D_MAIN + 2 * N_KV_HEADS * HEAD_DIM + D_MEM


def rms_norm_2(x, g):
    xf = x.astype(jnp.float32)
    y = xf * lax.rsqrt(jnp.mean(xf * xf, axis=-1, keepdims=True) + NORM_EPS)
    return (y * g.astype(jnp.float32)).astype(x.dtype)

def hyena_filters(L, w1, b1, w2, b2, w3, freq):
    f32 = jnp.float32
    t = jnp.linspace(0.0, 1.0, L, dtype=f32)[:, None]
    w = (2.0 * math.pi) * jnp.arange(L, dtype=f32)[:, None] / L
    bands = jnp.linspace(1e-4, HY_BANDS - 1, HY_BANDS, dtype=f32)[None, :]
    feats = jnp.concatenate([t, jnp.cos(bands * w), -jnp.sin(bands * w)], axis=-1)
    fr = freq.astype(f32)
    h = jnp.sin(fr * (feats @ w1.astype(f32) + b1.astype(f32)))
    h = jnp.sin(fr * (h @ w2.astype(f32) + b2.astype(f32)))
    h = (h @ w3.astype(f32)).reshape(L, HY_ORDER, 2, D_MAIN)
    max_decay = math.log(HY_DECAY_TARGET) / HY_FAST_PCT
    min_decay = math.log(HY_DECAY_TARGET) / HY_SLOW_PCT
    deltas = jnp.linspace(min_decay, max_decay, D_MAIN, dtype=f32)
    h = h * jnp.exp(-t[:, :, None, None] * jnp.abs(deltas))
    h = h / (jnp.sum(jnp.abs(h), axis=(0, 2), keepdims=True) + 1e-6)
    hf, hb = h[:, :, 0], h[:, :, 1]
    zero = jnp.zeros_like(hf[:1])
    return jnp.concatenate([hf[:1] + hb[:1], hf[1:], zero, hb[1:][::-1]], axis=0)

def long_conv(z, k_fft):
    T = z.shape[1]
    Z = jnp.fft.rfft(z, n=2 * T, axis=1)
    return jnp.fft.irfft(Z * k_fft[None], n=2 * T, axis=1)[:, :T]

def hyena_mixer(u, short_w, k_fft, skip):
    T = u.shape[1]
    pad = HY_SHORT // 2
    up = jnp.pad(u, ((0, 0), (pad, pad), (0, 0)))
    uc = sum(up[:, j:j + T] * short_w[j] for j in range(HY_SHORT))
    x1, x2, v = jnp.split(uc, 3, axis=-1)
    z = v.astype(jnp.float32)
    for o, gate in enumerate((x1, x2)):
        z = gate.astype(jnp.float32) * (long_conv(z, k_fft[:, o]) + skip[o].astype(jnp.float32) * z)
    return z.astype(u.dtype)

def axial_rope_tables(T):
    rows = T // GRID_W
    pos_row = jnp.repeat(jnp.arange(rows), GRID_W).astype(jnp.float32)
    pos_col = jnp.tile(jnp.arange(GRID_W), rows).astype(jnp.float32)
    inv = 1.0 / (ROPE_THETA_2 ** (jnp.arange(0, ROPE_AXIS_DIM, 2, dtype=jnp.float32) / ROPE_AXIS_DIM))
    ang = jnp.stack([pos_row[:, None] * inv, pos_col[:, None] * inv], axis=1)
    return jnp.cos(ang), jnp.sin(ang)

def apply_axial_rope(x, cos, sin):
    B, T, H, Dh = x.shape
    nf = ROPE_AXIS_DIM // 2
    xr = x.astype(jnp.float32).reshape(B, T, H, 2, 2, nf)
    c = cos[None, :, None]
    s = sin[None, :, None]
    xa, xb = xr[..., 0, :], xr[..., 1, :]
    out = jnp.stack([xa * c - xb * s, xa * s + xb * c], axis=-2)
    return out.reshape(B, T, H, Dh).astype(x.dtype)

def blocked_gqa(q, k, v):
    B, T, Hq, Dh = q.shape
    nb = T // Q_BLOCK
    qb = q.reshape(B, nb, Q_BLOCK, N_KV_HEADS, GQA_GROUP, Dh).transpose(1, 0, 2, 3, 4, 5)
    scale = Dh ** -0.5

    def one_block(qblk):
        s = jnp.einsum('bqhgd,bkhd->bhgqk', qblk, k).astype(jnp.float32) * scale
        p = jax.nn.softmax(s, axis=-1).astype(v.dtype)
        return jnp.einsum('bhgqk,bkhd->bqhgd', p, v)

    o = lax.map(one_block, qb)
    return o.transpose(1, 0, 2, 3, 4, 5).reshape(B, T, Hq * Dh)

def memory_cross_attn(cq, mem_n, w_kv):
    B, T, _ = cq.shape
    M = mem_n.shape[1]
    q = cq.reshape(B, T, MEM_HEADS, HEAD_DIM)
    mk, mv = jnp.split(mem_n @ w_kv, 2, axis=-1)
    mk = mk.reshape(B, M, MEM_HEADS, HEAD_DIM)
    mv = mv.reshape(B, M, MEM_HEADS, HEAD_DIM)
    s = jnp.einsum('bqhd,bmhd->bhqm', q, mk).astype(jnp.float32) * (HEAD_DIM ** -0.5)
    p = jax.nn.softmax(s, axis=-1).astype(mv.dtype)
    return jnp.einsum('bhqm,bmhd->bqhd', p, mv).reshape(B, T, D_MEM)

def expert_choice_ffn(xn, w_router, w_gate, w_up, w_down):
    B, T, D = xn.shape
    cap = EC_CAPACITY_FACTOR * T // N_EXPERTS
    aff = jax.nn.softmax((xn @ w_router).astype(jnp.float32), axis=-1)
    g, idx = lax.top_k(jnp.swapaxes(aff, 1, 2), cap)
    bidx = jnp.arange(B)[:, None, None]
    xg = xn[bidx, idx]
    hid = jax.nn.silu(jnp.einsum('becd,edf->becf', xg, w_gate)) * jnp.einsum('becd,edf->becf', xg, w_up)
    y = jnp.einsum('becf,efd->becd', hid, w_down) * g[..., None].astype(xn.dtype)
    return jnp.zeros_like(xn).at[bidx, idx].add(y)

def second_inputs(seed: int = 0) -> dict:
    key = jax.random.key(seed)
    ks = iter(jax.random.split(key, 32))

    def nrm(shape, scale):
        return jax.random.normal(next(ks), shape, jnp.float32) * scale

    def gain(shape):
        return 1.0 + nrm(shape, 0.02)

    D = D_MODEL
    return {
        'x': nrm((BATCH, SEQ, D), 1.0),
        'mem': nrm((BATCH, MEM_LEN, D), 1.0),
        'mix_norm_g': gain((DEPTH, D)),
        'ffn_norm_g': gain((DEPTH, D)),
        'mem_norm_g': gain((D,)),
        'final_norm_g': gain((D,)),
        'w_mem_kv': nrm((DEPTH, D, 2 * D_MEM), D ** -0.5),
        'w_out': nrm((DEPTH, D_MIX, D), D_MIX ** -0.5),
        'hy_w_in': nrm((N_HY_LAYERS, D, D_IN_HY), D ** -0.5),
        'hy_short_w': nrm((N_HY_LAYERS, HY_SHORT, 3 * D_MAIN), HY_SHORT ** -0.5),
        'hy_filt_w1': nrm((N_HY_LAYERS, HY_EMB, HY_FILT), HY_EMB ** -0.5),
        'hy_filt_b1': nrm((N_HY_LAYERS, HY_FILT), 0.02),
        'hy_filt_w2': nrm((N_HY_LAYERS, HY_FILT, HY_FILT), HY_FILT ** -0.5),
        'hy_filt_b2': nrm((N_HY_LAYERS, HY_FILT), 0.02),
        'hy_filt_w3': nrm((N_HY_LAYERS, HY_FILT, HY_ORDER * 2 * D_MAIN), HY_FILT ** -0.5),
        'hy_filt_freq': gain((N_HY_LAYERS, HY_FILT)),
        'hy_skip': nrm((N_HY_LAYERS, HY_ORDER, D_MAIN), 1.0),
        'at_w_in': nrm((N_AT_LAYERS, D, D_IN_AT), D ** -0.5),
        'at_q_norm_g': gain((N_AT_LAYERS, HEAD_DIM)),
        'at_k_norm_g': gain((N_AT_LAYERS, HEAD_DIM)),
        'router_w': nrm((DEPTH, D, N_EXPERTS), D ** -0.5),
        'exp_w_gate': nrm((DEPTH, N_EXPERTS, D, EXPERT_FF), D ** -0.5),
        'exp_w_up': nrm((DEPTH, N_EXPERTS, D, EXPERT_FF), D ** -0.5),
        'exp_w_down': nrm((DEPTH, N_EXPERTS, EXPERT_FF, D), EXPERT_FF ** -0.5),
    }

def second_block(x, mem, mix_norm_g, ffn_norm_g, mem_norm_g, final_norm_g, w_mem_kv, w_out,
              hy_w_in, hy_short_w, hy_filt_w1, hy_filt_b1, hy_filt_w2, hy_filt_b2, hy_filt_w3,
              hy_filt_freq, hy_skip, at_w_in, at_q_norm_g, at_k_norm_g,
              router_w, exp_w_gate, exp_w_up, exp_w_down):
    B, T, _ = x.shape
    cos, sin = axial_rope_tables(T)
    mem_n = rms_norm_2(mem, mem_norm_g)
    h = x
    for i in range(DEPTH):
        j = i // N_MIXERS
        u = rms_norm_2(h, mix_norm_g[i])
        if i % N_MIXERS == 0:
            proj = u @ hy_w_in[j]
            main_in, cq = proj[..., :3 * D_MAIN], proj[..., 3 * D_MAIN:]
            k_taps = hyena_filters(T, hy_filt_w1[j], hy_filt_b1[j], hy_filt_w2[j], hy_filt_b2[j],
                                   hy_filt_w3[j], hy_filt_freq[j])
            k_fft = jnp.fft.rfft(k_taps, axis=0)
            main = hyena_mixer(main_in, hy_short_w[j], k_fft, hy_skip[j])
        else:
            proj = u @ at_w_in[j]
            o1 = D_MAIN
            o2 = o1 + N_KV_HEADS * HEAD_DIM
            o3 = o2 + N_KV_HEADS * HEAD_DIM
            q = proj[..., :o1].reshape(B, T, N_Q_HEADS, HEAD_DIM)
            kk = proj[..., o1:o2].reshape(B, T, N_KV_HEADS, HEAD_DIM)
            vv = proj[..., o2:o3].reshape(B, T, N_KV_HEADS, HEAD_DIM)
            cq = proj[..., o3:]
            q = apply_axial_rope(rms_norm_2(q, at_q_norm_g[j]), cos, sin)
            kk = apply_axial_rope(rms_norm_2(kk, at_k_norm_g[j]), cos, sin)
            main = blocked_gqa(q, kk, vv)
        cross = memory_cross_attn(cq, mem_n, w_mem_kv[i])
        h = h + jnp.concatenate([main, cross], axis=-1) @ w_out[i]
        h = h + expert_choice_ffn(rms_norm_2(h, ffn_norm_g[i]), router_w[i],
                                  exp_w_gate[i], exp_w_up[i], exp_w_down[i])
    return rms_norm_2(h, final_norm_g)


def setup_inputs(seed=0):
    out = dict(first_inputs(seed))
    for name, value in second_inputs(seed + 1).items():
        if name != "x":
            out[name + "_2"] = value
    return out


def reference(
    x, norm_mix, w_in, qn_dsa, kn_dsa, hgrn_lb, hgrn_onorm, w_br_sb, w_br_dsa, w_br_hgrn, w_out,
    norm_mlp, w_up, w_down, mem_2, mix_norm_g_2, ffn_norm_g_2, mem_norm_g_2, final_norm_g_2,
    w_mem_kv_2, w_out_2, hy_w_in_2, hy_short_w_2, hy_filt_w1_2, hy_filt_b1_2, hy_filt_w2_2,
    hy_filt_b2_2, hy_filt_w3_2, hy_filt_freq_2, hy_skip_2, at_w_in_2, at_q_norm_g_2,
    at_k_norm_g_2, router_w_2, exp_w_gate_2, exp_w_up_2, exp_w_down_2,
):
    x = first_block(
        x, norm_mix, w_in, qn_dsa, kn_dsa, hgrn_lb, hgrn_onorm, w_br_sb, w_br_dsa, w_br_hgrn,
        w_out, norm_mlp, w_up, w_down,
    )
    return second_block(
        x, mem_2, mix_norm_g_2, ffn_norm_g_2, mem_norm_g_2, final_norm_g_2, w_mem_kv_2, w_out_2,
        hy_w_in_2, hy_short_w_2, hy_filt_w1_2, hy_filt_b1_2, hy_filt_w2_2, hy_filt_b2_2,
        hy_filt_w3_2, hy_filt_freq_2, hy_skip_2, at_w_in_2, at_q_norm_g_2, at_k_norm_g_2,
        router_w_2, exp_w_gate_2, exp_w_up_2, exp_w_down_2,
    )


_drawn_inputs = setup_inputs


def setup_inputs(seed=0):
    import zlib

    import numpy as np

    out = dict(_drawn_inputs(seed))
    spreads = {}
    factors = {'qn_dsa': 8.0,
     'kn_dsa': 8.0,
     'hgrn_lb': 3.936,
     'hgrn_onorm': 5.246,
     'ffn_norm_g_2': 3.47,
     'mem_norm_g_2': 8.0,
     'final_norm_g_2': 2.868,
     'hy_filt_b1_2': 5.543,
     'hy_filt_b2_2': 7.032,
     'hy_filt_freq_2': 8.0,
     'at_q_norm_g_2': 8.0,
     'at_k_norm_g_2': 8.0}
    for name, (base, spread) in spreads.items():
        noise = np.random.default_rng([zlib.crc32(name.encode()), seed]).standard_normal(out[name].shape)
        drawn = base * np.exp(spread * noise) if base else spread * noise
        out[name] = __import__('jax').numpy.asarray(drawn.astype(out[name].dtype))
    for name, factor in factors.items():
        out[name] = (out[name] * factor).astype(out[name].dtype)
    return out
```

```python
import math
from contextlib import ExitStack, contextmanager

import numpy as np

import concourse.bass as bass
from concourse import mybir

F32 = mybir.dt.float32
I32 = mybir.dt.int32
ALU = mybir.AluOpType
ACT = mybir.ActivationFunctionType
AX = mybir.AxisListType.X

P = 128
T = 256
NT = T // P
D = 1024
ND = D // P
DEPTH = 2
HD = 64
EPS = 1e-6
NEG = -1e30
N_SB = N_DSA = 6
N_IDX = 8
K_TOP = min(256, T // 4)
N_HG = 4
HG_DK = 128
D_FF = 4 * D
ROT = HD // 4
F_MIN = 1e-12
IDX_SCALE = (HD * N_IDX) ** -0.5
C_SQ, C_SK, C_SV = 0, 384, 768
C_DSA = 1152
W_DSA = 384 + 64 + 64 + 512 + 64 + 8
C_HQ = C_DSA + W_DSA
C_HI = C_HQ + 1024
C_GATE = C_HI + 512
D_IN = C_GATE + 3 * D
NBLK = 17
HG_LEVELS = (128, 64, 32, 16, 8, 4, 2, 1)
MASKED = (16, 8, 4, 2, 1, 0)
D_MAIN = 768
NM = D_MAIN // P
N_QH, N_KV, N_MEM = 12, 4, 4
N_EXP = 16
CAP = 2 * T // N_EXP
E_FF = 768
N_FEAT = 33
FILT = 64
ORD = 2
NC2 = ORD * D_MAIN
SLOTS = 6
SLOT = 3072
TINY = -3.0e38


class Counter:

    def __init__(self, prog, name, start=0):
        self.prog, self.name, self.count = prog, name, start
        self.sem = prog.nc.alloc_semaphore(name)
        prog.counters.append(self)

    def mark(self):
        return Mark(self, self.count, self.prog.loop)


class Mark:

    def __init__(self, counter, count, loop):
        self.counter, self.count, self.loop = counter, count, loop

    def value(self):
        loop = self.loop
        if loop is None:
            return self.count
        per = loop.per.get(self.counter.name, 0)
        if loop.closed:
            return self.count + (loop.n - 1) * per
        return loop.reg * per + self.count if per else self.count


class Loop:
    def __init__(self, name, n, per):
        self.name, self.n, self.per, self.closed, self.reg = name, n, per, False, None


class Engine:

    def __init__(self, prog, eng, name):
        self.prog, self.eng, self.name = prog, eng, name
        self.sig = Counter(prog, "s_" + name)
        self.seen = {}

    def __call__(self, *marks):
        for m in marks:
            if m is None:
                continue
            key = m.counter.name
            if m.loop is not None and m.loop.closed:
                m = Mark(m.counter, m.value(), None)
            got = self.seen.get((key, m.loop), -1)
            if got >= m.count:
                continue
            self.seen[(key, m.loop)] = m.count
            self.eng.wait_ge(m.counter.sem, m.value())
        return self.eng

    def done(self, inst, counter=None):
        s = counter or self.sig
        inst.then_inc(s.sem, 1)
        s.count += 1
        return s.mark()

    @property
    def last(self):
        return self.sig.mark()


class Program:

    def __init__(self, nc, per_iteration):
        self.nc, self.loop, self.counters = nc, None, []
        self.per_iteration = per_iteration
        self.pe = Engine(self, nc.tensor, "pe")
        self.act = Engine(self, nc.scalar, "act")
        self.dve = Engine(self, nc.vector, "dve")
        self.pool = Engine(self, nc.gpsimd, "pool")
        self.sp = Engine(self, nc.sync, "sp")
        self.engines = (self.pe, self.act, self.dve, self.pool)
        self.used = Counter(self, "used", SLOTS)
        nc.tensor.sem_inc(self.used.sem, SLOTS)
        self.landed = [Counter(self, f"landed{i}") for i in range(SLOTS)]
        self.ring = nc.alloc_sbuf_tensor("ring", [P, SLOTS, SLOT], F32)
        self.units = self.units_used = 0
        self.psum = nc.alloc_psum_tensor("psum", [P, 4, 2, 512], F32)
        self.free_marks = [[] for _ in range(4)]
        self.free_order = [0, 1, 2, 3]

    def meet(self):
        marks = [e.sig.mark() for e in self.engines] + [self.used.mark()]
        for e in self.engines:
            e(*[m for m in marks if m.count])
        self.free_marks = [[] for _ in range(4)]

    @contextmanager
    def loop_of(self, name, n):
        loop = Loop(name, n, self.per_iteration.get(name, {}))
        start = {s.name: s.count for s in self.counters}
        with self.nc.Fori(0, n) as i:
            loop.reg = i
            self.loop = loop
            self.meet()
            yield i
        self.loop = None
        gave = {s.name: s.count - start.get(s.name, 0) for s in self.counters}
        gave = {k: v for k, v in gave.items() if v}
        if name in self.per_iteration:
            assert gave == self.per_iteration[name]
        self.per_iteration[name] = gave
        loop.per, loop.closed = gave, True
        for s in self.counters:
            s.count += (n - 1) * gave.get(s.name, 0)
        self.units_used += (n - 1) * gave.get("used", 0)

    def dma(self, engine, name, pairs, *after):
        s = Counter(self, f"in_{name}")
        engine(*after)
        for to, of in pairs:
            engine.eng.dma_start(to, of).then_inc(s.sem, 16)
            s.count += 16
        return s.mark()

    def unit(self, src, rows, cols):
        slot = self.units % SLOTS
        need = Mark(self.used, self.units_used + 1, self.loop)
        self.sp(need)
        s = self.landed[slot]
        view = self.ring[:, slot, 0:rows * cols].rearrange("p (c n) -> p c n", c=rows)
        self.nc.sync.dma_start(view, src.rearrange("(c p) n -> p c n", p=P)).then_inc(s.sem, 16)
        s.count += 16
        self.units += 1
        self.units_used += 1
        return view, s.mark()

    def take(self):
        i = self.free_order.pop(0)
        self.pe(*self.free_marks[i])
        return i, self.psum[:, i, :, :]

    def give(self, i, *marks):
        self.free_marks[i] = list(marks)
        self.free_order.append(i)


class Kernel:

    def __init__(self, nc, per_iteration, ins, consts, out):
        self.nc, self.ins, self.c, self.out = nc, ins, consts, out
        self.prog = Program(nc, per_iteration)
        p = self.prog
        self.PE, self.A, self.V, self.G = p.pe, p.act, p.dve, p.pool
        self.room, self.names = ExitStack(), {}

    def sb(self, name, shape, dt=F32):
        self.names[name] = self.names.get(name, 0) + 1
        name += f"_{self.names[name]}" if self.names[name] > 1 else ""
        return self.room.enter_context(self.nc.sbuf_tensor(name, shape, dt))

    def flat(self, t):
        return t[:, :, :].rearrange("p a b -> p (a b)")

    @contextmanager
    def scope(self):
        outer = self.room
        with ExitStack() as self.room:
            yield
            self.prog.meet()
        self.room = outer


    def rstd(self, ss, n, out, after):
        V, A = self.V, self.A
        V(after)
        m = V.done(V.eng.tensor_scalar(out, ss, 1.0 / n, EPS, ALU.mult, ALU.add))
        A(m)
        m = A.done(A.eng.activation(out, out, ACT.Sqrt))
        V(m)
        return V.done(V.eng.reciprocal(out, out))

    def normed_rows(self, x, xn, *after):
        V, A = self.V, self.A
        A(*after)
        V(*after)
        for tt in range(NT):
            m = A.done(A.eng.activation(xn[:, tt, :], x[:, tt, :], ACT.Square,
                                        accum_out=self.ss[:, tt:tt + 1]))
        m = self.rstd(self.ss[:, 0:NT], D, self.rs[:, 0:NT], m)
        A(m)
        V(m)
        ma = A.done(A.eng.activation(xn[:, 0, :], x[:, 0, :], ACT.Copy, scale=self.rs[:, 0:1]))
        mv = V.done(V.eng.tensor_scalar(xn[:, 1, :], x[:, 1, :], self.rs[:, 1:2], None, ALU.mult))
        return ma, mv

    def turned(self, xn, xT, gain, *after):
        PE, A, V, p = self.PE, self.A, self.V, self.prog
        PE(*after, self.m_ident)
        marks = []
        for c in range(0, ND, 4):
            i, ps = p.take()
            for k in range(4):
                for tt in range(NT):
                    o = ps[:, k // 2, (k % 2) * T + tt * P:(k % 2) * T + tt * P + P]
                    last = PE.eng.transpose(o, xn[:, tt, (c + k) * P:(c + k + 1) * P], self.ident[:, :])
            m = PE.done(last)
            A(m)
            V(m)
            for k in range(4):
                o, s = xT[:, c + k, :], ps[:, k // 2, (k % 2) * T:(k % 2) * T + T]
                g = gain[:, c + k:c + k + 1]
                if k // 2:
                    a = A.done(A.eng.activation(o, s, ACT.Copy, scale=g))
                else:
                    v = V.done(V.eng.tensor_scalar(o, s, g, None, ALU.mult))
            p.give(i, a, v)
            marks = [a, v]
        return marks

    def unit(self, src, rows, cols):
        u, m = self.prog.unit(src, rows, cols)
        self.PE(m)
        return u

    def project_T(self, src, xT, cols, evacuate):
        PE, p = self.PE, self.prog
        u = self.unit(src, ND, cols)
        n = cols // P
        i, ps = p.take()
        for c in range(n):
            o = ps[:, c // 2, (c % 2) * T:(c % 2) * T + T]
            for d in range(ND):
                last = PE.eng.matmul(o, u[:, d, c * P:(c + 1) * P], xT[:, d, :],
                                     start=d == 0, stop=d == ND - 1)
        m = PE.done(last, p.used)
        flat = ps.rearrange("p a (b t) -> p (a b) t", t=T)[:, 0:n, :]
        p.give(i, *evacuate(n, flat, m))

    def project(self, src, xT, cols, evacuate):
        PE, p = self.PE, self.prog
        u = self.unit(src, ND, cols)
        i, ps = p.take()
        for tt in range(NT):
            for d in range(ND):
                last = PE.eng.matmul(ps[:, tt, 0:cols], xT[:, d, tt * P:(tt + 1) * P], u[:, d, :],
                                     start=d == 0, stop=d == ND - 1)
        m = PE.done(last, p.used)
        p.give(i, *evacuate(ps[:, :, 0:cols], m))

    def copy_to(self, dst, engine=None, scale=None):
        at = [0]

        def evacuate(n, ps, m):
            o = dst[:, at[0]:at[0] + n, :]
            at[0] += n
            return [self.copy(o, ps, m, engine, scale)]
        return evacuate

    def copy(self, o, i, m, engine=None, scale=None):
        engine = engine or self.A
        engine(m)
        if engine is self.A:
            r = engine.done(engine.eng.activation(o, i, ACT.Copy, scale=1.0 if scale is None else scale))
        elif scale is None:
            r = engine.done(engine.eng.tensor_copy(o, i))
        else:
            r = engine.done(engine.eng.tensor_scalar(o, i, scale, None, ALU.mult))
        self.m_copy = r
        return r

    def accumulate(self, srcs, lhsT, x, after):
        PE, V, p = self.PE, self.V, self.prog
        PE(*after)
        i, pa = p.take()
        j, pb = p.take()
        pair = (pa, pb)
        k, nk = 0, sum(r for _, r in srcs)
        for src, rows in srcs:
            u = self.unit(src, rows, D)
            for r in range(rows):
                for tt in range(NT):
                    for h in range(2):
                        last = PE.eng.matmul(pair[tt][:, h, :], lhsT[:, k, tt * P:(tt + 1) * P],
                                             u[:, r, h * 512:(h + 1) * 512],
                                             start=k == 0, stop=k == nk - 1)
                k += 1
            m = PE.done(last, p.used)
        V(m)
        marks = []
        for tt in range(NT):
            marks.append(V.done(V.eng.tensor_tensor(x[:, tt, :], x[:, tt, :],
                                                    pair[tt].rearrange("p a b -> p (a b)"), ALU.add)))
        p.give(i, marks[0])
        p.give(j, marks[1])
        return marks

    def row_panels(self, w, n):
        out, at = [], 0
        while at < n:
            r = min(3, n - at)
            out.append((w[at * P:(at + r) * P, :], r))
            at += r
        return out


    def setup(self):
        p, c, ins, sb = self.prog, self.c, self.ins, self.sb
        PE, A, V, G = self.PE, self.A, self.V, self.G
        self.ident = sb("ident", [P, P])
        self.x = sb("x", [P, NT, D])
        self.xT = sb("xT", [P, ND, T])
        self.xn = sb("xn", [P, NT, D])
        self.ss = sb("ss", [P, 32])
        self.rs = sb("rs", [P, 32])
        m_x = p.dma(A, "x", [(self.x[:, :, :], ins["x"][0].rearrange("(a p) d -> p a d", p=P))])
        self.m_ident = p.dma(A, "ident", [(self.ident[:, :], c["ident"])])
        rows, at = [], 0
        self.col = {}
        for name in ("norm_mix", "norm_mlp", "hgrn_lb", "mix_norm_g_2", "ffn_norm_g_2", "mem_norm_g_2"):
            a = ins[name]
            n = math.prod(a.shape) // P
            flat = a.rearrange("a (b p) -> (a b) p", p=P) if len(a.shape) == 2 else a.rearrange("(b p) -> b p", p=P)
            rows.append((at, n, flat))
            self.col[name] = at
            at += n
        n_short = 3 * 3 * NM
        rowbuf = sb("rowbuf", [P, 2, P])
        self.par = sb("par", [P, 2, P])
        pairs = [(rowbuf[a:a + n, 0, :], f) for a, n, f in rows]
        pairs.append((rowbuf[0:n_short, 1, :], ins["hy_short_w_2"][0].rearrange("a (b p) -> (a b) p", p=P)))
        m = p.dma(G, "rows", pairs)
        V()
        PE(m, self.m_ident)
        i, ps = p.take()
        PE.eng.transpose(ps[:, 0, 0:at], rowbuf[0:at, 0, :], self.ident[0:at, 0:at])
        m = PE.done(PE.eng.transpose(ps[:, 0, P:P + n_short], rowbuf[0:n_short, 1, :],
                                     self.ident[0:n_short, 0:n_short]))
        V(m)
        V.done(V.eng.tensor_copy(self.par[:, 0, 0:at], ps[:, 0, 0:at]))
        m_par = V.done(V.eng.tensor_copy(self.par[:, 1, 0:n_short], ps[:, 0, P:P + n_short]))
        p.give(i, m_par)
        self.m_par = m_par
        self.m_x = m_x

    def gains(self, name, l=0):
        at = self.col[name] + l * ND
        return self.par[:, 0, at:at + ND]


    def block1_memory(self):
        sb, p, c, A, G = self.sb, self.prog, self.c, self.A, self.G
        self.gate = sb("gate", [P, 4 * ND, T])
        self.mixT = sb("mixT", [P, ND, T])
        self.sqT = sb("sqT", [P, 3, T])
        self.skT = sb("skT", [P, 3, T])
        self.sv = sb("sv", [P, NT, 384])
        self.oT = sb("oT", [P, 3, T])
        self.dsa = sb("dsa", [P, NT, W_DSA])
        self.dT = sb("dT", [P, 9, T])
        self.rot = self.dT[:, 0:4, 0:NBLK * 8]
        self.score = sb("score", [P, NT, T])
        self.work = sb("work", [P, NT, T])
        self.top8 = sb("top8", [P, NT, 8])
        self.small = sb("small", [P, 64])
        self.big1 = self.xn[:, :, :].rearrange("p a (b t) -> p (a b) t", t=T)[:, 0:6, :]
        self.big2 = sb("big2", [P, 6, T])
        self.hqT = sb("hqT", [P, N_HG, T])
        self.hkT = sb("hkT", [P, N_HG, T])
        self.hbT = sb("hbT", [P, N_HG, T])
        self.hw = self.gate[:, 3 * ND:3 * ND + N_HG, :]
        self.hw2 = self.gate[:, 3 * ND + N_HG:4 * ND, :]
        self.hvg = sb("hvg", [P, NT, 512])
        self.att = sb("att", [P, N_HG, 384])
        self.ones = sb("ones", [P, T])
        self.negu = sb("negu", [P, P])
        self.negone = sb("negone", [P, P])
        self.strict = sb("strict", [P, P])
        self.lvl = sb("lvl", [P, len(MASKED), 32])
        self.rc = sb("rc", [P, NT, NBLK * 8])
        self.rsn = sb("rsn", [P, NT, NBLK * 8])
        self.m_c1 = p.dma(G, "consts1", [
            (self.negu[:, :], c["negu"]), (self.strict[:, :], c["strict"]),
            (self.lvl[:, :, :], c["levels"]), (self.rc[:, :, :], c["dsa_cos"]),
            (self.rsn[:, :, :], c["dsa_sin"])])
        V = self.V
        V.done(V.eng.memset(self.negone[:, :], -1.0))
        V.done(V.eng.memset(self.ones[:, :], 1.0))
        self.m_set1 = V.done(V.eng.memset(self.att[:, :, :], 0.0))
        self.gcur = sb("gcur", [P, 2 * ND])
        self.lb = sb("lb", [P, DEPTH, N_HG])
        self.lbc = sb("lbc", [P, 2, N_HG])
        self.qkg = sb("qkg", [P, 2, HD])
        self.og = sb("og", [P, 1])
        self.idle = sb("idle", [P, 1])
        self.idle_v = sb("idle_v", [P, 1])
        self.m_idle = G.done(G.eng.memset(self.idle[:, :], 0.0))
        at = self.col["hgrn_lb"]
        a = [self.par[:, 0, at + l * N_HG:at + (l + 1) * N_HG] for l in range(DEPTH)]
        s = self.small
        V(self.m_par)
        V.done(V.eng.tensor_tensor(s[:, 0:4], a[0], a[1], ALU.max))
        V(V.last)
        V.done(V.eng.tensor_tensor(s[:, 4:8], a[0], s[:, 0:4], ALU.subtract))
        m = V.done(V.eng.tensor_tensor(s[:, 8:12], a[1], s[:, 0:4], ALU.subtract))
        A(m)
        m = A.done(A.eng.activation(s[:, 4:12], s[:, 4:12], ACT.Exp))
        V(m)
        V.done(V.eng.tensor_tensor(s[:, 12:16], s[:, 4:8], s[:, 8:12], ALU.add))
        V(V.last)
        V.done(V.eng.reciprocal(s[:, 12:16], s[:, 12:16]))
        V(V.last)
        V.done(V.eng.tensor_tensor(s[:, 4:8], s[:, 4:8], s[:, 12:16], ALU.mult))
        V.done(V.eng.tensor_tensor(s[:, 8:12], s[:, 8:12], s[:, 12:16], ALU.mult))
        V(V.last)
        V.done(V.eng.tensor_tensor(s[:, 16:20], s[:, 4:8], s[:, 8:12], ALU.add))
        V.done(V.eng.tensor_tensor(self.lb[:, 0, :], s[:, 4:8], s[:, 4:8], ALU.subtract))
        V(V.last)
        V.done(V.eng.tensor_tensor(self.lb[:, 1, :], s[:, 16:20], s[:, 4:8], ALU.subtract))

    def layer_vectors(self, l):
        p, V, G, ins = self.prog, self.V, self.G, self.ins
        par, ds = self.par, bass.ds
        qk = [(self.qkg[:, k, :], ins[n][ds(l, 1), :].broadcast_to((P, HD)))
              for k, n in enumerate(("qn_dsa", "kn_dsa"))]
        og = [(self.og[h * HD:(h + 1) * HD, :], ins["hgrn_onorm"][ds(l, 1), :].rearrange("a d -> d a"))
              for h in range(2)]
        self.m_lv = p.dma(G, "layer_vectors", qk + og)
        V.done(V.eng.tensor_copy(self.gcur[:, 0:ND], par[:, 0, ds(self.col["norm_mix"] + l * ND, ND)]))
        V.done(V.eng.tensor_copy(self.gcur[:, ND:], par[:, 0, ds(self.col["norm_mlp"] + l * ND, ND)]))
        V.done(V.eng.tensor_copy(self.lbc[:, 0, :], self.lb[:, ds(l, 1), :].rearrange("p a b -> p (a b)")))
        V(V.last)
        self.m_cur = V.done(V.eng.tensor_scalar(self.lbc[:, 1, :], self.lbc[:, 0, :], -1.0, 1.0, ALU.mult, ALU.add))

    def held_back(self, t, *marks):
        G = self.G
        G(*marks, self.m_idle)
        self.m_idle = G.done(G.eng.tensor_tensor(t, t, t, ALU.add))


    def sb_scores(self, c):
        PE, A, V, p = self.PE, self.A, self.V, self.prog
        PE(self.m_sqk)
        i, ps = p.take()
        for h in range(2):
            r = slice(h * HD, (h + 1) * HD)
            PE.eng.matmul(ps[:, h, 0:T], self.skT[r, c, 0:P], self.sqT[r, c, :], start=True,
                          stop=False, skip_group_check=True)
            last = PE.eng.matmul(ps[:, h, T:T + P], self.skT[r, c, P:T], self.sqT[r, c, P:T],
                                 start=False, stop=False, skip_group_check=True)
        m = PE.done(last)
        z = ps[:, :, 0:384]
        e = self.big1[:, 3 * (c % 2):3 * (c % 2) + 3, :].rearrange("p a b -> p (a b)").rearrange("p (h n) -> p h n", h=2)
        A(m, self.sb_free[c % 2])
        for f, src, kw in ((ACT.Abs, z, {}), (ACT.Exp, e, {"scale": -1.0}), (ACT.Ln, e, {"bias": 1.0})):
            m = A.done(A.eng.activation(e, src, f, **kw))
            A(m)
        V(m, self.m_c1)
        V.done(V.eng.scalar_tensor_tensor(out=e, in0=z, scalar=0.0, in1=e, op0=ALU.max, op1=ALU.add))
        V(V.last)
        for h in range(2):
            d = e[:, h, :].rearrange("p (a b) -> p a b", a=3)[:, 0:3:2, :]
            m = V.done(V.eng.tensor_tensor(d, d, self.strict[:, :].unsqueeze(1).broadcast_to((P, 2, P)),
                                           ALU.mult))
        self.sb_state[c] = (i, ps, e, m)

    def sb_weights(self, c):
        PE, A, G = self.PE, self.A, self.G
        i, ps, e, m = self.sb_state[c]
        PE(m, self.m_set1)
        for h in range(2):
            PE.eng.matmul(ps[:, h, 0:384], self.negu[:, :], e[:, h, :], start=False, stop=False,
                          skip_group_check=True)
            last = PE.eng.matmul(ps[:, h, P:T], self.negone[:, :], e[:, h, T:384], start=False,
                                 stop=True, skip_group_check=True)
        m = PE.done(last)
        A(m)
        m = A.done(A.eng.activation(e, ps[:, :, 0:384], ACT.Exp))
        self.prog.give(i, m)
        self.held_back(self.idle[:, :], m)
        for h in range(2):
            d = e[:, h, :].rearrange("p (a b) -> p a b", a=3)[:, 0:3:2, :]
            m = G.done(G.eng.affine_select(out=d, in_=d, compare_op=ALU.is_gt, fill=0.0, base=0,
                                           pattern=[[0, 2], [1, P]], channel_multiplier=-1))
        self.sb_state[c] = (e, m)

    def sb_values(self, c, sb_oT):
        PE, p = self.PE, self.prog
        e, m = self.sb_state[c]
        PE(m, self.m_sv)
        i, ps = p.take()
        for h in range(2):
            o, f = slice(h * HD, (h + 1) * HD), slice((2 * c + h) * HD, (2 * c + h + 1) * HD)
            PE.eng.matmul(ps[o, h, 0:T], self.sv[:, 0, f], e[:, h, 0:T], start=True, stop=False,
                          skip_group_check=True)
            last = PE.eng.matmul(ps[o, h, P:T], self.sv[:, 1, f], e[:, h, T:384], start=False,
                                 stop=True, skip_group_check=True)
        m = PE.done(last)
        self.sb_free[c % 2] = m
        for h in range(2):
            o = slice(h * HD, (h + 1) * HD)
            m = self.copy(sb_oT[o, c, :], ps[o, h, 0:T], m, self.V)
        p.give(i, m)
        return m

    def branch(self, k, w, nrow, oT, after):
        PE, V, G, p = self.PE, self.V, self.G, self.prog
        PE(*after)
        u = self.unit(w, nrow, D)
        for f in range(0, ND, 4):
            i, ps = p.take()
            for q in range(4):
                for r in range(nrow):
                    last = PE.eng.matmul(ps[:, q // 2, (q % 2) * T:(q % 2) * T + T],
                                         u[:, r, (f + q) * P:(f + q + 1) * P], oT[:, r, :],
                                         start=r == 0, stop=r == nrow - 1)
            m = PE.done(last, p.used if f + 4 == ND else None)
            V(m, self.m_gate)
            y = ps.rearrange("p a (b t) -> p (a b) t", t=T)
            g = self.gate[:, k * ND + f:k * ND + f + 4, :]
            if k == 0:
                m = V.done(V.eng.tensor_tensor(self.mixT[:, f:f + 4, :], y, g, ALU.mult))
            else:
                m = V.done(V.eng.tensor_tensor(g, y, g, ALU.mult))
                G(m, self.m_mix.get(f))
                m2 = self.m_mix[f] = G.done(G.eng.tensor_tensor(self.mixT[:, f:f + 4, :], self.mixT[:, f:f + 4, :], g, ALU.add))
            p.give(i, m)
        return m if k == 0 else m2


    def dsa_rows(self):
        V, G = self.V, self.G
        d = self.dsa
        qk = d[:, :, 0:448].rearrange("p a (h e) -> p a h e", e=HD)
        sq = self.big2[:, 0:4, :].rearrange("p a b -> p (a b)")[:, 0:896]
        sq4 = sq.rearrange("p (a h e) -> p a h e", a=2, e=HD)
        V(self.m_dsa, self.m_lv)
        V.done(V.eng.tensor_tensor(sq4, qk, qk, ALU.mult))
        V(V.last)
        m = V.done(V.eng.tensor_reduce(self.small[:, 0:14], sq.rearrange("p (x e) -> p x e", e=HD), AX, ALU.add))
        m = self.rstd(self.small[:, 0:14], HD, self.small[:, 16:30], m)
        V(m)
        r = self.small[:, 16:30].rearrange("p (a h) -> p a h", a=2)
        for tt in range(NT):
            V.done(V.eng.tensor_tensor(qk[:, tt], qk[:, tt], r[:, tt].unsqueeze(2).broadcast_to((P, 7, HD)), ALU.mult))
        V(V.last)
        for tt in range(NT):
            V.done(V.eng.tensor_tensor(qk[:, tt, 0:6], qk[:, tt, 0:6],
                                       self.qkg[:, 0, :].unsqueeze(1).broadcast_to((P, 6, HD)), ALU.mult))
            V.done(V.eng.tensor_tensor(qk[:, tt, 6], qk[:, tt, 6], self.qkg[:, 1, :], ALU.mult))
        V.done(V.eng.tensor_scalar(d[:, :, 1088:1096], d[:, :, 1088:1096], IDX_SCALE, None, ALU.mult))
        V(V.last)
        blocks = d[:, :, 0:NBLK * HD].rearrange("p a (k e) -> p a k e", e=HD)
        n = NBLK * 8
        for tt in range(NT):
            x1, x2 = blocks[:, tt, :, 0:8], blocks[:, tt, :, 8:16]
            cs, sn = (t[:, tt, :].rearrange("p (k e) -> p k e", e=8) for t in (self.rc, self.rsn))
            t = [self.rot[:, k, 0:n].rearrange("p (k e) -> p k e", e=8) for k in range(4)]
            V.done(V.eng.tensor_tensor(t[0], x1, cs, ALU.mult))
            V.done(V.eng.tensor_tensor(t[1], x2, sn, ALU.mult))
            V.done(V.eng.tensor_tensor(t[2], x2, cs, ALU.mult))
            V.done(V.eng.tensor_tensor(t[3], x1, sn, ALU.mult))
            V(V.last)
            V.done(V.eng.tensor_tensor(x1, t[0], t[1], ALU.subtract))
            m = V.done(V.eng.tensor_tensor(x2, t[2], t[3], ALU.add))
            V(m)
        dup = sq[:, 0:512].rearrange("p (a k h e) -> p a k h e", a=2, k=2, h=2)
        for tt in range(NT):
            for k, at in ((0, 384), (1, 1024)):
                m = V.done(V.eng.tensor_copy(dup[:, tt, k], d[:, tt, at:at + HD].unsqueeze(1).broadcast_to((P, 2, HD))))
        self.dup = dup
        self.m_rows = m

    def dsa_turn(self):
        PE, p, d = self.PE, self.prog, self.dsa
        PE(self.m_rows)
        dup = self.dup

        def src(j, tt):
            if j < 3:
                return d[:, tt, j * P:(j + 1) * P]
            if j in (3, 8):
                return dup[:, tt, 0 if j == 3 else 1].rearrange("p h e -> p (h e)")
            return d[:, tt, 512 + (j - 4) * P:512 + (j - 3) * P]
        order = [4, 5, 6, 7, 8, 0, 1, 2, 3]
        for g in range(0, 9, 4):
            js = order[g:g + 4]
            i, ps = p.take()
            for q, j in enumerate(js):
                for tt in range(NT):
                    last = PE.eng.transpose(ps[:, q // 2, (q % 2) * T + tt * P:(q % 2) * T + tt * P + P],
                                            src(j, tt), self.ident[:, :])
            m = PE.done(last)
            flat = ps.rearrange("p a (b t) -> p (a b) t", t=T)
            done = []
            q = 0
            while q < len(js):
                n = 1
                while q + n < len(js) and js[q + n] == js[q] + n:
                    n += 1
                done.append(self.copy(self.dT[:, js[q]:js[q] + n, :], flat[:, q:q + n, :], m))
                q += n
            p.give(i, *done)
        self.m_dT = done[-1]

    def dsa_index(self, tt):
        PE, A, V, G, p = self.PE, self.A, self.V, self.G, self.prog
        n = (tt + 1) * P
        PE(self.m_dT)
        sc = self.score[:, tt, 0:n]
        hs = 4 if tt else 8
        first = True
        for h0 in range(0, N_IDX, hs):
            i, ps = p.take()
            for j in range(h0, h0 + hs):
                r = slice((j % 2) * HD, (j % 2 + 1) * HD)
                k = (j - h0) // 2
                last = PE.eng.matmul(ps[:, j % 2, k * n:(k + 1) * n],
                                     self.dT[r, 4 + j // 2, tt * P:(tt + 1) * P], self.dT[r, 8, 0:n],
                                     start=True, stop=True)
            m = PE.done(last)
            rel = self.big1[:, 0:4, :].rearrange("p a b -> p (a b)")
            A(m, self.m_rel)
            m = A.done(A.eng.activation(rel, ps.rearrange("p a b -> p (a b)"), ACT.Relu))
            p.give(i, m)
            V(m)
            for j in range(h0, h0 + hs):
                k = (j % 2) * (hs // 2) + (j - h0) // 2
                w = self.dsa[:, tt, 1088 + j:1089 + j]
                if first:
                    m = V.done(V.eng.tensor_scalar(sc, rel[:, k * n:(k + 1) * n], w, None, ALU.mult))
                else:
                    V(m)
                    m = V.done(V.eng.scalar_tensor_tensor(out=sc, in0=rel[:, k * n:(k + 1) * n], scalar=w, in1=sc,
                                                          op0=ALU.mult, op1=ALU.add))
                first = False
            self.m_rel = m
        self.held_back(self.idle[:, :], m)
        self.m_sc[tt] = G.done(G.eng.affine_select(out=sc, in_=sc, compare_op=ALU.is_ge, fill=NEG, base=tt * P,
                                                   pattern=[[-1, n]], channel_multiplier=1))

    def dsa_select(self):
        V = self.V
        step = self.topk_step
        V.eng.sem_clear(step)
        V(*self.m_sc)
        V.done(V.eng.tensor_copy(self.idle_v[:, :], self.score[:, 0, 0:1]))
        n_step = 0
        for r in range(K_TOP // 8):
            src = self.score if r == 0 else self.work
            for tt in range(NT):
                if r:
                    V.eng.wait_ge(step, n_step - 1)
                V.eng.max(out=self.top8[:, tt, :], in_=src[:, tt, 0:(tt + 1) * P]).then_inc(step, 1)
                n_step += 1
            for tt in range(NT):
                n = (tt + 1) * P
                V.eng.wait_ge(step, n_step - 1)
                V.eng.match_replace(out=self.work[:, tt, 0:n], in_to_replace=self.top8[:, tt, :],
                                    in_values=src[:, tt, 0:n], imm_value=TINY).then_inc(step, 1)
                n_step += 1
        V.eng.wait_ge(step, n_step)
        for tt in range(NT):
            n = (tt + 1) * P
            w, s = self.work[:, tt, 0:n], self.score[:, tt, 0:n]
            V.done(V.eng.tensor_scalar(w, w, 2 * NEG, None, ALU.is_lt))
            V(V.last)
            V.done(V.eng.scalar_tensor_tensor(out=w, in0=s, scalar=0.5 * NEG, in1=w, op0=ALU.is_gt, op1=ALU.mult))
            V(V.last)
            m = V.done(V.eng.tensor_scalar(w, w, -NEG, NEG, ALU.mult, ALU.add))
        self.m_bias = m

    def dsa_attend(self, tt):
        PE, A, V, p = self.PE, self.A, self.V, self.prog
        n = (tt + 1) * P
        bias = self.work[:, tt, 0:n]
        lg = self.big1[:, :, 0:n] if tt else self.big1[:, 0:3, :].rearrange("p a (b n) -> p (a b) n", n=P)
        slots = [0, 2, 1, 3, 4, 5] if tt else [0, 2, 4, 1, 3, 5]
        PE(self.m_dT)
        V(self.m_bias, self.m_lg)
        for group in ([[0, 2, 1, 3], [4, 5]] if tt else [[0, 2, 4, 1, 3, 5]]):
            i, ps = p.take()
            k = len(group) // 2
            for q, h in enumerate(group):
                r = slice((h % 2) * HD, (h % 2 + 1) * HD)
                last = PE.eng.matmul(ps[:, h % 2, (q % k) * n:(q % k + 1) * n],
                                     self.dT[r, h // 2, tt * P:(tt + 1) * P], self.dT[r, 3, 0:n], start=True, stop=True)
            m = PE.done(last)
            V(m)
            for b in range(2):
                s0 = slots.index(group[b * k])
                m = V.done(V.eng.scalar_tensor_tensor(
                    out=lg[:, s0:s0 + k, :], in0=ps[:, b, 0:k * n].rearrange("p (a n) -> p a n", n=n),
                    scalar=HD ** -0.5, in1=bias.unsqueeze(1).broadcast_to((P, k, n)), op0=ALU.mult, op1=ALU.add))
            p.give(i, m)
        V(V.last)
        s = self.small
        V.done(V.eng.tensor_reduce(s[:, 32:38], lg, AX, ALU.max))
        V(V.last)
        m = V.done(V.eng.tensor_scalar(s[:, 32:38], s[:, 32:38], -1.0, None, ALU.mult))
        A(m)
        for h in range(6):
            m = A.done(A.eng.activation(lg[:, h, :], lg[:, h, :], ACT.Exp, bias=s[:, 32 + h:33 + h],
                                        accum_out=s[:, 40 + h:41 + h]))
        V(m)
        V.done(V.eng.reciprocal(s[:, 40:46], s[:, 40:46]))
        V(V.last)
        m = V.done(V.eng.tensor_tensor(lg, lg, s[:, 40:46].unsqueeze(2).broadcast_to((P, 6, n)), ALU.mult))
        PE(m)
        for kt in range(tt + 1):
            i, ps = p.take()
            for h in range(6):
                last = PE.eng.transpose(ps[:, h % 2, (h // 2) * P:(h // 2 + 1) * P],
                                        lg[:, slots.index(h), kt * P:(kt + 1) * P], self.ident[:, :])
            m = PE.done(last)
            A(self.m_pt)
            m = self.copy(self.ptv(kt), ps[:, :, 0:384], m)
            p.give(i, m)
        self.m_lg = m
        PE(m)
        i, ps = p.take()
        for b in range(2):
            for kt in range(tt + 1):
                last = PE.eng.matmul(ps[b * HD:(b + 1) * HD, b, 0:384], self.dsa[:, kt, 448:512], self.ptv(kt)[:, b, :],
                                     start=kt == 0, stop=kt == tt)
        m = PE.done(last)
        self.m_pt = m
        for b in range(2):
            m = self.copy(self.dsa_oT[b * HD:(b + 1) * HD, :, tt * P:(tt + 1) * P],
                          ps[b * HD:(b + 1) * HD, b, 0:384].rearrange("p (a n) -> p a n", n=P), m, self.V)
        p.give(i, m)
        return m

    def ptv(self, kt):
        return self.big2[:, 3 * kt:3 * kt + 3, :].rearrange("p a b -> p (a b)").rearrange("p (h n) -> p h n", h=2)


    def hg_gates(self):
        A, V = self.A, self.V
        q, k, b = self.hqT, self.hkT, self.hbT
        V(self.m_hf)
        for h in range(N_HG):
            m = V.done(V.eng.tensor_scalar(b[:, h, :], k[:, h, :], self.lbc[:, 1, h:h + 1], self.lbc[:, 0, h:h + 1],
                                           ALU.mult, ALU.add))
        V(m)
        V.done(V.eng.tensor_scalar(k[:, :, :], b[:, :, :], -1.0, 1.0, ALU.mult, ALU.add))
        m = V.done(V.eng.tensor_scalar(self.hw[:, :, :], b[:, :, :], F_MIN, None, ALU.max))
        A(m)
        m = A.done(A.eng.activation(self.hw[:, :, :], self.hw[:, :, :], ACT.Ln))
        V(m, self.m_set1)
        for h in range(N_HG):
            m = V.done(V.eng.tensor_tensor_scan(b[:, h, :], self.ones[:, :], self.hw[:, h, :], 0.0, ALU.mult, ALU.add))
        self.m_b = m

    def hg_level(self, m_, w, free):
        A, V = self.A, self.V

        def halves(t):
            v = t[:, :, :].rearrange("p h t -> p (h t)").rearrange("p (n a m) -> p n a m", a=2, m=m_)
            return v[:, :, 0, :], v[:, :, 1, :]
        b1, b2 = halves(self.hbT)
        e1, e2 = halves(w)
        n = N_HG * T // (2 * m_)
        ref = b1[:, :, m_ - 1:m_].broadcast_to((P, n, m_))
        V(self.m_b, free)
        V.done(V.eng.tensor_tensor(e2, b2, ref, ALU.subtract))
        m = V.done(V.eng.tensor_tensor(e1, ref, b1, ALU.subtract))
        A(m)
        m = A.done(A.eng.activation(w[:, :, :], w[:, :, :], ACT.Exp))
        V(m)
        V.done(V.eng.tensor_tensor(e2, e2, halves(self.hqT)[1], ALU.mult))
        return V.done(V.eng.tensor_tensor(e1, e1, halves(self.hkT)[0], ALU.mult))

    def hg_big(self):
        PE, V, p = self.PE, self.V, self.prog
        for m_ in HG_LEVELS[:3]:
            w = (self.hw, self.hw2)[m_ == 64]
            m = self.hg_level(m_, w, self.hw_free[m_ == 64])
            PE(m)
            i, ps = p.take()
            outs = []
            for s0 in range(0, T, 2 * m_):
                st, r = s0 // P, s0 % P
                t0 = s0 + m_
                col = t0 if st == 0 else T + t0 - P
                for h in range(N_HG):
                    last = PE.eng.matmul(ps[r:r + m_, st, h * P:h * P + m_], w[:, h, s0:s0 + m_], w[:, h, t0:t0 + m_],
                                         start=True, stop=True)
                outs.append((st, r, col))
            m = PE.done(last)
            self.hw_free[m_ == 64] = m
            V(m)
            for st, r, col in outs:
                m = V.done(V.eng.tensor_copy(self.att[r:r + m_, :, col:col + m_],
                                             ps[r:r + m_, st, :].rearrange("p (h n) -> p h n", n=P)[:, :, 0:m_]))
            p.give(i, m)

    def hg_small(self):
        PE, V, p = self.PE, self.V, self.prog
        part = self.gatebuf
        for g in range(0, len(MASKED), 3):
            i, ps = p.take()
            j = None
            for q, m_ in enumerate(MASKED[g:g + 3]):
                if m_:
                    k = q % 2
                    w = (self.hw, self.hw2)[k]
                    m = self.hg_level(m_, w, self.hw_free[k])
                    PE(m)
                    lw = rw = w
                else:
                    lw, rw = self.hkT, self.hqT
                    PE(self.m_b, self.m_hq)
                if q == 2:
                    j, ps2 = p.take()
                bank = ps[:, q, :] if q < 2 else ps2[:, 0, :]
                for h in range(N_HG):
                    for blk in range(T // 32):
                        r = 32 * (blk % 4)
                        col = h * 64 + (blk // 4) * 32
                        t = slice(blk * 32, blk * 32 + 32)
                        last = PE.eng.matmul(bank[r:r + 32, col:col + 32], lw[:, h, t], rw[:, h, t], start=True, stop=True)
                m = PE.done(last)
                if m_:
                    self.hw_free[k] = m
                V(m)
                lv = g + q
                m = V.done(V.eng.tensor_tensor(
                    part[:, lv, 0:256].rearrange("p (x t) -> p x t", t=32),
                    bank[:, 0:256].rearrange("p (x t) -> p x t", t=32),
                    self.lvl[:, lv, :].unsqueeze(1).broadcast_to((P, 8, 32)), ALU.mult))
            p.give(i, m)
            p.give(j, m)
        V(V.last)
        for lv in range(1, len(MASKED)):
            V.done(V.eng.tensor_tensor(part[:, 0, 0:256], part[:, 0, 0:256], part[:, lv, 0:256], ALU.add))
            V(V.last)
        for r in range(4):
            q = slice(32 * r, 32 * r + 32)
            for st in range(2):
                col = 32 * r + (T if st else 0)
                m = V.done(V.eng.tensor_copy(self.att[q, :, col:col + 32],
                                             part[q, 0, 0:256].rearrange("p (h a t) -> p h a t", a=2, t=32)[:, :, st, :]))
        self.m_att = m

    def hg_out(self):
        PE, A, V, p = self.PE, self.A, self.V, self.prog
        PE(self.m_att, self.m_hvg)
        i, ps = p.take()
        for tt in range(NT):
            for h in range(N_HG):
                for kt in range(tt + 1):
                    col = tt * P if kt == 0 else T
                    last = PE.eng.matmul(ps[:, tt, h * HD:(h + 1) * HD], self.att[:, h, col:col + P],
                                         self.hvg[:, kt, h * HD:(h + 1) * HD], start=kt == 0, stop=kt == tt)
        m = PE.done(last)
        o, sq = self.hw[:, 0:2, :], self.hw2[:, 0:2, :]
        A(m, self.hw_free[0], self.hw_free[1])
        m2 = A.done(A.eng.activation(o, ps[:, :, 0:256], ACT.Copy))
        m = A.done(A.eng.activation(sq, ps[:, :, 0:256], ACT.Square))
        p.give(i, m)
        V(m)
        s = self.small
        m = V.done(V.eng.tensor_reduce(s[:, 48:56], sq.rearrange("p a (h e) -> p (a h) e", e=HD), AX, ALU.add))
        m = self.rstd(s[:, 48:56], HD, s[:, 56:64], m)
        V(m)
        o3 = o.rearrange("p a (h e) -> p (a h) e", e=HD)
        V.done(V.eng.tensor_tensor(o3, o3, s[:, 56:64].unsqueeze(2).broadcast_to((P, 8, HD)), ALU.mult))
        V(V.last)
        m = V.done(V.eng.tensor_tensor(o, o, self.hvg[:, :, 256:512], ALU.mult))
        PE(m)
        i, ps = p.take()
        for c in range(2):
            for tt in range(NT):
                last = PE.eng.transpose(ps[:, 0, c * T + tt * P:c * T + tt * P + P], o[:, tt, c * P:(c + 1) * P], self.ident[:, :])
        m = PE.done(last)
        m = self.copy(self.hg_oT[:, :, :].rearrange("p a b -> p (a b)"), ps[:, 0, :], m, self.A, scale=self.og[:, 0:1])
        p.give(i, m)
        return m

    def mlp(self, l, ds):
        A, V, G, p, ins = self.A, self.V, self.G, self.prog, self.ins
        xn = self.normed_rows(self.x, self.xn, *self.m_xs)
        ready = self.turned(self.xn, self.xT, self.gcur[:, ND:], *xn)
        self.PE(*ready)
        hid, at = self.gate, [0]
        self.hid_marks = []

        def evacuate(n, ps, m):
            o = hid[:, at[0]:at[0] + n, :]
            at[0] += n
            A(m)
            m = A.done(A.eng.activation(o, ps, ACT.Relu))
            V(m)
            self.hid_marks.append(V.done(V.eng.tensor_tensor(o, o, o, ALU.mult)))
            return [m]
        w = ins["w_up"][ds(l, 1), :, :].rearrange("a d n -> (a d) n")
        for c in range(0, D_FF, 384):
            n = min(384, D_FF - c)
            self.project_T(w[:, c:c + n], self.xT, n, evacuate)
        w = ins["w_down"][ds(l, 1), :, :].rearrange("a d n -> (a d) n")
        self.m_xs = self.accumulate(self.row_panels(w, D_FF // P), hid, self.x, [self.hid_marks[-1]])

    def block1(self):
        p, ins, A, V, PE = self.prog, self.ins, self.A, self.V, self.PE
        self.block1_memory()
        self.gatebuf = self.mixT[:, 0:len(MASKED), :]
        self.hg_oT = self.skT[:, 0:2, :]
        self.dsa_oT = self.sqT[:, :, :]
        A(self.m_x)
        V(self.m_x)
        ds = bass.ds
        self.topk_step = p.nc.alloc_semaphore("topk_step")
        with p.loop_of("layers", DEPTH) as l:
            self.sb_state, self.sb_free = {}, [None, None]
            self.hw_free = [None, None]
            self.m_sc = [None] * NT
            self.m_rel = self.m_lg = self.m_pt = None
            self.m_mix = {}
            self.layer_vectors(l)
            xn = self.normed_rows(self.x, self.xn)
            V(self.m_cur)
            A(self.m_cur)
            ready = self.turned(self.xn, self.xT, self.gcur[:, 0:ND], *xn)
            PE(*ready)
            w = ins["w_in"][ds(l, 1), :, :].rearrange("a d n -> (a d) n")
            xT = self.xT
            self.project_T(w[:, C_SQ:C_SQ + 384], xT, 384, self.copy_to(self.sqT, scale=HD ** -0.5))
            self.project_T(w[:, C_SK:C_SK + 384], xT, 384, self.copy_to(self.skT))
            self.m_sqk = self.m_copy

            def evac(dst):
                def f(ps, m):
                    self.m_ev = self.copy(dst, ps, m)
                    return [self.m_ev]
                return f
            self.project(w[:, C_SV:C_SV + 384], xT, 384, evac(self.sv[:, :, :]))
            self.m_sv = self.m_ev
            self.sb_scores(0)
            for c in range(0, W_DSA, 384):
                n = min(384, W_DSA - c)
                self.project(w[:, C_DSA + c:C_DSA + c + n], xT, n, evac(self.dsa[:, :, c:c + n]))
                if c == 0:
                    self.sb_weights(0)
                    self.sb_scores(1)
                elif c == 384:
                    self.sb_values(0, self.oT)
                    self.sb_weights(1)
            self.m_dsa = self.m_ev
            self.sb_scores(2)
            self.sb_values(1, self.oT)
            self.dsa_rows()
            at = [0]

            def hqf(n, ps, m):
                A(m)
                out = []
                js = range(at[0], at[0] + n)
                at[0] += n
                for k, j in enumerate(js):
                    dst = (self.hqT if j < N_HG else self.hkT)[:, j % N_HG, :]
                    self.m_hf = A.done(A.eng.activation(dst, ps[:, k, :], ACT.Sigmoid))
                for k, j in enumerate(js):
                    if j < N_HG:
                        V(self.m_hf)
                        dst = self.hqT[:, j, :]
                        self.m_hq = V.done(V.eng.tensor_tensor(dst, ps[:, k, :], dst, ALU.mult))
                        out = [self.m_hq]
                return out + [self.m_hf]
            for k, (c, n) in enumerate(((0, 384), (384, 384), (768, 256))):
                self.project_T(w[:, C_HQ + c:C_HQ + c + n], xT, n, hqf)
                if k == 0:
                    self.sb_weights(2)
                if k == 1:
                    self.sb_values(2, self.oT)
            self.dsa_turn()
            self.dsa_index(0)

            def silu_hg(ps, m):
                A(m)
                V(m)
                a = A.done(A.eng.activation(self.hvg[:, :, 256:512], ps, ACT.Sigmoid))
                V(a)
                self.m_hvg = V.done(V.eng.tensor_tensor(self.hvg[:, :, 256:512], ps, self.hvg[:, :, 256:512], ALU.mult))
                return [self.m_hvg]
            self.project(w[:, C_HI:C_HI + 256], xT, 256, evac(self.hvg[:, :, 0:256]))
            self.dsa_index(1)
            self.project(w[:, C_HI + 256:C_HI + 512], xT, 256, silu_hg)
            self.hg_gates()
            self.dsa_select()
            gate_at = [0]

            def gates(n, ps, m):
                A(m)
                o = self.gate[:, gate_at[0]:gate_at[0] + n, :]
                gate_at[0] += n
                self.m_gate = A.done(A.eng.activation(o, ps, ACT.Sigmoid))
                return [self.m_gate]

            def gate_unit(k):
                c, n = ((0, 384), (384, 384), (768, 256))[k % 3]
                c += C_GATE + (k // 3) * D
                self.project_T(w[:, c:c + n], xT, n, gates)
            for k in range(3):
                gate_unit(k)
            self.hg_big()
            for k in range(3, 5):
                gate_unit(k)
            self.dsa_attend(0)
            for k in range(5, 7):
                gate_unit(k)
            m_dsa = self.dsa_attend(1)
            for k in range(7, 9):
                gate_unit(k)
            self.hg_small()
            br = {n: ins[n][ds(l, 1), :, :].rearrange("a d n -> (a d) n") for n in ("w_br_sb", "w_br_dsa", "w_br_hgrn", "w_out")}
            self.branch(0, br["w_br_sb"], 3, self.oT, [V.last])
            self.branch(1, br["w_br_dsa"], 3, self.dsa_oT, [m_dsa])
            m_hg = self.hg_out()
            m = self.branch(2, br["w_br_hgrn"], 2, self.hg_oT, [m_hg])
            self.m_xs = self.accumulate(self.row_panels(br["w_out"], ND), self.mixT, self.x, [m])
            self.mlp(l, ds)



    def block2_memory(self):
        sb, p, ins, c = self.sb, self.prog, self.ins, self.c
        G, V, PE = self.G, self.V, self.PE
        self.mkT = sb("mkT", [P, DEPTH, 2, T])
        self.mv = sb("mv", [P, DEPTH, NT, N_MEM * HD])
        self.router = sb("router", [P, DEPTH, ND, N_EXP])
        self.iota = sb("iota", [P, CAP])
        self.mainT = sb("mainT", [P, ND, T])
        self.cqT = sb("cqT", [P, 2, T])
        self.prob = self.flat(self.xn).rearrange("p (k h t) -> p k h t", k=2, h=4)
        self.probT = self.flat(self.xT).rearrange("p (k a h q) -> p k a h q", k=2, a=NT, h=4)
        self.st = sb("st", [P, 64])
        pairs = [(self.router[:, i], ins["router_w_2"][i].rearrange("(c p) e -> p c e", p=P)) for i in range(DEPTH)]
        self.m_c2 = p.dma(G, "consts2", pairs + [(self.iota[:, :], c["iota"])])
        self.att_free = [None, None]

    def memory_kv(self):
        p, ins, A, V, PE = self.prog, self.ins, self.A, self.V, self.PE
        with self.scope():
            mem = self.sb("mem", [P, NT, D])
            m = p.dma(self.G, "mem", [(mem[:, :, :], ins["mem_2"][0].rearrange("(a p) d -> p a d", p=P))])
            A(m)
            V(m)
            xn = self.normed_rows(mem, self.xn)
            PE(*self.turned(self.xn, self.xT, self.gains("mem_norm_g_2"), *xn))
            for i in range(DEPTH):
                w = ins["w_mem_kv_2"][i]
                self.project_T(w[:, 0:256], self.xT, 256, self.copy_to(self.mkT[:, i]))
                self.project(w[:, 256:512], self.xT, 256,
                             lambda ps, m, i=i: [self.copy(self.mv[:, i], ps, m)])

    def attend_scores(self, k, tt, qT, kT, scale):
        PE, A, V, p = self.PE, self.A, self.V, self.prog
        i, ps = p.take()
        for h in range(4):
            last = PE.eng.matmul(ps[:, h % 2, (h // 2) * T:(h // 2 + 1) * T], qT(h)[:, tt * P:(tt + 1) * P], kT(h),
                                 start=True, stop=True)
        m = PE.done(last)
        pr, s = self.prob[:, k], self.st
        V(m, self.att_free[k])
        mx, sm = s[:, 8 * k:8 * k + 4], s[:, 16 + 8 * k:20 + 8 * k]
        V.done(V.eng.tensor_reduce(mx, ps.rearrange("p a (b n) -> p (a b) n", n=T), AX, ALU.max))
        V(V.last)
        m = V.done(V.eng.tensor_scalar(mx, mx, -scale, None, ALU.mult))
        A(m, self.att_free[k])
        for q in range(4):
            m = A.done(A.eng.activation(pr[:, q, :], ps[:, q // 2, (q % 2) * T:(q % 2 + 1) * T], ACT.Exp,
                                        scale=scale, bias=mx[:, q:q + 1], accum_out=sm[:, q:q + 1]))
        p.give(i, m)
        V(m)
        V.done(V.eng.reciprocal(sm, sm))
        V(V.last)
        return V.done(V.eng.tensor_tensor(pr, pr, sm.unsqueeze(2).broadcast_to((P, 4, T)), ALU.mult))

    def attend_values(self, k, tt, v, oT, m):
        PE, A, V, p = self.PE, self.A, self.V, self.prog
        pr, pt = self.prob[:, k], self.probT[:, k]
        PE(m)
        i, ps = p.take()
        for kt in range(NT):
            for q in range(4):
                last = PE.eng.transpose(ps[:, kt, q * P:(q + 1) * P], pr[:, q, kt * P:(kt + 1) * P], self.ident[:, :])
        m = PE.done(last)
        self.att_free[k] = m
        ma = self.copy(pt[:, 0].rearrange("p h q -> p (h q)"), ps[:, 0, :], m, A)
        mv = self.copy(pt[:, 1].rearrange("p h q -> p (h q)"), ps[:, 1, :], m, V)
        p.give(i, ma, mv)
        PE(ma, mv)
        i, ps = p.take()
        for h in range(4):
            o = slice((h % 2) * HD, (h % 2 + 1) * HD)
            q = (h % 2) * 2 + h // 2
            for kt in range(NT):
                last = PE.eng.matmul(ps[o, h % 2, (h // 2) * P:(h // 2 + 1) * P], v(kt, h), pt[:, kt, q, :],
                                     start=kt == 0, stop=kt == NT - 1)
        m = PE.done(last)
        out = []
        for b, e in ((0, A), (1, V)):
            o = slice(b * HD, (b + 1) * HD)
            out.append(self.copy(oT[o, :, tt * P:(tt + 1) * P],
                                 ps[o, b, 0:2 * P].rearrange("p (a n) -> p a n", n=P), m, e))
        p.give(i, *out)
        return out

    def attend(self, jobs):
        out, held = [], None
        for n, job in enumerate(jobs + [None]):
            new = None
            if job:
                tt, qT, kT, v, oT = job
                new = (n % 2, tt, v, oT, self.attend_scores(n % 2, tt, qT, kT, HD ** -0.5))
            if held:
                out = self.attend_values(*held)
            held = new
        return out

    def half(self, h):
        return slice((h % 2) * HD, (h % 2 + 1) * HD)

    def cross_jobs(self, i):
        return [(tt, lambda h: self.cqT[self.half(h), h // 2, :],
                 lambda h: self.mkT[self.half(h), i, h // 2, :],
                 lambda kt, h: self.mv[:, i, kt, h * HD:(h + 1) * HD], self.mainT[:, NM:NM + 2, :])
                for tt in range(NT)]

    def sine(self, ps, bias, freq, h, tmp, m):
        A, V = self.A, self.V
        big = 1.5 * 2.0 ** 23
        hi = 6.28125
        V(m)
        V.done(V.eng.tensor_scalar(h, ps, bias, freq, ALU.add, ALU.mult))
        V(V.last)
        V.done(V.eng.tensor_scalar(tmp, h, 1 / (2 * math.pi), big, ALU.mult, ALU.add))
        V(V.last)
        V.done(V.eng.tensor_scalar(tmp, tmp, big, None, ALU.subtract))
        for part in (hi, 2 * math.pi - hi):
            V(V.last)
            V.done(V.eng.scalar_tensor_tensor(out=h, in0=tmp, scalar=-part, in1=h, op0=ALU.mult, op1=ALU.add))
        V(V.last)
        lim = 3.1415925
        m = V.done(V.eng.tensor_scalar(h, h, lim, -lim, ALU.min, ALU.max))
        A(m)
        return A.done(A.eng.activation(h, h, ACT.Sin))

    def hyena_filters(self):
        p, ins, c, sb = self.prog, self.ins, self.c, self.sb
        PE, A, V, G = self.PE, self.A, self.V, self.G
        with self.scope():
            featsT = sb("featsT", [N_FEAT, T])
            w1 = sb("w1", [N_FEAT, FILT])
            w2 = sb("w2", [FILT, FILT])
            w3 = sb("w3", [FILT, 4 * D_MAIN])
            vec = sb("vec", [FILT, 3])
            decay = sb("decay", [P, NT, D_MAIN])
            hs = sb("hs", [P, NT, NC2])
            hd = sb("hd", [P, NT, NC2])
            h1 = sb("h1", [FILT, T])
            h2 = sb("h2", [FILT, T])
            tmp = sb("tmp", [FILT, T])
            n = NT * 2 * 384
            taps, mag = (self.flat(t)[:, 0:n].rearrange("p (a d n) -> p a d n", a=NT, d=2) for t in (self.xn, self.xT))
            rn = sb("rn", [P, 384])
            skip = self.flat(self.mainT)[0:1, 0:NC2]
            ones = sb("ones2", [P, P])
            m = p.dma(G, "filt", [
                (featsT[:, :], c["featsT"]), (w1[:, :], ins["hy_filt_w1_2"][0]), (w2[:, :], ins["hy_filt_w2_2"][0]),
                (w3[:, :], ins["hy_filt_w3_2"][0]), (decay[:, :, :], c["decay"]),
                (skip, ins["hy_skip_2"].rearrange("a o c -> a (o c)"))]
                + [(vec[:, k:k + 1], ins[n].rearrange("a f -> f a")) for k, n in
                   enumerate(("hy_filt_b1_2", "hy_filt_b2_2", "hy_filt_freq_2"))])
            m_ones = V.done(V.eng.memset(ones[:, :], 1.0))
            PE(m)
            V(m)
            for w, src, b, dst in ((w1, featsT, 0, h1), (w2, h1, 1, h2)):
                i, ps = p.take()
                m = PE.done(PE.eng.matmul(ps[0:FILT, 0, 0:T], w[:, :], src[:, :], start=True, stop=True))
                m = self.sine(ps[0:FILT, 0, 0:T], vec[:, b:b + 1], vec[:, 2:3], dst[:, :], tmp[:, :], m)
                p.give(i, m)
                PE(m)
            PE(m_ones, self.m_dft)
            m_mag = m_taps = None
            for o in range(ORD):
                for q in range(2):
                    blk = slice(o * D_MAIN + q * 384, o * D_MAIN + (q + 1) * 384)
                    for tt in range(NT):
                        i, ps = p.take()
                        for d in range(2):
                            at = (2 * o + d) * D_MAIN + q * 384
                            last = PE.eng.matmul(ps[:, d, 0:384], h2[:, tt * P:(tt + 1) * P], w3[:, at:at + 384],
                                                 start=True, stop=True)
                        m = PE.done(last)
                        V(m, m_taps)
                        m = V.done(V.eng.tensor_tensor(taps[:, tt], ps[:, :, 0:384],
                                                       decay[:, tt, q * 384:(q + 1) * 384].unsqueeze(1)
                                                       .broadcast_to((P, 2, 384)), ALU.mult))
                        p.give(i, m)
                        A(m, m_mag)
                        m = A.done(A.eng.activation(mag[:, tt], taps[:, tt], ACT.Abs))
                    PE(m)
                    i, ps = p.take()
                    for n in range(4):
                        last = PE.eng.matmul(ps[:, 0, 0:384], ones[:, :], mag[:, n // 2, n % 2, :], start=n == 0, stop=n == 3)
                    m = m_mag = PE.done(last)
                    V(m)
                    m = V.done(V.eng.tensor_scalar(rn[:, :], ps[:, 0, 0:384], 1e-6, None, ALU.add))
                    p.give(i, m)
                    V(m)
                    V.done(V.eng.reciprocal(rn[:, :], rn[:, :]))
                    V.done(V.eng.tensor_tensor(hs[:, :, blk], taps[:, :, 0, :], taps[:, :, 1, :], ALU.add))
                    m_taps = V.done(V.eng.tensor_tensor(hd[:, :, blk], taps[:, :, 0, :], taps[:, :, 1, :], ALU.subtract))
                    V(m_taps)
                    r = rn[:, :].unsqueeze(1).broadcast_to((P, NT, 384))
                    V.done(V.eng.tensor_tensor(hs[:, :, blk], hs[:, :, blk], r, ALU.mult))
                    m = V.done(V.eng.tensor_tensor(hd[:, :, blk], hd[:, :, blk], r, ALU.mult))
            V(m)
            m = V.done(V.eng.tensor_tensor(hs[0:1, 0, :], hs[0:1, 0, :], skip, ALU.add))
            PE(m)
            for fc in range(4):
                src = hs if fc < 2 else hd
                for q in range(0, 4, 2):
                    i, ps = p.take()
                    for b in range(2):
                        for tt in range(NT):
                            last = PE.eng.matmul(ps[:, b, 0:384], self.dft[:, tt, fc * P:(fc + 1) * P],
                                                 src[:, tt, (q + b) * 384:(q + b + 1) * 384], start=tt == 0, stop=tt == 1)
                    m = PE.done(last)
                    o = self.spec[:, fc, q * 384:(q + 2) * 384].rearrange("p (b n) -> p b n", b=2)
                    m = self.copy(o, ps[:, :, 0:384], m, A if q else V)
                    p.give(i, m)
            V(*[e.last for e in (A, V)])
            V.done(V.eng.tensor_copy(self.spec_i0[:, :], self.spec[:, 0, :]))
            V.done(V.eng.memset(self.spec[0:1, 2, :], 0.0))
            for q in range(0, 4, 2):
                i, ps = p.take()
                for b in range(2):
                    for tt in range(NT):
                        last = PE.eng.matmul(ps[0:1, b, 0:384], self.dft[:, tt, T:T + 1],
                                             hs[:, tt, (q + b) * 384:(q + b + 1) * 384], start=tt == 0, stop=tt == 1)
                m = PE.done(last)
                V(m, V.last)
                m = V.done(V.eng.tensor_copy(self.spec_i0[0:1, q * 384:(q + 2) * 384].rearrange("p (b n) -> p b n", b=2),
                                             ps[0:1, :, 0:384]))
                p.give(i, m)

    def spectrum(self, z, zf, m):
        PE, A, V, p = self.PE, self.A, self.V, self.prog
        PE(*m)
        marks = []
        for fc in range(4):
            i, ps = p.take()
            for b in range(2):
                for tt in range(NT):
                    last = PE.eng.matmul(ps[:, b, 0:384], self.dft[:, tt, fc * P:(fc + 1) * P],
                                         z[:, tt, b * 384:(b + 1) * 384], start=tt == 0, stop=tt == 1)
            m = PE.done(last)
            m = self.copy(zf[:, fc, :].rearrange("p (b n) -> p b n", b=2), ps[:, :, 0:384], m, A)
            p.give(i, m)
            marks.append(m)
        return marks

    def filtered(self, o, zf, pf, tmp, marks):
        V, G = self.V, self.G
        k = slice(o * D_MAIN, (o + 1) * D_MAIN)
        sp = self.spec
        V(*marks)
        G(*marks)
        G(V.last)
        mg = [G.done(G.eng.tensor_tensor(tmp[:, f, :], zf[:, 2 + f, :], sp[:, 2 + f, k], ALU.mult)) for f in range(2)]
        V.done(V.eng.tensor_tensor(pf[0], zf[:, 0:2, :], sp[:, 0:2, k], ALU.mult))
        V.done(V.eng.tensor_tensor(pf[1], zf[:, 0:2, :], sp[:, 2:4, k], ALU.mult))
        V(V.last, mg[1])
        m = V.done(V.eng.tensor_tensor(pf[0], pf[0], tmp, ALU.subtract))
        V(m)
        V.done(V.eng.tensor_tensor(tmp[:, 0, :], zf[:, 2, :], self.spec_i0[:, k], ALU.mult))
        V.done(V.eng.tensor_tensor(tmp[:, 1, :], zf[:, 3, :], sp[:, 1, k], ALU.mult))
        V(V.last)
        return V.done(V.eng.tensor_tensor(pf[1], pf[1], tmp, ALU.add))

    def hyena(self):
        p, ins, sb = self.prog, self.ins, self.sb
        PE, A, V, G = self.PE, self.A, self.V, self.G
        NU = 3 * NM
        with self.scope():
            self.dft = sb("dft", [P, NT, 2 * T])
            self.idft = sb("idft", [P, 4, T])
            self.spec = sb("spec", [P, 4, NC2])
            self.spec_i0 = sb("spec_i0", [P, NC2])
            self.m_dft = p.dma(G, "dft", [(self.dft[:, :, :], self.c["dft"]), (self.idft[:, :, :], self.c["idft"])])
            self.hyena_filters()
            uT = sb("uT", [P, NU, T + 2])
            ucT = sb("ucT", [P, NU, T])
            xv = sb("xv", [P, NT, 2 * D_MAIN])
            V.done(V.eng.memset(uT[:, :, 0:1], 0.0))
            V.done(V.eng.memset(uT[:, :, T + 1:T + 2], 0.0))
            V(self.m_xs[0], self.m_xs[1])
            A(*self.m_xs)
            xn = self.normed_rows(self.x, self.xn)
            PE(*self.turned(self.xn, self.xT, self.gains("mix_norm_g_2", 0), *xn))
            w = ins["hy_w_in_2"][0]
            sw = self.par[:, 1, :]
            uc_marks = {}

            def streams(c0):
                def f(n, ps, m):
                    m = self.copy(uT[:, c0:c0 + n, 1:T + 1], ps, m, A)
                    V(m)
                    for k in range(c0, c0 + n):
                        o = ucT[:, k, :]
                        V.done(V.eng.tensor_scalar(o, uT[:, k, 0:T], sw[:, k:k + 1], None, ALU.mult))
                    for j in (1, 2):
                        for k in range(c0, c0 + n):
                            V(V.last)
                            uc_marks[k] = V.done(V.eng.scalar_tensor_tensor(
                                out=ucT[:, k, :], in0=uT[:, k, j:j + T], scalar=sw[:, j * NU + k:j * NU + k + 1],
                                in1=ucT[:, k, :], op0=ALU.mult, op1=ALU.add))
                    return [m]
                return f
            order = [12, 15, 0, 3, 6, 9]
            for c0 in order:
                self.project_T(w[:, c0 * P:(c0 + 3) * P], self.xT, 384, streams(c0))
            self.project_T(w[:, NU * P:NU * P + 256], self.xT, 256, self.copy_to(self.cqT))
            m_cq = self.m_copy
            chunks = list(range(NM)) + list(range(2 * NM, 3 * NM))
            xv_marks = []
            for g in (8, 4, 0):
                i, ps = p.take()
                for q in range(4):
                    k = chunks[g + q]
                    PE(uc_marks[k])
                    for tt in range(NT):
                        last = PE.eng.transpose(ps[:, tt, q * P:(q + 1) * P], ucT[:, k, tt * P:(tt + 1) * P], self.ident[:, :])
                m = PE.done(last)
                ms = [self.copy(xv[:, tt, g * P:(g + 4) * P], ps[:, tt, :], m, (A, V)[tt]) for tt in range(NT)]
                p.give(i, *ms)
                xv_marks += ms
            room = self.flat(uT)
            zf = room[:, 0:4 * D_MAIN].rearrange("p (a b) -> p a b", a=4)
            tmp = room[:, 4 * D_MAIN:6 * D_MAIN].rearrange("p (a b) -> p a b", a=2)
            pf = [ucT[:, k:k + NM, :].rearrange("p a b -> p (a b)").rearrange("p (a b) -> p a b", a=2) for k in (0, 2 * NM)]
            z = xv[:, :, D_MAIN:]
            A(*uc_marks.values())
            m = self.filtered(0, zf, pf, tmp, self.spectrum(z, zf, xv_marks))
            PE(m_cq)
            PE(m)
            for tt in range(NT):
                i, ps = p.take()
                for b in range(2):
                    for fc in range(4):
                        last = PE.eng.matmul(ps[:, b, 0:384], self.idft[:, fc, tt * P:(tt + 1) * P],
                                             pf[fc // 2][:, fc % 2, b * 384:(b + 1) * 384], start=fc == 0, stop=fc == 3)
                m = PE.done(last)
                V(m)
                m = V.done(V.eng.tensor_tensor(z[:, tt].rearrange("p (b n) -> p b n", b=2), ps[:, :, 0:384],
                                               xv[:, tt, 0:D_MAIN].rearrange("p (b n) -> p b n", b=2), ALU.mult))
                p.give(i, m)
            m_sp = self.spectrum(z, zf, [m])
            m_cross = self.attend(self.cross_jobs(0))
            m = self.filtered(1, zf, pf, tmp, m_sp)
            PE(m)
            for c0 in (0, 4):
                n = min(4, NM - c0)
                i, ps = p.take()
                for q in range(n):
                    for fc in range(4):
                        last = PE.eng.matmul(ps[:, q // 2, (q % 2) * T:(q % 2) * T + T],
                                             pf[fc // 2][:, fc % 2, (c0 + q) * P:(c0 + q + 1) * P], self.idft[:, fc, :],
                                             start=fc == 0, stop=fc == 3)
                m = PE.done(last)
                V(m)
                m = V.done(V.eng.tensor_tensor(self.mainT[:, c0:c0 + n, :],
                                               ps.rearrange("p a (b t) -> p (a b) t", t=T)[:, 0:n, :],
                                               ucT[:, NM + c0:NM + c0 + n, :], ALU.mult))
                p.give(i, m)
            self.m_xs = self.accumulate(self.row_panels(ins["w_out_2"][0], ND), self.mainT, self.x, [m, *m_cross])

    def gqa(self):
        p, ins, sb = self.prog, self.ins, self.sb
        PE, A, V, G = self.PE, self.A, self.V, self.G
        NH = N_QH + N_KV
        W = (NH + N_KV) * HD
        with self.scope():
            qkv = sb("qkv", [P, NT, W])
            gain = sb("gain", [P, 2, HD])
            cs = sb("cs", [P, NT, 2, 2, 16])
            tmp = sb("tmp3", [P, 4, 512])
            dup = sb("dup", [P, NT, N_KV, 2, HD])
            qT = sb("qT", [P, NM, T])
            kT = sb("kT", [P, N_KV, T])
            m_in = p.dma(G, "gqa", [
                (gain[:, 0, :], ins["at_q_norm_g_2"].broadcast_to((P, HD))),
                (gain[:, 1, :], ins["at_k_norm_g_2"].broadcast_to((P, HD))),
                (cs[:, :, :, :, :], self.c["axial"])])
            V(*self.m_xs)
            A(*self.m_xs)
            xn = self.normed_rows(self.x, self.xn)
            PE(*self.turned(self.xn, self.xT, self.gains("mix_norm_g_2", 1), *xn))
            w = ins["at_w_in_2"][0]
            for c in range(0, W, 384):
                n = min(384, W - c)
                self.project(w[:, c:c + n], self.xT, n, lambda ps, m, c=c, n=n: [self.copy(qkv[:, :, c:c + n], ps, m)])
            m_qkv = self.m_copy
            self.project_T(w[:, W:W + 256], self.xT, 256, self.copy_to(self.cqT))
            V(m_qkv, m_in)
            marks = []
            for tt in range(NT):
                x = qkv[:, tt, 0:NH * HD]
                x3 = x.rearrange("p (h e) -> p h e", e=HD)
                sq = tmp[:, 0:2, :].rearrange("p a b -> p (a b)")
                V(V.last)
                V.done(V.eng.tensor_tensor(sq, x, x, ALU.mult))
                V(V.last)
                m = V.done(V.eng.tensor_reduce(self.st[:, 32:48], sq.rearrange("p (h e) -> p h e", e=HD), AX, ALU.add))
                m = self.rstd(self.st[:, 32:48], HD, self.st[:, 48:64], m)
                V(m)
                V.done(V.eng.tensor_tensor(x3, x3, self.st[:, 48:64].unsqueeze(2).broadcast_to((P, NH, HD)), ALU.mult))
                V(V.last)
                for k, (a, b) in enumerate(((0, N_QH), (N_QH, NH))):
                    V.done(V.eng.tensor_tensor(x3[:, a:b], x3[:, a:b], gain[:, k, :].unsqueeze(1).broadcast_to((P, b - a, HD)), ALU.mult))
                V(V.last)
                v = x.rearrange("p (h a s f) -> p s h a f", a=2, s=2, f=16)
                t = [tmp[:, k, :].rearrange("p (h a f) -> p h a f", a=2, f=16) for k in range(4)]
                c, s = (cs[:, tt, k].unsqueeze(1).broadcast_to((P, NH, 2, 16)) for k in range(2))
                V.done(V.eng.tensor_tensor(t[0], v[:, 0], c, ALU.mult))
                V.done(V.eng.tensor_tensor(t[1], v[:, 1], s, ALU.mult))
                V.done(V.eng.tensor_tensor(t[2], v[:, 0], s, ALU.mult))
                V.done(V.eng.tensor_tensor(t[3], v[:, 1], c, ALU.mult))
                V(V.last)
                V.done(V.eng.tensor_tensor(v[:, 0], t[0], t[1], ALU.subtract))
                V.done(V.eng.tensor_tensor(v[:, 1], t[2], t[3], ALU.add))
                V(V.last)
                marks.append(V.done(V.eng.tensor_copy(dup[:, tt], x3[:, N_QH:NH].unsqueeze(2).broadcast_to((P, N_KV, 2, HD)))))
            PE(*marks)
            srcs = [lambda tt, c=c: qkv[:, tt, c * P:(c + 1) * P] for c in range(NM)]
            srcs += [lambda tt, c=c: dup[:, tt, c].rearrange("p a b -> p (a b)") for c in range(N_KV)]
            dst = [qT[:, c, :] for c in range(NM)] + [kT[:, c, :] for c in range(N_KV)]
            for g, n in ((0, 4), (4, 2), (6, 4)):
                i, ps = p.take()
                for q in range(n):
                    for tt in range(NT):
                        last = PE.eng.transpose(ps[:, q // 2, (q % 2) * T + tt * P:(q % 2) * T + tt * P + P], srcs[g + q](tt), self.ident[:, :])
                m = PE.done(last)
                o = qT[:, g:g + n, :] if g < NM else kT[:, g - NM:g - NM + n, :]
                m = self.copy(o, ps.rearrange("p a (b t) -> p (a b) t", t=T)[:, 0:n, :], m)
                p.give(i, m)
            PE(m)
            per = N_QH // N_KV
            jobs = [(tt, lambda h, g=g: qT[self.half(h), 2 * g + h // 2, :],
                     lambda h, g=g: kT[self.half(h), (4 * g + h) // per, :],
                     lambda kt, h, g=g: qkv[:, kt, (NH + (4 * g + h) // per) * HD:(NH + (4 * g + h) // per + 1) * HD],
                     self.mainT[:, 2 * g:2 * g + 2, :]) for g in range(3) for tt in range(NT)]
            m = self.attend(self.cross_jobs(1) + jobs)
            self.m_xs = self.accumulate(self.row_panels(ins["w_out_2"][1], ND), self.mainT, self.x, m)

    def experts(self, i):
        p, ins, sb = self.prog, self.ins, self.sb
        PE, A, V, G = self.PE, self.A, self.V, self.G
        NG = N_EXP // 4
        with self.scope():
            aff = sb("aff", [P, NT, N_EXP])
            affT = sb("affT", [N_EXP, T])
            work = sb("work2", [N_EXP, T])
            slot = sb("slot", [N_EXP, T])
            ones = sb("ones3", [N_EXP, T])
            top8 = sb("top8b", [N_EXP, 8])
            slots = sb("slots", [P, NT, N_EXP])
            pick = sb("pick", [P, NT, N_EXP * CAP])
            share = sb("share", [P, NT, N_EXP * CAP])
            shareT = sb("shareT", [P, NG, T])
            pick_g = sb("pick_g", [P, NT, P])
            share_g = sb("share_g", [P, T])
            xgT = sb("xgT", [P, ND, P])
            sig = sb("sig", [P, 2, 256])
            hid = sb("hid", [P, 2, 256])
            hidT = sb("hidT", [P, 2, 2, 96])
            y = sb("y", [P, 2, 512])
            m_ones = V.done(V.eng.memset(ones[:, :], 1.0))
            V(*self.m_xs)
            A(*self.m_xs)
            xn = self.normed_rows(self.x, self.xn)
            gain = self.gains("ffn_norm_g_2", i)
            PE(*self.turned(self.xn, self.xT, gain, *xn), self.m_c2)
            k, ps = p.take()
            for tt in range(NT):
                for d in range(ND):
                    last = PE.eng.matmul(ps[:, 0, tt * N_EXP:(tt + 1) * N_EXP], self.xT[:, d, tt * P:(tt + 1) * P],
                                         self.router[:, i, d, :], start=d == 0, stop=d == ND - 1)
            m = PE.done(last)
            s = self.st
            V(m)
            af = aff[:, :, :]
            lg = ps[:, 0, 0:NT * N_EXP].rearrange("p (a e) -> p a e", a=NT)
            V.done(V.eng.tensor_reduce(s[:, 0:NT], lg, AX, ALU.max))
            V(V.last)
            m = V.done(V.eng.tensor_tensor(af, lg, s[:, 0:NT].unsqueeze(2).broadcast_to((P, NT, N_EXP)), ALU.subtract))
            p.give(k, m)
            A(m)
            m = A.done(A.eng.activation(af, af, ACT.Exp))
            V(m)
            V.done(V.eng.tensor_reduce(s[:, 4:4 + NT], af, AX, ALU.add))
            V(V.last)
            V.done(V.eng.reciprocal(s[:, 4:4 + NT], s[:, 4:4 + NT]))
            V(V.last)
            m = V.done(V.eng.tensor_tensor(af, af, s[:, 4:4 + NT].unsqueeze(2).broadcast_to((P, NT, N_EXP)), ALU.mult))
            PE(m)
            k, ps = p.take()
            for tt in range(NT):
                last = PE.eng.transpose(ps[0:N_EXP, 0, tt * P:(tt + 1) * P], aff[:, tt, :], self.ident[:, :])
            m = PE.done(last)
            V(m)
            m = V.done(V.eng.tensor_copy(affT[:, :], ps[0:N_EXP, 0, 0:T]))
            p.give(k, m)
            for r in range(CAP // 8):
                src = affT if r == 0 else work
                V(V.last)
                V.done(V.eng.max(out=top8[:, :], in_=src[:, :]))
                V(V.last)
                V.done(V.eng.match_replace(out=work[:, :], in_to_replace=top8[:, :], in_values=src[:, :], imm_value=TINY))
            V(V.last)
            V.done(V.eng.tensor_scalar(work[:, :], work[:, :], 2 * NEG, None, ALU.is_lt))
            V(V.last, m_ones)
            V.done(V.eng.tensor_tensor_scan(slot[:, :], ones[:, :], work[:, :], 0.0, ALU.mult, ALU.add))
            V(V.last)
            m = V.done(V.eng.tensor_tensor(slot[:, :], slot[:, :], work[:, :], ALU.mult))
            PE(m)
            k, ps = p.take()
            for tt in range(NT):
                last = PE.eng.transpose(ps[:, 0, tt * N_EXP:(tt + 1) * N_EXP], slot[:, tt * P:(tt + 1) * P], self.ident[0:N_EXP, 0:N_EXP])
            m = PE.done(last)
            V(m)
            m = V.done(V.eng.tensor_copy(slots[:, :, :], ps[:, 0, 0:NT * N_EXP].rearrange("p (a e) -> p a e", a=NT)))
            p.give(k, m)
            V(m, self.m_c2)
            for tt in range(NT):
                pk = pick[:, tt].rearrange("p (e r) -> p e r", r=CAP)
                V.done(V.eng.tensor_tensor(pk, slots[:, tt, :].unsqueeze(2).broadcast_to((P, N_EXP, CAP)),
                                           self.iota[:, :].unsqueeze(1).broadcast_to((P, N_EXP, CAP)), ALU.is_equal))
            V(V.last)
            for tt in range(NT):
                pk, sh = (t[:, tt].rearrange("p (e r) -> p e r", r=CAP) for t in (pick, share))
                m = V.done(V.eng.tensor_tensor(sh, pk, aff[:, tt, :].unsqueeze(2).broadcast_to((P, N_EXP, CAP)), ALU.mult))
            PE(m)
            k, ps = p.take()
            for g in range(NG):
                for tt in range(NT):
                    last = PE.eng.transpose(ps[:, g // 2, (g % 2) * T + tt * P:(g % 2) * T + tt * P + P],
                                            share[:, tt, g * P:(g + 1) * P], self.ident[:, :])
            m = PE.done(last)
            m = self.copy(shareT[:, :, :], ps.rearrange("p a (b t) -> p (a b) t", t=T), m)
            p.give(k, m)

            ds = bass.ds
            with p.loop_of(f"experts{i}", NG) as g:
                self.expert_group(i, g, ds, pick, pick_g, shareT, share_g, xgT, sig, hid, hidT, y, gain)

    def expert_group(self, i, g, ds, pick, pick_g, shareT, share_g, xgT, sig, hid, hidT, y, gain):
        p, ins = self.prog, self.ins
        PE, A, V = self.PE, self.A, self.V
        V.done(V.eng.tensor_copy(pick_g[:, :, :], pick[:, :, ds(g * P, P)]))
        m_sh = V.done(V.eng.tensor_copy(share_g[:, :], shareT[:, ds(g, 1), :].rearrange("p a t -> p (a t)")))
        PE(m_sh)
        k, ps = p.take()
        for d in range(ND):
            for tt in range(NT):
                last = PE.eng.matmul(ps[:, d // 4, (d % 4) * P:(d % 4 + 1) * P], self.xn[:, tt, d * P:(d + 1) * P],
                                     pick_g[:, tt, :], start=tt == 0, stop=tt == 1)
        m = PE.done(last)
        A(m)
        V(m)
        for d in range(ND):
            o, s, gn = xgT[:, d, :], ps[:, d // 4, (d % 4) * P:(d % 4 + 1) * P], gain[:, d:d + 1]
            if d < 4:
                a = A.done(A.eng.activation(o, s, ACT.Copy, scale=gn))
            else:
                v = V.done(V.eng.tensor_scalar(o, s, gn, None, ALU.mult))
        p.give(k, a, v)
        PE(a, v)
        ky, py = p.take()
        state = {}

        def up(e):
            k, ps = p.take()
            for b, name in enumerate(("exp_w_gate_2", "exp_w_up_2")):
                w = ins[name][i, ds(g * 4 + e, 1), :, :].rearrange("a d n -> (a d) n")
                for r0 in range(0, ND, 4):
                    u = self.unit(w[r0 * P:(r0 + 4) * P, :], 4, E_FF)
                    for r in range(4):
                        for j in range(3):
                            last = PE.eng.matmul(ps[32 * j:32 * j + 32, b, 0:256], xgT[:, r0 + r, 32 * e:32 * e + 32],
                                                 u[:, r, j * 256:(j + 1) * 256],
                                                 start=r0 + r == 0, stop=r0 + r == ND - 1)
                    m = PE.done(last, p.used)
                if b == 0:
                    A(m, state.get(("free", e % 2)))
                    m_sig = A.done(A.eng.activation(sig[0:96, e % 2, :], ps[0:96, 0, 0:256], ACT.Sigmoid))
                    V(m_sig)
                    V.done(V.eng.tensor_tensor(sig[0:96, e % 2, :], ps[0:96, 0, 0:256], sig[0:96, e % 2, :], ALU.mult))
            V(m, V.last, state.get(("free", e % 2)))
            m = V.done(V.eng.tensor_tensor(hid[0:96, e % 2, :], ps[0:96, 1, 0:256], sig[0:96, e % 2, :], ALU.mult))
            p.give(k, m)
            state[e] = m

        def down(e):
            PE(state[e])
            k, ps = p.take()
            for c in range(2):
                last = PE.eng.transpose(ps[:, 0, c * 96:(c + 1) * 96], hid[0:96, e % 2, c * P:(c + 1) * P], self.ident[0:96, 0:96])
            m = PE.done(last)
            state["free", e % 2] = m
            A(state.get(("t", e % 2)))
            m = self.copy(hidT[:, e % 2].rearrange("p a b -> p (a b)"), ps[:, 0, 0:192], m, A)
            p.give(k, m)
            PE(m)
            w = ins["exp_w_down_2"][i, ds(g * 4 + e, 1), :, :].rearrange("a d n -> (a d) n")
            for r0 in range(0, NM, 3):
                u = self.unit(w[r0 * P:(r0 + 3) * P, :], 3, D)
                for r in range(3):
                    j, c = (r0 + r) // 2, (r0 + r) % 2
                    for b in range(2):
                        last = PE.eng.matmul(py[32 * e:32 * e + 32, b, :], hidT[:, e % 2, c, 32 * j:32 * j + 32],
                                             u[:, r, b * 512:(b + 1) * 512], start=r0 + r == 0, stop=r0 + r == NM - 1)
                m = PE.done(last, p.used)
            state["t", e % 2] = m
            return m
        up(0)
        for e in range(1, 4):
            up(e)
            down(e - 1)
        m = down(3)
        ma = self.copy(y[:, 0, :], py[:, 0, :], m, A)
        mv = self.copy(y[:, 1, :], py[:, 1, :], m, V)
        p.give(ky, ma, mv)
        PE(ma, mv)
        for tt in range(NT):
            k, ps = p.take()
            for b in range(2):
                last = PE.eng.matmul(ps[:, b, :], share_g[:, tt * P:(tt + 1) * P], y[:, b, :], start=True, stop=True)
            m = PE.done(last)
            V(m)
            m = V.done(V.eng.tensor_tensor(self.x[:, tt, :], self.x[:, tt, :], ps.rearrange("p a b -> p (a b)"), ALU.add))
            p.give(k, m)
        self.m_xs = [m]

    def block2(self):
        self.block2_memory()
        self.memory_kv()
        self.hyena()
        self.experts(0)
        self.gqa()
        self.experts(1)

    def finish(self):
        p, V, A = self.prog, self.V, self.A
        with self.scope():
            g = self.sb("final_gain", [P, D])
            m = p.dma(self.G, "final", [(g[:, :], self.ins["final_norm_g_2"].unsqueeze(0).broadcast_to((P, D)))])
            V(m)
            marks = self.normed_rows(self.x, self.xn, *self.m_xs)
            V(*marks)
            stored = Counter(p, "stored")
            out = self.out[0].rearrange("(a p) d -> p a d", p=P)
            for tt in range(NT):
                m = V.done(V.eng.tensor_tensor(self.xn[:, tt, :], self.xn[:, tt, :], g[:, :], ALU.mult))
                self.prog.sp(m)
                self.nc.sync.dma_start(out[:, tt, :], self.xn[:, tt, :]).then_inc(stored.sem, 16)
                stored.count += 16
            self.prog.sp(stored.mark())

    def run(self):
        self.setup()
        with self.scope():
            self.block1()
        self.block2()
        self.finish()
        self.room.close()


_DRAM_CONSTS = ("ident", "negu", "strict", "levels", "dsa_cos", "dsa_sin")


def constants():
    f = np.float32
    out = {"ident": np.eye(P, dtype=f)}
    s = np.arange(P)
    out["negu"] = -(s[:, None] >= s[None, :]).astype(f)
    out["strict"] = (s[:, None] < s[None, :]).astype(f)
    r = s % 32
    lv = []
    for m in MASKED:
        t = np.arange(32)
        if m:
            same = (r[:, None] // (2 * m)) == (t[None, :] // (2 * m))
            lv.append(same & (r[:, None] % (2 * m) < m) & (t[None, :] % (2 * m) >= m))
        else:
            lv.append(r[:, None] == t[None, :])
    out["levels"] = np.stack(lv, 1).astype(f)
    half = ROT // 2
    inv = f(500000.0) ** (-(np.arange(half, dtype=f) * f(2.0)) / f(ROT))
    ang = np.arange(T, dtype=f)[:, None] * inv[None, :].astype(f)
    cos, sin = (np.tile(g(ang.astype(np.float64))[:, None, :], (1, NBLK, 1)) for g in (np.cos, np.sin))
    cos[:, 7], sin[:, 7] = 1.0, 0.0
    for n, a in (("dsa_cos", cos), ("dsa_sin", sin)):
        out[n] = np.ascontiguousarray(a.reshape(NT, P, NBLK * half).transpose(1, 0, 2)).astype(f)
    out["iota"] = np.broadcast_to(np.arange(1, CAP + 1, dtype=f), (P, CAP)).copy()
    t, k = np.arange(T)[:, None], np.arange(T)[None, :]
    ph = np.pi * ((t * k) % (2 * T)) / T
    fwd = np.concatenate([np.cos(ph), -np.sin(ph)], 1)
    fwd[:, T] = (-1.0) ** np.arange(T)
    out["dft"] = np.ascontiguousarray(fwd.reshape(NT, P, 2 * T).transpose(1, 0, 2)).astype(f)
    scale = np.full(2 * T, 2.0)
    scale[0] = scale[T] = 1.0
    inv_ = (fwd * scale / (2 * T)).T
    out["idft"] = np.ascontiguousarray(inv_.reshape(4, P, T).transpose(1, 0, 2)).astype(f)
    tl = np.linspace(0.0, 1.0, T, dtype=f)[:, None]
    wl = (f(2.0 * math.pi) * np.arange(T, dtype=f)[:, None] / f(T)).astype(f)
    bands = np.linspace(1e-4, 15, 16, dtype=f)[None, :]
    bw = (bands * wl).astype(np.float64)
    out["featsT"] = np.ascontiguousarray(np.concatenate([tl, np.cos(bw), -np.sin(bw)], 1).T).astype(f)
    lo, hi = math.log(1e-2) / 1.5, math.log(1e-2) / 0.3
    dec = np.exp(-tl.astype(np.float64) * np.abs(np.linspace(lo, hi, D_MAIN, dtype=f)))
    out["decay"] = np.ascontiguousarray(dec.reshape(NT, P, D_MAIN).transpose(1, 0, 2)).astype(f)
    pos = np.stack([np.repeat(np.arange(T // 64), 64), np.tile(np.arange(64), T // 64)], 1).astype(f)
    inv2 = f(1.0) / (f(10000.0) ** (np.arange(0, 32, 2, dtype=f) / f(32)))
    an = (pos[:, :, None] * inv2).astype(f).astype(np.float64)
    ax = np.stack([np.cos(an), np.sin(an)], 1).reshape(NT, P, 2, 2, 16).transpose(1, 0, 2, 3, 4)
    out["axial"] = np.ascontiguousarray(ax).astype(f)
    return out


OUT = "out_0_dram"


def build(new_bass, arrays):
    per_iteration = {}
    for _ in range(2):
        nc = new_bass()
        aps = {n: nc.dram_tensor(n, a.shape, F32, kind="ExternalInput").ap() for n, a in arrays.items()}
        ins = {n[3:]: a for n, a in aps.items() if n.startswith("in_")}
        consts = {n[6:]: a for n, a in aps.items() if n.startswith("const_")}
        out = nc.dram_tensor(OUT, (1, T, D), F32, kind="ExternalOutput").ap()
        Kernel(nc, per_iteration, ins, consts, out).run()
    return nc


def kernel(**inputs):
    import concourse.bacc as bacc
    from concourse.bass_utils import run_bass_kernel_spmd

    arrays = {f"in_{n}": np.ascontiguousarray(a) for n, a in inputs.items()}
    arrays |= {f"const_{n}": a for n, a in constants().items()}
    nc = build(lambda: bacc.Bacc("TRN2", target_bir_lowering=False, num_devices=1), arrays)
    r = run_bass_kernel_spmd(nc, [arrays], core_ids=[0])
    return r.results[0][OUT]
```

```python
import math
from contextlib import ExitStack, contextmanager

import numpy as np

import concourse.bass as bass
from concourse import mybir

F32 = mybir.dt.float32
I32 = mybir.dt.int32
ALU = mybir.AluOpType
ACT = mybir.ActivationFunctionType
AX = mybir.AxisListType.X

P = 128
T = 256
NT = T // P
D = 1024
ND = D // P
DEPTH = 2
HD = 64
EPS = 1e-6
NEG = -1e30
N_SB = N_DSA = 6
N_IDX = 8
K_TOP = min(256, T // 4)
N_HG = 4
HG_DK = 128
D_FF = 4 * D
ROT = HD // 4
F_MIN = 1e-12
IDX_SCALE = (HD * N_IDX) ** -0.5
C_SQ, C_SK, C_SV = 0, 384, 768
C_DSA = 1152
W_DSA = 384 + 64 + 64 + 512 + 64 + 8
C_HQ = C_DSA + W_DSA
C_HI = C_HQ + 1024
C_GATE = C_HI + 512
D_IN = C_GATE + 3 * D
NBLK = 17
HG_LEVELS = (128, 64, 32, 16, 8, 4, 2, 1)
MASKED = (16, 8, 4, 2, 1, 0)
D_MAIN = 768
NM = D_MAIN // P
N_QH, N_KV, N_MEM = 12, 4, 4
N_EXP = 16
CAP = 2 * T // N_EXP
E_FF = 768
N_FEAT = 33
FILT = 64
ORD = 2
NC2 = ORD * D_MAIN
SLOTS = 6
MORE = 6
SLOT = 3072
TINY = -3.0e38


class Counter:

    def __init__(self, prog, name, start=0):
        self.prog, self.name, self.count = prog, name, start
        self.sem = prog.nc.alloc_semaphore(name)
        prog.counters.append(self)

    def mark(self):
        return Mark(self, self.count, self.prog.loop)


class Mark:

    def __init__(self, counter, count, loop):
        self.counter, self.count, self.loop = counter, count, loop

    def value(self):
        loop = self.loop
        if loop is None:
            return self.count
        per = loop.per.get(self.counter.name, 0)
        if loop.closed:
            return self.count + (loop.n - 1) * per
        return loop.reg * per + self.count if per else self.count


class Loop:
    def __init__(self, name, n, per):
        self.name, self.n, self.per, self.closed, self.reg = name, n, per, False, None


class Engine:

    def __init__(self, prog, eng, name):
        self.prog, self.eng, self.name = prog, eng, name
        self.sig = Counter(prog, "s_" + name)
        self.seen = {}

    def __call__(self, *marks):
        for m in marks:
            if m is None:
                continue
            key = m.counter.name
            if m.loop is not None and m.loop.closed:
                m = Mark(m.counter, m.value(), None)
            got = self.seen.get((key, m.loop), -1)
            if got >= m.count:
                continue
            self.seen[(key, m.loop)] = m.count
            self.eng.wait_ge(m.counter.sem, m.value())
        return self.eng

    def done(self, inst, counter=None):
        s = counter or self.sig
        inst.then_inc(s.sem, 1)
        s.count += 1
        return s.mark()

    @property
    def last(self):
        return self.sig.mark()


class Program:

    def __init__(self, nc, per_iteration):
        self.nc, self.loop, self.counters = nc, None, []
        self.per_iteration = per_iteration
        self.pe = Engine(self, nc.tensor, "pe")
        self.act = Engine(self, nc.scalar, "act")
        self.dve = Engine(self, nc.vector, "dve")
        self.pool = Engine(self, nc.gpsimd, "pool")
        self.sp = Engine(self, nc.sync, "sp")
        self.engines = (self.pe, self.act, self.dve, self.pool)
        self.used = Counter(self, "used", SLOTS)
        nc.tensor.sem_inc(self.used.sem, SLOTS)
        self.landed = [Counter(self, f"landed{i}") for i in range(SLOTS + MORE)]
        self.ring = nc.alloc_sbuf_tensor("ring", [P, SLOTS, SLOT], F32)
        self.order = [(self.ring, i) for i in range(SLOTS)]
        self.units_used = 0
        self.psum = nc.alloc_psum_tensor("psum", [P, 4, 2, 512], F32)
        self.free_marks = [[] for _ in range(4)]
        self.free_order = [0, 1, 2, 3]

    def meet(self):
        marks = [e.sig.mark() for e in self.engines] + [self.used.mark()]
        for e in self.engines:
            e(*[m for m in marks if m.count])
        self.free_marks = [[] for _ in range(4)]

    @contextmanager
    def loop_of(self, name, n):
        loop = Loop(name, n, self.per_iteration.get(name, {}))
        start = {s.name: s.count for s in self.counters}
        with self.nc.Fori(0, n) as i:
            loop.reg = i
            self.loop = loop
            self.meet()
            yield i
        self.loop = None
        gave = {s.name: s.count - start.get(s.name, 0) for s in self.counters}
        gave = {k: v for k, v in gave.items() if v}
        if name in self.per_iteration:
            assert gave == self.per_iteration[name]
        self.per_iteration[name] = gave
        loop.per, loop.closed = gave, True
        for s in self.counters:
            s.count += (n - 1) * gave.get(s.name, 0)
        self.units_used += (n - 1) * gave.get("used", 0)

    def dma(self, engine, name, pairs, *after):
        s = Counter(self, f"in_{name}")
        engine(*after)
        for to, of in pairs:
            engine.eng.dma_start(to, of).then_inc(s.sem, 16)
            s.count += 16
        return s.mark()

    def unit(self, src, rows, cols):
        slot = self.order.pop(0)
        self.order.append(slot)
        ring, at = slot
        need = Mark(self.used, self.units_used + 1, self.loop)
        self.sp(need)
        s = self.landed[at if ring is self.ring else SLOTS + at]
        view = ring[:, at, 0:rows * cols].rearrange("p (c n) -> p c n", c=rows)
        self.nc.sync.dma_start(view, src.rearrange("(c p) n -> p c n", p=P)).then_inc(s.sem, 16)
        s.count += 16
        self.units_used += 1
        return view, s.mark()

    def grow(self, more):
        self.pe.eng.sem_inc(self.used.sem, MORE)
        self.used.count += MORE
        self.order += [(more, i) for i in range(MORE)]

    def shrink(self):
        self.units_used += MORE
        self.order = [s for s in self.order if s[0] is self.ring]

    def take(self):
        i = self.free_order.pop(0)
        self.pe(*self.free_marks[i])
        return i, self.psum[:, i, :, :]

    def give(self, i, *marks):
        self.free_marks[i] = list(marks)
        self.free_order.append(i)


class Kernel:

    def __init__(self, nc, per_iteration, ins, consts, out):
        self.nc, self.ins, self.c, self.out = nc, ins, consts, out
        self.prog = Program(nc, per_iteration)
        p = self.prog
        self.PE, self.A, self.V, self.G = p.pe, p.act, p.dve, p.pool
        self.room, self.names, self.fillers = ExitStack(), {}, []

    def sb(self, name, shape, dt=F32):
        self.names[name] = self.names.get(name, 0) + 1
        name += f"_{self.names[name]}" if self.names[name] > 1 else ""
        return self.room.enter_context(self.nc.sbuf_tensor(name, shape, dt))

    def flat(self, t):
        return t[:, :, :].rearrange("p a b -> p (a b)")

    @contextmanager
    def scope(self):
        outer = self.room
        with ExitStack() as self.room:
            yield
            self.prog.meet()
        self.room = outer


    def rstd(self, ss, n, out, after):
        V, A = self.V, self.A
        V(after)
        m = V.done(V.eng.tensor_scalar(out, ss, 1.0 / n, EPS, ALU.mult, ALU.add))
        A(m)
        m = A.done(A.eng.activation(out, out, ACT.Sqrt))
        V(m)
        return V.done(V.eng.reciprocal(out, out))

    def normed_rows(self, x, xn, *after):
        V, A = self.V, self.A
        after = after or [None] * NT
        out = []
        for tt, m in enumerate(after):
            A(m)
            V(m)
            m = A.done(A.eng.activation(xn[:, tt, :], x[:, tt, :], ACT.Square,
                                        accum_out=self.ss[:, tt:tt + 1]))
            m = self.rstd(self.ss[:, tt:tt + 1], D, self.rs[:, tt:tt + 1], m)
            V(m)
            out.append(V.done(V.eng.tensor_scalar(xn[:, tt, :], x[:, tt, :], self.rs[:, tt:tt + 1], None, ALU.mult)))
        return out

    def turned(self, xn, xT, gain, *after):
        PE, A, V, p = self.PE, self.A, self.V, self.prog
        PE(*after, self.m_ident)
        marks = []
        for c in range(0, ND, 4):
            i, ps = p.take()
            for k in range(4):
                for tt in range(NT):
                    o = ps[:, k // 2, (k % 2) * T + tt * P:(k % 2) * T + tt * P + P]
                    last = PE.eng.transpose(o, xn[:, tt, (c + k) * P:(c + k + 1) * P], self.ident[:, :])
            m = PE.done(last)
            A(m)
            V(m)
            for k in range(4):
                o, s = xT[:, c + k, :], ps[:, k // 2, (k % 2) * T:(k % 2) * T + T]
                g = gain[:, c + k:c + k + 1]
                if k // 2:
                    a = A.done(A.eng.activation(o, s, ACT.Copy, scale=g))
                else:
                    v = V.done(V.eng.tensor_scalar(o, s, g, None, ALU.mult))
            p.give(i, a, v)
            marks = [a, v]
        return marks

    def fill(self, n=1):
        for _ in range(n):
            if self.fillers:
                self.fillers.pop(0)()

    def unit(self, src, rows, cols):
        u, m = self.prog.unit(src, rows, cols)
        self.PE(m)
        return u

    def project_T(self, src, xT, cols, evacuate):
        PE, p = self.PE, self.prog
        u = self.unit(src, ND, cols)
        n = cols // P
        i, ps = p.take()
        for c in range(n):
            o = ps[:, c // 2, (c % 2) * T:(c % 2) * T + T]
            for d in range(ND):
                last = PE.eng.matmul(o, u[:, d, c * P:(c + 1) * P], xT[:, d, :],
                                     start=d == 0, stop=d == ND - 1)
        m = PE.done(last, p.used)
        flat = ps.rearrange("p a (b t) -> p (a b) t", t=T)[:, 0:n, :]
        p.give(i, *evacuate(n, flat, m))

    def project(self, src, xT, cols, evacuate):
        PE, p = self.PE, self.prog
        u = self.unit(src, ND, cols)
        i, ps = p.take()
        for tt in range(NT):
            for d in range(ND):
                last = PE.eng.matmul(ps[:, tt, 0:cols], xT[:, d, tt * P:(tt + 1) * P], u[:, d, :],
                                     start=d == 0, stop=d == ND - 1)
        m = PE.done(last, p.used)
        p.give(i, *evacuate(ps[:, :, 0:cols], m))

    def copy_to(self, dst, engine=None, scale=None):
        at = [0]

        def evacuate(n, ps, m):
            o = dst[:, at[0]:at[0] + n, :]
            at[0] += n
            return [self.copy(o, ps, m, engine, scale)]
        return evacuate

    def copy(self, o, i, m, engine=None, scale=None):
        engine = engine or self.A
        engine(m)
        if engine is self.A:
            r = engine.done(engine.eng.activation(o, i, ACT.Copy, scale=1.0 if scale is None else scale))
        elif scale is None:
            r = engine.done(engine.eng.tensor_copy(o, i))
        else:
            r = engine.done(engine.eng.tensor_scalar(o, i, scale, None, ALU.mult))
        self.m_copy = r
        return r

    def accumulate(self, srcs, lhsT, x, ready):
        PE, V, p = self.PE, self.V, self.prog
        PE(*ready(0))
        i, pa = p.take()
        j, pb = p.take()
        pair = (pa, pb)
        for n, (src, at, rows) in enumerate(srcs):
            PE(*(ready(n) if n else ()))
            u = self.unit(src, rows, D)
            end = n == len(srcs) - 1
            steps = [(r, tt) for r in range(rows) for tt in range(NT)]
            if end:
                steps.sort(key=lambda s: s[1])
            for r, tt in steps:
                for h in range(2):
                    last = PE.eng.matmul(pair[tt][:, h, :], lhsT[:, at + r, tt * P:(tt + 1) * P],
                                         u[:, r, h * 512:(h + 1) * 512],
                                         start=n == 0 and r == 0, stop=end and r == rows - 1)
                if end and (r, tt) == (rows - 1, 0):
                    m0 = PE.done(last)
            m1 = PE.done(last, p.used)
        marks = []
        for tt, m in ((0, m0), (1, m1)):
            V(m)
            marks.append(V.done(V.eng.tensor_tensor(x[:, tt, :], x[:, tt, :],
                                                    pair[tt].rearrange("p a b -> p (a b)"), ALU.add)))
        p.give(i, marks[0])
        p.give(j, marks[1])
        return marks

    def row_panels(self, w, n, first=0):
        out, at = [], first
        while at < n:
            r = min(3, n - at)
            out.append((w[at * P:(at + r) * P, :], at, r))
            at += r
        return out


    def setup(self):
        p, c, ins, sb = self.prog, self.c, self.ins, self.sb
        PE, A, V, G = self.PE, self.A, self.V, self.G
        self.ident = sb("ident", [P, P])
        self.x = sb("x", [P, NT, D])
        self.xT = sb("xT", [P, ND, T])
        self.xn = sb("xn", [P, NT, D])
        self.ss = sb("ss", [P, 32])
        self.rs = sb("rs", [P, 32])
        m_x = p.dma(A, "x", [(self.x[:, :, :], ins["x"][0].rearrange("(a p) d -> p a d", p=P))])
        self.m_ident = p.dma(A, "ident", [(self.ident[:, :], c["ident"])])
        rows, at = [], 0
        self.col = {}
        for name in ("norm_mix", "norm_mlp", "hgrn_lb", "mix_norm_g_2", "ffn_norm_g_2", "mem_norm_g_2"):
            a = ins[name]
            n = math.prod(a.shape) // P
            flat = a.rearrange("a (b p) -> (a b) p", p=P) if len(a.shape) == 2 else a.rearrange("(b p) -> b p", p=P)
            rows.append((at, n, flat))
            self.col[name] = at
            at += n
        n_short = 3 * 3 * NM
        rowbuf = sb("rowbuf", [P, 2, P])
        self.par = sb("par", [P, 2, P])
        pairs = [(rowbuf[a:a + n, 0, :], f) for a, n, f in rows]
        pairs.append((rowbuf[0:n_short, 1, :], ins["hy_short_w_2"][0].rearrange("a (b p) -> (a b) p", p=P)))
        m = p.dma(p.sp, "rows", pairs)
        PE(m, self.m_ident)
        i, ps = p.take()
        PE.eng.transpose(ps[:, 0, 0:at], rowbuf[0:at, 0, :], self.ident[0:at, 0:at])
        m = PE.done(PE.eng.transpose(ps[:, 0, P:P + n_short], rowbuf[0:n_short, 1, :],
                                     self.ident[0:n_short, 0:n_short]))
        V(m)
        V.done(V.eng.tensor_copy(self.par[:, 0, 0:at], ps[:, 0, 0:at]))
        m_par = V.done(V.eng.tensor_copy(self.par[:, 1, 0:n_short], ps[:, 0, P:P + n_short]))
        p.give(i, m_par)
        self.m_par = m_par
        self.m_x = m_x

    def gains(self, name, l=0):
        at = self.col[name] + l * ND
        return self.par[:, 0, at:at + ND]


    def block1_memory(self):
        sb, p, c, A, G = self.sb, self.prog, self.c, self.A, self.G
        self.gate = sb("gate", [P, 4 * ND, T])
        self.mixT = sb("mixT", [P, ND, T])
        self.sqT = sb("sqT", [P, 3, T])
        self.skT = sb("skT", [P, 3, T])
        self.sv = sb("sv", [P, NT, 384])
        self.oT = sb("oT", [P, 3, T])
        self.dsa = sb("dsa", [P, NT, W_DSA])
        self.dT = sb("dT", [P, 9, T])
        self.rot = self.dT[:, 0:4, 0:NBLK * 8]
        self.score = sb("score", [P, NT, T])
        self.work = sb("work", [P, NT, T])
        self.top8 = sb("top8", [P, NT, 8])
        self.small = sb("small", [P, 64])
        self.big1 = self.xn[:, :, :].rearrange("p a (b t) -> p (a b) t", t=T)[:, 0:6, :]
        self.big2 = sb("big2", [P, 6, T])
        self.hqT = sb("hqT", [P, N_HG, T])
        self.hkT = sb("hkT", [P, N_HG, T])
        self.hbT = sb("hbT", [P, N_HG, T])
        self.hw = self.gate[:, 3 * ND:3 * ND + N_HG, :]
        self.hw2 = self.gate[:, 3 * ND + N_HG:4 * ND, :]
        self.hvg = sb("hvg", [P, NT, 512])
        self.att = sb("att", [P, N_HG, 384])
        self.ones = sb("ones", [P, T])
        self.negu = sb("negu", [P, P])
        self.negone = sb("negone", [P, P])
        self.strict = sb("strict", [P, P])
        self.lvl = sb("lvl", [P, len(MASKED), 32])
        self.rc = sb("rc", [P, NT, NBLK * 8])
        self.rsn = sb("rsn", [P, NT, NBLK * 8])
        self.m_c1 = p.dma(G, "consts1", [
            (self.negu[:, :], c["negu"]), (self.strict[:, :], c["strict"]),
            (self.lvl[:, :, :], c["levels"]), (self.rc[:, :, :], c["dsa_cos"]),
            (self.rsn[:, :, :], c["dsa_sin"])])
        V = self.V
        V.done(V.eng.memset(self.negone[:, :], -1.0))
        V.done(V.eng.memset(self.ones[:, :], 1.0))
        self.m_set1 = V.done(V.eng.memset(self.att[:, :, :], 0.0))
        self.gcur = sb("gcur", [P, 2 * ND])
        self.lb = sb("lb", [P, DEPTH, N_HG])
        self.lbc = sb("lbc", [P, 2, N_HG])
        self.qkg = sb("qkg", [P, 2, HD])
        self.og = sb("og", [P, 1])
        self.idle = sb("idle", [P, 1])
        self.idle_v = sb("idle_v", [P, 1])
        self.m_idle = G.done(G.eng.memset(self.idle[:, :], 0.0))
        at = self.col["hgrn_lb"]
        a = [self.par[:, 0, at + l * N_HG:at + (l + 1) * N_HG] for l in range(DEPTH)]
        s = self.small
        V(self.m_par)
        V.done(V.eng.tensor_tensor(s[:, 0:4], a[0], a[1], ALU.max))
        V(V.last)
        V.done(V.eng.tensor_tensor(s[:, 4:8], a[0], s[:, 0:4], ALU.subtract))
        m = V.done(V.eng.tensor_tensor(s[:, 8:12], a[1], s[:, 0:4], ALU.subtract))
        A(m)
        m = A.done(A.eng.activation(s[:, 4:12], s[:, 4:12], ACT.Exp))
        V(m)
        V.done(V.eng.tensor_tensor(s[:, 12:16], s[:, 4:8], s[:, 8:12], ALU.add))
        V(V.last)
        V.done(V.eng.reciprocal(s[:, 12:16], s[:, 12:16]))
        V(V.last)
        V.done(V.eng.tensor_tensor(s[:, 4:8], s[:, 4:8], s[:, 12:16], ALU.mult))
        V.done(V.eng.tensor_tensor(s[:, 8:12], s[:, 8:12], s[:, 12:16], ALU.mult))
        V(V.last)
        V.done(V.eng.tensor_tensor(s[:, 16:20], s[:, 4:8], s[:, 8:12], ALU.add))
        V.done(V.eng.tensor_tensor(self.lb[:, 0, :], s[:, 4:8], s[:, 4:8], ALU.subtract))
        V(V.last)
        V.done(V.eng.tensor_tensor(self.lb[:, 1, :], s[:, 16:20], s[:, 4:8], ALU.subtract))

    def layer_vectors(self, l):
        p, V, G, ins = self.prog, self.V, self.G, self.ins
        par, ds = self.par, bass.ds
        qk = [(self.qkg[:, k, :], ins[n][ds(l, 1), :].broadcast_to((P, HD)))
              for k, n in enumerate(("qn_dsa", "kn_dsa"))]
        og = [(self.og[h * HD:(h + 1) * HD, :], ins["hgrn_onorm"][ds(l, 1), :].rearrange("a d -> d a"))
              for h in range(2)]
        self.m_lv = p.dma(G, "layer_vectors", qk + og)
        V.done(V.eng.tensor_copy(self.gcur[:, 0:ND], par[:, 0, ds(self.col["norm_mix"] + l * ND, ND)]))
        V.done(V.eng.tensor_copy(self.gcur[:, ND:], par[:, 0, ds(self.col["norm_mlp"] + l * ND, ND)]))
        V.done(V.eng.tensor_copy(self.lbc[:, 0, :], self.lb[:, ds(l, 1), :].rearrange("p a b -> p (a b)")))
        V(V.last)
        self.m_cur = V.done(V.eng.tensor_scalar(self.lbc[:, 1, :], self.lbc[:, 0, :], -1.0, 1.0, ALU.mult, ALU.add))

    def held_back(self, t, *marks):
        G = self.G
        G(*marks, self.m_idle)
        self.m_idle = G.done(G.eng.tensor_tensor(t, t, t, ALU.add))


    def sb_scores(self, c):
        PE, A, V, p = self.PE, self.A, self.V, self.prog
        PE(self.m_sqk)
        i, ps = p.take()
        for h in range(2):
            r = slice(h * HD, (h + 1) * HD)
            PE.eng.matmul(ps[:, h, 0:T], self.skT[r, c, 0:P], self.sqT[r, c, :], start=True,
                          stop=False, skip_group_check=True)
            last = PE.eng.matmul(ps[:, h, T:T + P], self.skT[r, c, P:T], self.sqT[r, c, P:T],
                                 start=False, stop=False, skip_group_check=True)
        m = PE.done(last)
        z = ps[:, :, 0:384]
        e = self.big1[:, 3 * (c % 2):3 * (c % 2) + 3, :].rearrange("p a b -> p (a b)").rearrange("p (h n) -> p h n", h=2)
        A(m, self.sb_free[c % 2])
        for f, src, kw in ((ACT.Abs, z, {}), (ACT.Exp, e, {"scale": -1.0}), (ACT.Ln, e, {"bias": 1.0})):
            m = A.done(A.eng.activation(e, src, f, **kw))
            A(m)
        V(m, self.m_c1)
        V.done(V.eng.scalar_tensor_tensor(out=e, in0=z, scalar=0.0, in1=e, op0=ALU.max, op1=ALU.add))
        V(V.last)
        for h in range(2):
            d = e[:, h, :].rearrange("p (a b) -> p a b", a=3)[:, 0:3:2, :]
            m = V.done(V.eng.tensor_tensor(d, d, self.strict[:, :].unsqueeze(1).broadcast_to((P, 2, P)),
                                           ALU.mult))
        self.sb_state[c] = (i, ps, e, m)

    def sb_weights(self, c):
        PE, A, G = self.PE, self.A, self.G
        i, ps, e, m = self.sb_state[c]
        PE(m, self.m_set1)
        for h in range(2):
            PE.eng.matmul(ps[:, h, 0:384], self.negu[:, :], e[:, h, :], start=False, stop=False,
                          skip_group_check=True)
            last = PE.eng.matmul(ps[:, h, P:T], self.negone[:, :], e[:, h, T:384], start=False,
                                 stop=True, skip_group_check=True)
        m = PE.done(last)
        A(m)
        m = A.done(A.eng.activation(e, ps[:, :, 0:384], ACT.Exp))
        self.prog.give(i, m)
        self.held_back(self.idle[:, :], m)
        for h in range(2):
            d = e[:, h, :].rearrange("p (a b) -> p a b", a=3)[:, 0:3:2, :]
            m = G.done(G.eng.affine_select(out=d, in_=d, compare_op=ALU.is_gt, fill=0.0, base=0,
                                           pattern=[[0, 2], [1, P]], channel_multiplier=-1))
        self.sb_state[c] = (e, m)

    def sb_values(self, c, sb_oT):
        PE, p = self.PE, self.prog
        e, m = self.sb_state[c]
        PE(m, self.m_sv)
        i, ps = p.take()
        for h in range(2):
            o, f = slice(h * HD, (h + 1) * HD), slice((2 * c + h) * HD, (2 * c + h + 1) * HD)
            PE.eng.matmul(ps[o, h, 0:T], self.sv[:, 0, f], e[:, h, 0:T], start=True, stop=False,
                          skip_group_check=True)
            last = PE.eng.matmul(ps[o, h, P:T], self.sv[:, 1, f], e[:, h, T:384], start=False,
                                 stop=True, skip_group_check=True)
        m = PE.done(last)
        self.sb_free[c % 2] = m
        for h in range(2):
            o = slice(h * HD, (h + 1) * HD)
            m = self.copy(sb_oT[o, c, :], ps[o, h, 0:T], m, self.V)
        p.give(i, m)
        return m

    def branch(self, k, w, nrow, oT, after):
        PE, V, G, p = self.PE, self.V, self.G, self.prog
        for f in range(0, ND, 4):
            if f:
                yield
            if f == 0:
                PE(*after())
                u = self.unit(w, nrow, D)
            i, ps = p.take()
            for q in range(4):
                for r in range(nrow):
                    last = PE.eng.matmul(ps[:, q // 2, (q % 2) * T:(q % 2) * T + T],
                                         u[:, r, (f + q) * P:(f + q + 1) * P], oT[:, r, :],
                                         start=r == 0, stop=r == nrow - 1)
            m = PE.done(last, p.used if f + 4 == ND else None)
            V(m, self.m_gate)
            y = ps.rearrange("p a (b t) -> p (a b) t", t=T)
            g = self.gate[:, k * ND + f:k * ND + f + 4, :]
            if k == 0:
                m = V.done(V.eng.tensor_tensor(self.mixT[:, f:f + 4, :], y, g, ALU.mult))
            else:
                m = V.done(V.eng.tensor_tensor(g, y, g, ALU.mult))
                G(m, self.m_mix.get(f))
                m2 = self.m_mix[f] = G.done(G.eng.tensor_tensor(self.mixT[:, f:f + 4, :], self.mixT[:, f:f + 4, :], g, ALU.add))
            p.give(i, m)
        yield m if k == 0 else m2


    def dsa_rows(self):
        V, G = self.V, self.G
        d = self.dsa
        qk = d[:, :, 0:448].rearrange("p a (h e) -> p a h e", e=HD)
        sq = self.big2[:, 0:4, :].rearrange("p a b -> p (a b)")[:, 0:896]
        sq4 = sq.rearrange("p (a h e) -> p a h e", a=2, e=HD)
        V(self.m_dsa, self.m_lv)
        V.done(V.eng.tensor_tensor(sq4, qk, qk, ALU.mult))
        V(V.last)
        m = V.done(V.eng.tensor_reduce(self.small[:, 0:14], sq.rearrange("p (x e) -> p x e", e=HD), AX, ALU.add))
        m = self.rstd(self.small[:, 0:14], HD, self.small[:, 16:30], m)
        V(m)
        r = self.small[:, 16:30].rearrange("p (a h) -> p a h", a=2)
        for tt in range(NT):
            V.done(V.eng.tensor_tensor(qk[:, tt], qk[:, tt], r[:, tt].unsqueeze(2).broadcast_to((P, 7, HD)), ALU.mult))
        V(V.last)
        for tt in range(NT):
            V.done(V.eng.tensor_tensor(qk[:, tt, 0:6], qk[:, tt, 0:6],
                                       self.qkg[:, 0, :].unsqueeze(1).broadcast_to((P, 6, HD)), ALU.mult))
            V.done(V.eng.tensor_tensor(qk[:, tt, 6], qk[:, tt, 6], self.qkg[:, 1, :], ALU.mult))
        V.done(V.eng.tensor_scalar(d[:, :, 1088:1096], d[:, :, 1088:1096], IDX_SCALE, None, ALU.mult))
        V(V.last)
        blocks = d[:, :, 0:NBLK * HD].rearrange("p a (k e) -> p a k e", e=HD)
        n = NBLK * 8
        for tt in range(NT):
            x1, x2 = blocks[:, tt, :, 0:8], blocks[:, tt, :, 8:16]
            cs, sn = (t[:, tt, :].rearrange("p (k e) -> p k e", e=8) for t in (self.rc, self.rsn))
            t = [self.rot[:, k, 0:n].rearrange("p (k e) -> p k e", e=8) for k in range(4)]
            V.done(V.eng.tensor_tensor(t[0], x1, cs, ALU.mult))
            V.done(V.eng.tensor_tensor(t[1], x2, sn, ALU.mult))
            V.done(V.eng.tensor_tensor(t[2], x2, cs, ALU.mult))
            V.done(V.eng.tensor_tensor(t[3], x1, sn, ALU.mult))
            V(V.last)
            V.done(V.eng.tensor_tensor(x1, t[0], t[1], ALU.subtract))
            m = V.done(V.eng.tensor_tensor(x2, t[2], t[3], ALU.add))
            V(m)
        dup = sq[:, 0:512].rearrange("p (a k h e) -> p a k h e", a=2, k=2, h=2)
        for tt in range(NT):
            for k, at in ((0, 384), (1, 1024)):
                m = V.done(V.eng.tensor_copy(dup[:, tt, k], d[:, tt, at:at + HD].unsqueeze(1).broadcast_to((P, 2, HD))))
        self.dup = dup
        self.m_rows = m

    def dsa_turn(self):
        PE, p, d = self.PE, self.prog, self.dsa
        PE(self.m_rows)
        dup = self.dup

        def src(j, tt):
            if j < 3:
                return d[:, tt, j * P:(j + 1) * P]
            if j in (3, 8):
                return dup[:, tt, 0 if j == 3 else 1].rearrange("p h e -> p (h e)")
            return d[:, tt, 512 + (j - 4) * P:512 + (j - 3) * P]
        order = [4, 5, 6, 7, 8, 0, 1, 2, 3]
        for g in range(0, 9, 4):
            js = order[g:g + 4]
            i, ps = p.take()
            for q, j in enumerate(js):
                for tt in range(NT):
                    last = PE.eng.transpose(ps[:, q // 2, (q % 2) * T + tt * P:(q % 2) * T + tt * P + P],
                                            src(j, tt), self.ident[:, :])
            m = PE.done(last)
            flat = ps.rearrange("p a (b t) -> p (a b) t", t=T)
            done = []
            q = 0
            while q < len(js):
                n = 1
                while q + n < len(js) and js[q + n] == js[q] + n:
                    n += 1
                done.append(self.copy(self.dT[:, js[q]:js[q] + n, :], flat[:, q:q + n, :], m))
                q += n
            p.give(i, *done)
        self.m_dT = done[-1]

    def dsa_index(self, tt):
        PE, A, V, G, p = self.PE, self.A, self.V, self.G, self.prog
        n = (tt + 1) * P
        PE(self.m_dT)
        sc = self.score[:, tt, 0:n]
        hs = 4 if tt else 8
        first = True
        for h0 in range(0, N_IDX, hs):
            i, ps = p.take()
            for j in range(h0, h0 + hs):
                r = slice((j % 2) * HD, (j % 2 + 1) * HD)
                k = (j - h0) // 2
                last = PE.eng.matmul(ps[:, j % 2, k * n:(k + 1) * n],
                                     self.dT[r, 4 + j // 2, tt * P:(tt + 1) * P], self.dT[r, 8, 0:n],
                                     start=True, stop=True)
            m = PE.done(last)
            rel = self.big1[:, 0:4, :].rearrange("p a b -> p (a b)")
            A(m, self.m_rel)
            m = A.done(A.eng.activation(rel, ps.rearrange("p a b -> p (a b)"), ACT.Relu))
            p.give(i, m)
            V(m)
            for j in range(h0, h0 + hs):
                k = (j % 2) * (hs // 2) + (j - h0) // 2
                w = self.dsa[:, tt, 1088 + j:1089 + j]
                if first:
                    m = V.done(V.eng.tensor_scalar(sc, rel[:, k * n:(k + 1) * n], w, None, ALU.mult))
                else:
                    V(m)
                    m = V.done(V.eng.scalar_tensor_tensor(out=sc, in0=rel[:, k * n:(k + 1) * n], scalar=w, in1=sc,
                                                          op0=ALU.mult, op1=ALU.add))
                first = False
            self.m_rel = m
        self.held_back(self.idle[:, :], m)
        self.m_sc[tt] = G.done(G.eng.affine_select(out=sc, in_=sc, compare_op=ALU.is_ge, fill=NEG, base=tt * P,
                                                   pattern=[[-1, n]], channel_multiplier=1))

    def dsa_select(self):
        V = self.V
        step = self.topk_step
        V.eng.sem_clear(step)
        V(*self.m_sc)
        V.done(V.eng.tensor_copy(self.idle_v[:, :], self.score[:, 0, 0:1]))
        n_step = 0
        for r in range(K_TOP // 8):
            src = self.score if r == 0 else self.work
            for tt in range(NT):
                if r:
                    V.eng.wait_ge(step, n_step - 1)
                V.eng.max(out=self.top8[:, tt, :], in_=src[:, tt, 0:(tt + 1) * P]).then_inc(step, 1)
                n_step += 1
            for tt in range(NT):
                n = (tt + 1) * P
                V.eng.wait_ge(step, n_step - 1)
                V.eng.match_replace(out=self.work[:, tt, 0:n], in_to_replace=self.top8[:, tt, :],
                                    in_values=src[:, tt, 0:n], imm_value=TINY).then_inc(step, 1)
                n_step += 1
        V.eng.wait_ge(step, n_step)
        for tt in range(NT):
            n = (tt + 1) * P
            w, s = self.work[:, tt, 0:n], self.score[:, tt, 0:n]
            V.done(V.eng.tensor_scalar(w, w, 2 * NEG, None, ALU.is_lt))
            V(V.last)
            V.done(V.eng.scalar_tensor_tensor(out=w, in0=s, scalar=0.5 * NEG, in1=w, op0=ALU.is_gt, op1=ALU.mult))
            V(V.last)
            m = V.done(V.eng.tensor_scalar(w, w, -NEG, NEG, ALU.mult, ALU.add))
        self.m_bias = m

    def dsa_attend(self, tt):
        PE, A, V, p = self.PE, self.A, self.V, self.prog
        n = (tt + 1) * P
        bias = self.work[:, tt, 0:n]
        lg = self.big1[:, :, 0:n] if tt else self.big1[:, 0:3, :].rearrange("p a (b n) -> p (a b) n", n=P)
        slots = [0, 2, 1, 3, 4, 5] if tt else [0, 2, 4, 1, 3, 5]
        PE(self.m_dT)
        V(self.m_bias, self.m_lg)
        for group in ([[0, 2, 1, 3], [4, 5]] if tt else [[0, 2, 4, 1, 3, 5]]):
            i, ps = p.take()
            k = len(group) // 2
            for q, h in enumerate(group):
                r = slice((h % 2) * HD, (h % 2 + 1) * HD)
                last = PE.eng.matmul(ps[:, h % 2, (q % k) * n:(q % k + 1) * n],
                                     self.dT[r, h // 2, tt * P:(tt + 1) * P], self.dT[r, 3, 0:n], start=True, stop=True)
            m = PE.done(last)
            V(m)
            for b in range(2):
                s0 = slots.index(group[b * k])
                m = V.done(V.eng.scalar_tensor_tensor(
                    out=lg[:, s0:s0 + k, :], in0=ps[:, b, 0:k * n].rearrange("p (a n) -> p a n", n=n),
                    scalar=HD ** -0.5, in1=bias.unsqueeze(1).broadcast_to((P, k, n)), op0=ALU.mult, op1=ALU.add))
            p.give(i, m)
        V(V.last)
        s = self.small
        V.done(V.eng.tensor_reduce(s[:, 32:38], lg, AX, ALU.max))
        V(V.last)
        m = V.done(V.eng.tensor_scalar(s[:, 32:38], s[:, 32:38], -1.0, None, ALU.mult))
        A(m)
        for h in range(6):
            m = A.done(A.eng.activation(lg[:, h, :], lg[:, h, :], ACT.Exp, bias=s[:, 32 + h:33 + h],
                                        accum_out=s[:, 40 + h:41 + h]))
        V(m)
        V.done(V.eng.reciprocal(s[:, 40:46], s[:, 40:46]))
        V(V.last)
        m = V.done(V.eng.tensor_tensor(lg, lg, s[:, 40:46].unsqueeze(2).broadcast_to((P, 6, n)), ALU.mult))
        self.fill()
        PE(m)
        for kt in range(tt + 1):
            i, ps = p.take()
            for h in range(6):
                last = PE.eng.transpose(ps[:, h % 2, (h // 2) * P:(h // 2 + 1) * P],
                                        lg[:, slots.index(h), kt * P:(kt + 1) * P], self.ident[:, :])
            m = PE.done(last)
            A(self.m_pt)
            m = self.copy(self.ptv(kt), ps[:, :, 0:384], m)
            p.give(i, m)
        self.m_lg = m
        PE(m)
        i, ps = p.take()
        for b in range(2):
            for kt in range(tt + 1):
                last = PE.eng.matmul(ps[b * HD:(b + 1) * HD, b, 0:384], self.dsa[:, kt, 448:512], self.ptv(kt)[:, b, :],
                                     start=kt == 0, stop=kt == tt)
        m = PE.done(last)
        self.m_pt = m
        for b in range(2):
            m = self.copy(self.dsa_oT[b * HD:(b + 1) * HD, :, tt * P:(tt + 1) * P],
                          ps[b * HD:(b + 1) * HD, b, 0:384].rearrange("p (a n) -> p a n", n=P), m, self.V)
        p.give(i, m)
        return m

    def ptv(self, kt):
        return self.big2[:, 3 * kt:3 * kt + 3, :].rearrange("p a b -> p (a b)").rearrange("p (h n) -> p h n", h=2)


    def hg_gates(self):
        A, V = self.A, self.V
        q, k, b = self.hqT, self.hkT, self.hbT
        V(self.m_hf)
        for h in range(N_HG):
            m = V.done(V.eng.tensor_scalar(b[:, h, :], k[:, h, :], self.lbc[:, 1, h:h + 1], self.lbc[:, 0, h:h + 1],
                                           ALU.mult, ALU.add))
        V(m)
        V.done(V.eng.tensor_scalar(k[:, :, :], b[:, :, :], -1.0, 1.0, ALU.mult, ALU.add))
        m = V.done(V.eng.tensor_scalar(self.hw[:, :, :], b[:, :, :], F_MIN, None, ALU.max))
        A(m)
        m = A.done(A.eng.activation(self.hw[:, :, :], self.hw[:, :, :], ACT.Ln))
        V(m, self.m_set1)
        for h in range(N_HG):
            m = V.done(V.eng.tensor_tensor_scan(b[:, h, :], self.ones[:, :], self.hw[:, h, :], 0.0, ALU.mult, ALU.add))
        self.m_b = m

    def hg_level(self, m_, w, free):
        A, V = self.A, self.V

        def halves(t):
            v = t[:, :, :].rearrange("p h t -> p (h t)").rearrange("p (n a m) -> p n a m", a=2, m=m_)
            return v[:, :, 0, :], v[:, :, 1, :]
        b1, b2 = halves(self.hbT)
        e1, e2 = halves(w)
        n = N_HG * T // (2 * m_)
        ref = b1[:, :, m_ - 1:m_].broadcast_to((P, n, m_))
        V(self.m_b, free)
        V.done(V.eng.tensor_tensor(e2, b2, ref, ALU.subtract))
        m = V.done(V.eng.tensor_tensor(e1, ref, b1, ALU.subtract))
        A(m)
        m = A.done(A.eng.activation(w[:, :, :], w[:, :, :], ACT.Exp))
        V(m)
        V.done(V.eng.tensor_tensor(e2, e2, halves(self.hqT)[1], ALU.mult))
        return V.done(V.eng.tensor_tensor(e1, e1, halves(self.hkT)[0], ALU.mult))

    def hg_big(self):
        PE, V, p = self.PE, self.V, self.prog
        for m_ in HG_LEVELS[:3]:
            w = (self.hw, self.hw2)[m_ == 64]
            m = self.hg_level(m_, w, self.hw_free[m_ == 64])
            self.fill()
            PE(m)
            i, ps = p.take()
            outs = []
            for s0 in range(0, T, 2 * m_):
                st, r = s0 // P, s0 % P
                t0 = s0 + m_
                col = t0 if st == 0 else T + t0 - P
                for h in range(N_HG):
                    last = PE.eng.matmul(ps[r:r + m_, st, h * P:h * P + m_], w[:, h, s0:s0 + m_], w[:, h, t0:t0 + m_],
                                         start=True, stop=True)
                outs.append((st, r, col))
            m = PE.done(last)
            self.hw_free[m_ == 64] = m
            V(m)
            for st, r, col in outs:
                m = V.done(V.eng.tensor_copy(self.att[r:r + m_, :, col:col + m_],
                                             ps[r:r + m_, st, :].rearrange("p (h n) -> p h n", n=P)[:, :, 0:m_]))
            p.give(i, m)

    def hg_small(self):
        PE, V, p = self.PE, self.V, self.prog
        part = self.gatebuf
        for g in range(0, len(MASKED), 3):
            i, ps = p.take()
            j = None
            for q, m_ in enumerate(MASKED[g:g + 3]):
                if m_:
                    k = q % 2
                    w = (self.hw, self.hw2)[k]
                    m = self.hg_level(m_, w, self.hw_free[k])
                    self.fill()
                    PE(m)
                    lw = rw = w
                else:
                    lw, rw = self.hkT, self.hqT
                    PE(self.m_b, self.m_hq)
                if q == 2:
                    j, ps2 = p.take()
                bank = ps[:, q, :] if q < 2 else ps2[:, 0, :]
                for h in range(N_HG):
                    for blk in range(T // 32):
                        r = 32 * (blk % 4)
                        col = h * 64 + (blk // 4) * 32
                        t = slice(blk * 32, blk * 32 + 32)
                        last = PE.eng.matmul(bank[r:r + 32, col:col + 32], lw[:, h, t], rw[:, h, t], start=True, stop=True)
                m = PE.done(last)
                if m_:
                    self.hw_free[k] = m
                V(m)
                lv = g + q
                m = V.done(V.eng.tensor_tensor(
                    part[:, lv, 0:256].rearrange("p (x t) -> p x t", t=32),
                    bank[:, 0:256].rearrange("p (x t) -> p x t", t=32),
                    self.lvl[:, lv, :].unsqueeze(1).broadcast_to((P, 8, 32)), ALU.mult))
            p.give(i, m)
            p.give(j, m)
        V(V.last)
        for lv in range(1, len(MASKED)):
            V.done(V.eng.tensor_tensor(part[:, 0, 0:256], part[:, 0, 0:256], part[:, lv, 0:256], ALU.add))
            V(V.last)
        for r in range(4):
            q = slice(32 * r, 32 * r + 32)
            for st in range(2):
                col = 32 * r + (T if st else 0)
                m = V.done(V.eng.tensor_copy(self.att[q, :, col:col + 32],
                                             part[q, 0, 0:256].rearrange("p (h a t) -> p h a t", a=2, t=32)[:, :, st, :]))
        self.m_att = m

    def hg_out(self):
        PE, A, V, p = self.PE, self.A, self.V, self.prog
        self.fill()
        PE(self.m_att, self.m_hvg)
        i, ps = p.take()
        for tt in range(NT):
            for h in range(N_HG):
                for kt in range(tt + 1):
                    col = tt * P if kt == 0 else T
                    last = PE.eng.matmul(ps[:, tt, h * HD:(h + 1) * HD], self.att[:, h, col:col + P],
                                         self.hvg[:, kt, h * HD:(h + 1) * HD], start=kt == 0, stop=kt == tt)
        m = PE.done(last)
        o, sq = self.hw[:, 0:2, :], self.hw2[:, 0:2, :]
        A(m, self.hw_free[0], self.hw_free[1])
        m2 = A.done(A.eng.activation(o, ps[:, :, 0:256], ACT.Copy))
        m = A.done(A.eng.activation(sq, ps[:, :, 0:256], ACT.Square))
        p.give(i, m)
        V(m)
        s = self.small
        m = V.done(V.eng.tensor_reduce(s[:, 48:56], sq.rearrange("p a (h e) -> p (a h) e", e=HD), AX, ALU.add))
        m = self.rstd(s[:, 48:56], HD, s[:, 56:64], m)
        V(m)
        o3 = o.rearrange("p a (h e) -> p (a h) e", e=HD)
        V.done(V.eng.tensor_tensor(o3, o3, s[:, 56:64].unsqueeze(2).broadcast_to((P, 8, HD)), ALU.mult))
        V(V.last)
        m = V.done(V.eng.tensor_tensor(o, o, self.hvg[:, :, 256:512], ALU.mult))
        self.fill()
        PE(m)
        i, ps = p.take()
        for c in range(2):
            for tt in range(NT):
                last = PE.eng.transpose(ps[:, 0, c * T + tt * P:c * T + tt * P + P], o[:, tt, c * P:(c + 1) * P], self.ident[:, :])
        m = PE.done(last)
        m = self.copy(self.hg_oT[:, :, :].rearrange("p a b -> p (a b)"), ps[:, 0, :], m, self.A, scale=self.og[:, 0:1])
        p.give(i, m)
        return m

    def mlp(self, l, ds):
        A, V, G, p, ins = self.A, self.V, self.G, self.prog, self.ins
        xn = self.normed_rows(self.x, self.xn, *self.m_xs)
        ready = self.turned(self.xn, self.xT, self.gcur[:, ND:], *xn)
        self.PE(*ready)
        hid, at = self.gate, [0]
        self.hid_marks = []

        def evacuate(n, ps, m):
            o = hid[:, at[0]:at[0] + n, :]
            at[0] += n
            A(m)
            m = A.done(A.eng.activation(o, ps, ACT.Relu))
            V(m)
            self.hid_marks.append(V.done(V.eng.tensor_tensor(o, o, o, ALU.mult)))
            return [m]
        w = ins["w_up"][ds(l, 1), :, :].rearrange("a d n -> (a d) n")
        for c in range(0, D_FF, 384):
            n = min(384, D_FF - c)
            self.project_T(w[:, c:c + n], self.xT, n, evacuate)
        w = ins["w_down"][ds(l, 1), :, :].rearrange("a d n -> (a d) n")
        self.m_xs = self.accumulate(self.row_panels(w, D_FF // P), hid, self.x,
                                    lambda n: [self.hid_marks[n]])

    def block1(self):
        p, ins, A, V, PE = self.prog, self.ins, self.A, self.V, self.PE
        self.block1_memory()
        self.gatebuf = self.big2[:, :, :]
        self.hg_oT = self.skT[:, 0:2, :]
        self.dsa_oT = self.sqT[:, :, :]
        A(self.m_x)
        V(self.m_x)
        p.sp(self.m_x)
        ds = bass.ds
        self.topk_step = p.nc.alloc_semaphore("topk_step")
        with p.loop_of("layers", DEPTH) as l:
            self.sb_state, self.sb_free = {}, [None, None]
            self.hw_free = [None, None]
            self.m_sc = [None] * NT
            self.m_rel = self.m_lg = self.m_pt = None
            self.m_mix = {}
            self.layer_vectors(l)
            xn = self.normed_rows(self.x, self.xn)
            V(self.m_cur)
            A(self.m_cur)
            ready = self.turned(self.xn, self.xT, self.gcur[:, 0:ND], *xn)
            PE(*ready)
            w = ins["w_in"][ds(l, 1), :, :].rearrange("a d n -> (a d) n")
            xT = self.xT
            self.project_T(w[:, C_SQ:C_SQ + 384], xT, 384, self.copy_to(self.sqT, scale=HD ** -0.5))
            self.project_T(w[:, C_SK:C_SK + 384], xT, 384, self.copy_to(self.skT))
            self.m_sqk = self.m_copy

            def evac(dst):
                def f(ps, m):
                    self.m_ev = self.copy(dst, ps, m)
                    return [self.m_ev]
                return f
            self.project(w[:, C_SV:C_SV + 384], xT, 384, evac(self.sv[:, :, :]))
            self.m_sv = self.m_ev
            self.sb_scores(0)
            for c in range(0, W_DSA, 384):
                n = min(384, W_DSA - c)
                self.project(w[:, C_DSA + c:C_DSA + c + n], xT, n, evac(self.dsa[:, :, c:c + n]))
                if c == 0:
                    self.sb_weights(0)
                    self.sb_scores(1)
                elif c == 384:
                    self.sb_values(0, self.oT)
                    self.sb_weights(1)
            self.m_dsa = self.m_ev
            self.sb_scores(2)
            self.sb_values(1, self.oT)
            self.dsa_rows()
            at = [0]

            def hqf(n, ps, m):
                A(m)
                out = []
                js = range(at[0], at[0] + n)
                at[0] += n
                for k, j in enumerate(js):
                    dst = (self.hqT if j < N_HG else self.hkT)[:, j % N_HG, :]
                    self.m_hf = A.done(A.eng.activation(dst, ps[:, k, :], ACT.Sigmoid))
                for k, j in enumerate(js):
                    if j < N_HG:
                        V(self.m_hf)
                        dst = self.hqT[:, j, :]
                        self.m_hq = V.done(V.eng.tensor_tensor(dst, ps[:, k, :], dst, ALU.mult))
                        out = [self.m_hq]
                return out + [self.m_hf]
            for k, (c, n) in enumerate(((0, 384), (384, 384), (768, 256))):
                self.project_T(w[:, C_HQ + c:C_HQ + c + n], xT, n, hqf)
                if k == 0:
                    self.sb_weights(2)
                if k == 1:
                    self.m_oT = self.sb_values(2, self.oT)
            self.dsa_turn()
            self.dsa_index(0)
            self.hg_gates()

            def silu_hg(ps, m):
                A(m)
                V(m)
                a = A.done(A.eng.activation(self.hvg[:, :, 256:512], ps, ACT.Sigmoid))
                V(a)
                self.m_hvg = V.done(V.eng.tensor_tensor(self.hvg[:, :, 256:512], ps, self.hvg[:, :, 256:512], ALU.mult))
                return [self.m_hvg]
            gate_at = [0]

            def gates(n, ps, m):
                A(m)
                o = self.gate[:, gate_at[0]:gate_at[0] + n, :]
                gate_at[0] += n
                self.m_gate = A.done(A.eng.activation(o, ps, ACT.Sigmoid))
                return [self.m_gate]

            def gate_unit(k):
                c, n = ((0, 384), (384, 384), (768, 256))[k % 3]
                c += C_GATE + (k // 3) * D
                self.project_T(w[:, c:c + n], xT, n, gates)
            br = {n: ins[n][ds(l, 1), :, :].rearrange("a d n -> (a d) n") for n in ("w_br_sb", "w_br_dsa", "w_br_hgrn", "w_out")}
            b_sb = self.branch(0, br["w_br_sb"], 3, self.oT, lambda: [self.m_oT])
            b_dsa = self.branch(1, br["w_br_dsa"], 3, self.dsa_oT, lambda: [self.m_dsa_oT])
            self.fillers = [lambda k=k: gate_unit(k) for k in range(9)]
            self.fillers[4:4] = [
                lambda: self.project(w[:, C_HI:C_HI + 256], xT, 256, evac(self.hvg[:, :, 0:256])),
                lambda: self.project(w[:, C_HI + 256:C_HI + 512], xT, 256, silu_hg)]
            self.fillers += [lambda: next(b_sb), lambda: next(b_sb), lambda: next(b_dsa), lambda: next(b_dsa)]
            self.fill()
            self.dsa_index(1)
            self.dsa_select()
            self.fill(3)
            self.dsa_attend(0)
            self.m_dsa_oT = self.dsa_attend(1)
            self.hg_big()
            self.hg_small()
            m_hg = self.hg_out()
            self.fill(len(self.fillers))
            b_hg = self.branch(2, br["w_br_hgrn"], 2, self.hg_oT, lambda: [m_hg])
            next(b_hg)
            m = next(b_hg)
            self.m_xs = self.accumulate(self.row_panels(br["w_out"], ND), self.mixT, self.x, lambda n: [m])
            self.mlp(l, ds)



    def block2_memory(self):
        sb, p, ins, c = self.sb, self.prog, self.ins, self.c
        G, V, PE = self.G, self.V, self.PE
        self.mkT = sb("mkT", [P, DEPTH, 2, T])
        self.mv = sb("mv", [P, DEPTH, NT, N_MEM * HD])
        self.router = sb("router", [P, DEPTH, ND, N_EXP])
        self.iota = sb("iota", [P, CAP])
        self.mainT = sb("mainT", [P, ND, T])
        self.cqT = sb("cqT", [P, 2, T])
        self.prob = self.flat(self.xn).rearrange("p (k h t) -> p k h t", k=2, h=4)
        self.probT = self.flat(self.xT).rearrange("p (k a h q) -> p k a h q", k=2, a=NT, h=4)
        self.st = sb("st", [P, 64])
        pairs = [(self.router[:, i], ins["router_w_2"][i].rearrange("(c p) e -> p c e", p=P)) for i in range(DEPTH)]
        self.m_c2 = p.dma(G, "consts2", pairs + [(self.iota[:, :], c["iota"])])
        self.att_free = [None, None]

    def memory_units(self):
        units = []
        for i in range(DEPTH):
            w = self.ins["w_mem_kv_2"][i]
            units.append(lambda w=w, i=i: self.project_T(w[:, 0:256], self.xT, 256, self.copy_to(self.mkT[:, i])))
            units.append(lambda w=w, i=i: self.project(w[:, 256:512], self.xT, 256,
                                                       lambda ps, m: [self.copy(self.mv[:, i], ps, m)]))
        return units

    def attend_steps(self, jobs):
        PE, A, V, p, scale = self.PE, self.A, self.V, self.prog, HD ** -0.5
        out, last_job = [], None
        for n, job in enumerate(jobs + [None]):
            k, was = n % 2, (n - 1) % 2
            if job:
                tt, qT, kT, v, oT = job
                i, ps = p.take()
                for h in range(4):
                    last = PE.eng.matmul(ps[:, h % 2, (h // 2) * T:(h // 2 + 1) * T], qT(h)[:, tt * P:(tt + 1) * P],
                                         kT(h), start=True, stop=True)
                m = PE.done(last)
                pr, s = self.prob[:, k], self.st
                mx, sm = s[:, 8 * k:8 * k + 4], s[:, 16 + 8 * k:20 + 8 * k]
                V(m, self.att_free[k])
                V.done(V.eng.tensor_reduce(mx, ps.rearrange("p a (b n) -> p (a b) n", n=T), AX, ALU.max))
                V(V.last)
                m_max = V.done(V.eng.tensor_scalar(mx, mx, -scale, None, ALU.mult))
            if last_job:
                tt1, v1, oT1, m = last_job
                pr1, pt = self.prob[:, was], self.probT[:, was]
                PE(m)
                j, pt_ps = p.take()
                for kt in range(NT):
                    for q in range(4):
                        last = PE.eng.transpose(pt_ps[:, kt, q * P:(q + 1) * P], pr1[:, q, kt * P:(kt + 1) * P],
                                                self.ident[:, :])
                m = self.att_free[was] = PE.done(last)
                ma = self.copy(pt[:, 0].rearrange("p h q -> p (h q)"), pt_ps[:, 0, :], m, A)
                mv = self.copy(pt[:, 1].rearrange("p h q -> p (h q)"), pt_ps[:, 1, :], m, V)
                p.give(j, ma, mv)
            if job:
                A(m_max, self.att_free[k])
                for q in range(4):
                    m = A.done(A.eng.activation(pr[:, q, :], ps[:, q // 2, (q % 2) * T:(q % 2 + 1) * T], ACT.Exp,
                                                scale=scale, bias=mx[:, q:q + 1], accum_out=sm[:, q:q + 1]))
                p.give(i, m)
                V(m)
                V.done(V.eng.reciprocal(sm, sm))
                V(V.last)
                m_prob = V.done(V.eng.tensor_tensor(pr, pr, sm.unsqueeze(2).broadcast_to((P, 4, T)), ALU.mult))
            if last_job:
                PE(ma, mv)
                j, o_ps = p.take()
                for h in range(4):
                    o = slice((h % 2) * HD, (h % 2 + 1) * HD)
                    q = (h % 2) * 2 + h // 2
                    for kt in range(NT):
                        last = PE.eng.matmul(o_ps[o, h % 2, (h // 2) * P:(h // 2 + 1) * P], v1(kt, h), pt[:, kt, q, :],
                                             start=kt == 0, stop=kt == NT - 1)
                m = PE.done(last)
                out = []
                for b, e in ((0, A), (1, V)):
                    o = slice(b * HD, (b + 1) * HD)
                    out.append(self.copy(oT1[o, :, tt1 * P:(tt1 + 1) * P],
                                         o_ps[o, b, 0:2 * P].rearrange("p (a n) -> p a n", n=P), m, e))
                p.give(j, *out)
            last_job = (tt, v, oT, m_prob) if job else None
            yield out

    def attend(self, jobs):
        for out in self.attend_steps(jobs):
            pass
        return out

    def half(self, h):
        return slice((h % 2) * HD, (h % 2 + 1) * HD)

    def cross_jobs(self, i):
        return [(tt, lambda h: self.cqT[self.half(h), h // 2, :],
                 lambda h: self.mkT[self.half(h), i, h // 2, :],
                 lambda kt, h: self.mv[:, i, kt, h * HD:(h + 1) * HD], self.mainT[:, NM:NM + 2, :])
                for tt in range(NT)]

    def sine(self, ps, bias, freq, h, tmp, m):
        A, V = self.A, self.V
        big = 1.5 * 2.0 ** 23
        hi = 6.28125
        V(m)
        V.done(V.eng.tensor_scalar(h, ps, bias, freq, ALU.add, ALU.mult))
        V(V.last)
        V.done(V.eng.tensor_scalar(tmp, h, 1 / (2 * math.pi), big, ALU.mult, ALU.add))
        V(V.last)
        V.done(V.eng.tensor_scalar(tmp, tmp, big, None, ALU.subtract))
        for part in (hi, 2 * math.pi - hi):
            V(V.last)
            V.done(V.eng.scalar_tensor_tensor(out=h, in0=tmp, scalar=-part, in1=h, op0=ALU.mult, op1=ALU.add))
        V(V.last)
        lim = 3.1415925
        m = V.done(V.eng.tensor_scalar(h, h, lim, -lim, ALU.min, ALU.max))
        A(m)
        return A.done(A.eng.activation(h, h, ACT.Sin))

    def hyena_filters(self):
        p, ins, c, sb = self.prog, self.ins, self.c, self.sb
        PE, A, V, G = self.PE, self.A, self.V, self.G
        with self.scope():
            featsT = sb("featsT", [N_FEAT, T])
            w1 = sb("w1", [N_FEAT, FILT])
            w2 = sb("w2", [FILT, FILT])
            w3 = sb("w3", [FILT, 4 * D_MAIN])
            vec = sb("vec", [FILT, 3])
            decay = sb("decay", [P, NT, D_MAIN])
            hs = sb("hs", [P, NT, NC2])
            hd = sb("hd", [P, NT, NC2])
            h1, h2 = self.cqT[0:FILT, 0, :], self.cqT[0:FILT, 1, :]
            tmp = self.mainT[0:FILT, 6, :]
            ones = self.mainT[:, 7, 0:P]
            mem = sb("mem", [P, NT, D])
            n = NT * 2 * 384
            taps, mag = (self.flat(t)[:, 0:n].rearrange("p (a d n) -> p a d n", a=NT, d=2) for t in (self.xn, mem))
            rn = self.flat(self.mainT)[:, 0:384]
            skip = self.spec_i0[0:1, :]
            m_mem = p.dma(p.sp, "mem", [(mem[:, :, :], ins["mem_2"][0].rearrange("(a p) d -> p a d", p=P))], G.last)
            m = p.dma(p.sp, "filt", [
                (featsT[:, :], c["featsT"]), (w1[:, :], ins["hy_filt_w1_2"][0]), (w2[:, :], ins["hy_filt_w2_2"][0]),
                (w3[:, :], ins["hy_filt_w3_2"][0]), (decay[:, :, :], c["decay"]),
                (skip, ins["hy_skip_2"].rearrange("a o c -> a (o c)"))]
                + [(vec[:, k:k + 1], ins[n].rearrange("a f -> f a")) for k, n in
                   enumerate(("hy_filt_b1_2", "hy_filt_b2_2", "hy_filt_freq_2"))])
            m_ones = V.done(V.eng.memset(ones, 1.0))
            A(m_mem)
            V(m_mem)
            xn = self.normed_rows(mem, self.xn)
            A(*xn)
            PE(*self.turned(self.xn, self.xT, self.gains("mem_norm_g_2"), *xn))
            self.fillers = self.memory_units()
            PE(m)
            V(m)
            for w, src, b, dst in ((w1, featsT[:, :], 0, h1), (w2, h1, 1, h2)):
                i, ps = p.take()
                m = PE.done(PE.eng.matmul(ps[0:FILT, 0, 0:T], w[:, :], src, start=True, stop=True))
                m = self.sine(ps[0:FILT, 0, 0:T], vec[:, b:b + 1], vec[:, 2:3], dst, tmp, m)
                p.give(i, m)
                PE(m)
            PE(m_ones, self.m_dft)
            m_mag = m_taps = None
            m_filt = []
            for o in range(ORD):
                for q in range(2):
                    blk = slice(o * D_MAIN + q * 384, o * D_MAIN + (q + 1) * 384)
                    for tt in range(NT):
                        i, ps = p.take()
                        for d in range(2):
                            at = (2 * o + d) * D_MAIN + q * 384
                            last = PE.eng.matmul(ps[:, d, 0:384], h2[:, tt * P:(tt + 1) * P], w3[:, at:at + 384],
                                                 start=True, stop=True)
                        m = PE.done(last)
                        V(m, m_taps)
                        m = V.done(V.eng.tensor_tensor(taps[:, tt], ps[:, :, 0:384],
                                                       decay[:, tt, q * 384:(q + 1) * 384].unsqueeze(1)
                                                       .broadcast_to((P, 2, 384)), ALU.mult))
                        p.give(i, m)
                        A(m, m_mag)
                        m = A.done(A.eng.activation(mag[:, tt], taps[:, tt], ACT.Abs))
                    self.fill()
                    PE(m)
                    i, ps = p.take()
                    for n in range(4):
                        last = PE.eng.matmul(ps[:, 0, 0:384], ones, mag[:, n // 2, n % 2, :], start=n == 0, stop=n == 3)
                    m = m_mag = PE.done(last)
                    V(m)
                    m = V.done(V.eng.tensor_scalar(rn, ps[:, 0, 0:384], 1e-6, None, ALU.add))
                    p.give(i, m)
                    V(m)
                    V.done(V.eng.reciprocal(rn, rn))
                    V.done(V.eng.tensor_tensor(hs[:, :, blk], taps[:, :, 0, :], taps[:, :, 1, :], ALU.add))
                    m_taps = V.done(V.eng.tensor_tensor(hd[:, :, blk], taps[:, :, 0, :], taps[:, :, 1, :], ALU.subtract))
                    V(m_taps)
                    r = rn.unsqueeze(1).broadcast_to((P, NT, 384))
                    V.done(V.eng.tensor_tensor(hs[:, :, blk], hs[:, :, blk], r, ALU.mult))
                    m = V.done(V.eng.tensor_tensor(hd[:, :, blk], hd[:, :, blk], r, ALU.mult))
                V(m)
                row = slice(o * D_MAIN, (o + 1) * D_MAIN)
                m_filt.append(V.done(V.eng.tensor_tensor(hs[0:1, 0, row], hs[0:1, 0, row], skip[:, row], ALU.add)))
            for q in range(0, 4, 2):
                PE(m_filt[q // 2])
                for fc in range(4):
                    src = hs if fc < 2 else hd
                    i, ps = p.take()
                    for b in range(2):
                        for tt in range(NT):
                            last = PE.eng.matmul(ps[:, b, 0:384], self.dft[:, tt, fc * P:(fc + 1) * P],
                                                 src[:, tt, (q + b) * 384:(q + b + 1) * 384], start=tt == 0, stop=tt == 1)
                    m = PE.done(last)
                    o = self.spec[:, fc, q * 384:(q + 2) * 384].rearrange("p (b n) -> p b n", b=2)
                    m = self.copy(o, ps[:, :, 0:384], m, A)
                    p.give(i, m)
                if q == 0:
                    A(m_taps)
                    self.m_xn = self.normed_rows(self.x, self.xn, *self.m_xs)
            V(*[e.last for e in (A, V)])
            V.done(V.eng.tensor_copy(self.spec_i0[:, :], self.spec[:, 0, :]))
            V.done(V.eng.memset(self.spec[0:1, 2, :], 0.0))
            for q in range(0, 4, 2):
                i, ps = p.take()
                for b in range(2):
                    for tt in range(NT):
                        last = PE.eng.matmul(ps[0:1, b, 0:384], self.dft[:, tt, T:T + 1],
                                             hs[:, tt, (q + b) * 384:(q + b + 1) * 384], start=tt == 0, stop=tt == 1)
                m = PE.done(last)
                V(m, V.last)
                m = V.done(V.eng.tensor_copy(self.spec_i0[0:1, q * 384:(q + 2) * 384].rearrange("p (b n) -> p b n", b=2),
                                             ps[0:1, :, 0:384]))
                p.give(i, m)

    def spectrum(self, z, zf, m):
        PE, A, V, p = self.PE, self.A, self.V, self.prog
        PE(*m)
        marks = []
        for fc in range(4):
            i, ps = p.take()
            for b in range(2):
                for tt in range(NT):
                    last = PE.eng.matmul(ps[:, b, 0:384], self.dft[:, tt, fc * P:(fc + 1) * P],
                                         z[:, tt, b * 384:(b + 1) * 384], start=tt == 0, stop=tt == 1)
            m = PE.done(last)
            m = self.copy(zf[:, fc, :].rearrange("p (b n) -> p b n", b=2), ps[:, :, 0:384], m, A)
            p.give(i, m)
            marks.append(m)
        return marks

    def filtered(self, o, zf, pf, tmp, marks):
        V, G = self.V, self.G
        sp = self.spec
        V(*marks)
        G(*marks, V.last)
        for b in range(2):
            c = slice(b * 384, (b + 1) * 384)
            k = slice(o * D_MAIN + b * 384, o * D_MAIN + (b + 1) * 384)
            for f in range(2):
                mg = G.done(G.eng.tensor_tensor(tmp[:, f, c], zf[:, 2 + f, c], sp[:, 2 + f, k], ALU.mult))
            V.done(V.eng.tensor_tensor(pf[0][:, :, c], zf[:, 0:2, c], sp[:, 0:2, k], ALU.mult))
            V.done(V.eng.tensor_tensor(pf[1][:, :, c], zf[:, 0:2, c], sp[:, 2:4, k], ALU.mult))
            V(V.last, mg)
            V.done(V.eng.tensor_tensor(pf[0][:, :, c], pf[0][:, :, c], tmp[:, :, c], ALU.subtract))
            V(V.last)
            V.done(V.eng.tensor_tensor(tmp[:, 0, c], zf[:, 2, c], self.spec_i0[:, k], ALU.mult))
            V.done(V.eng.tensor_tensor(tmp[:, 1, c], zf[:, 3, c], sp[:, 1, k], ALU.mult))
            V(V.last)
            yield V.done(V.eng.tensor_tensor(pf[1][:, :, c], pf[1][:, :, c], tmp[:, :, c], ALU.add))

    def hyena(self):
        p, ins, sb = self.prog, self.ins, self.sb
        PE, A, V, G = self.PE, self.A, self.V, self.G
        NU = 3 * NM
        with self.scope():
            self.dft = sb("dft", [P, NT, 2 * T])
            self.idft = sb("idft", [P, 4, T])
            self.spec = sb("spec", [P, 4, NC2])
            self.spec_i0 = sb("spec_i0", [P, NC2])
            self.m_dft = p.dma(G, "dft", [(self.dft[:, :, :], self.c["dft"]), (self.idft[:, :, :], self.c["idft"])])
            self.hyena_filters()
            uT = sb("uT", [P, NU, T + 2])
            ucT = sb("ucT", [P, NU, T])
            xv = sb("xv", [P, NT, 2 * D_MAIN])
            V.done(V.eng.memset(uT[:, :, 0:1], 0.0))
            V.done(V.eng.memset(uT[:, :, T + 1:T + 2], 0.0))
            PE(*self.turned(self.xn, self.xT, self.gains("mix_norm_g_2", 0), *self.m_xn))
            w = ins["hy_w_in_2"][0]
            sw = self.par[:, 1, :]
            uc_marks = {}

            def streams(c0):
                def f(n, ps, m):
                    m = self.copy(uT[:, c0:c0 + n, 1:T + 1], ps, m, A)
                    V(m)
                    for k in range(c0, c0 + n):
                        o = ucT[:, k, :]
                        V.done(V.eng.tensor_scalar(o, uT[:, k, 0:T], sw[:, k:k + 1], None, ALU.mult))
                    for j in (1, 2):
                        for k in range(c0, c0 + n):
                            V(V.last)
                            uc_marks[k] = V.done(V.eng.scalar_tensor_tensor(
                                out=ucT[:, k, :], in0=uT[:, k, j:j + T], scalar=sw[:, j * NU + k:j * NU + k + 1],
                                in1=ucT[:, k, :], op0=ALU.mult, op1=ALU.add))
                    return [m]
                return f
            order = [12, 15, 0, 3, 6, 9]
            for c0 in order:
                self.project_T(w[:, c0 * P:(c0 + 3) * P], self.xT, 384, streams(c0))
            chunks = list(range(NM)) + list(range(2 * NM, 3 * NM))
            xv_marks = []
            for g in (8, 4, 0):
                i, ps = p.take()
                for q in range(4):
                    k = chunks[g + q]
                    PE(uc_marks[k])
                    for tt in range(NT):
                        last = PE.eng.transpose(ps[:, tt, q * P:(q + 1) * P], ucT[:, k, tt * P:(tt + 1) * P], self.ident[:, :])
                m = PE.done(last)
                ms = [self.copy(xv[:, tt, g * P:(g + 4) * P], ps[:, tt, :], m, (A, V)[tt]) for tt in range(NT)]
                p.give(i, *ms)
                xv_marks += ms
            room = self.flat(uT)
            zf = room[:, 0:4 * D_MAIN].rearrange("p (a b) -> p a b", a=4)
            tmp = room[:, 4 * D_MAIN:6 * D_MAIN].rearrange("p (a b) -> p a b", a=2)
            pf = [ucT[:, k:k + NM, :].rearrange("p a b -> p (a b)").rearrange("p (a b) -> p a b", a=2) for k in (0, 2 * NM)]
            z = xv[:, :, D_MAIN:]
            A(*uc_marks.values())
            halves = list(self.filtered(0, zf, pf, tmp, self.spectrum(z, zf, xv_marks)))
            self.project_T(w[:, NU * P:NU * P + 256], self.xT, 256, self.copy_to(self.cqT))
            PE(self.m_copy)
            xz = []
            for b in range(2):
                PE(halves[b])
                i, ps = p.take()
                for tt in range(NT):
                    for fc in range(4):
                        last = PE.eng.matmul(ps[:, tt, 0:384], self.idft[:, fc, tt * P:(tt + 1) * P],
                                             pf[fc // 2][:, fc % 2, b * 384:(b + 1) * 384], start=fc == 0, stop=fc == 3)
                m = PE.done(last)
                V(m)
                m = V.done(V.eng.tensor_tensor(z[:, :, b * 384:(b + 1) * 384], ps[:, :, 0:384],
                                               xv[:, :, b * 384:(b + 1) * 384], ALU.mult))
                p.give(i, m)
                xz.append(m)
            cross = self.attend_steps(self.cross_jobs(0))
            next(cross)
            marks = self.spectrum(z, zf, xz)
            next(cross)
            m_cross = next(cross)
            halves = list(self.filtered(1, zf, pf, tmp, marks))

            def ready(n):
                if n == 0:
                    return m_cross
                b = n - 1
                PE(halves[b])
                i, ps = p.take()
                for q in range(3):
                    for fc in range(4):
                        last = PE.eng.matmul(ps[:, q // 2, (q % 2) * T:(q % 2) * T + T],
                                             pf[fc // 2][:, fc % 2, (3 * b + q) * P:(3 * b + q + 1) * P],
                                             self.idft[:, fc, :], start=fc == 0, stop=fc == 3)
                m = PE.done(last)
                V(m)
                m = V.done(V.eng.tensor_tensor(self.mainT[:, 3 * b:3 * b + 3, :],
                                               ps.rearrange("p a (b t) -> p (a b) t", t=T)[:, 0:3, :],
                                               ucT[:, NM + 3 * b:NM + 3 * b + 3, :], ALU.mult))
                p.give(i, m)
                return [m]
            w = ins["w_out_2"][0]
            panels = self.row_panels(w, ND, NM) + self.row_panels(w, NM)
            self.m_xs = self.accumulate(panels, self.mainT, self.x, ready)
            self.m_xn = self.normed_rows(self.x, self.xn, *self.m_xs)

    def gqa(self):
        p, ins, sb = self.prog, self.ins, self.sb
        PE, A, V, G = self.PE, self.A, self.V, self.G
        NH = N_QH + N_KV
        W = (NH + N_KV) * HD
        with self.scope():
            qkv = sb("qkv", [P, NT, W])
            gain = sb("gain", [P, 2, HD])
            cs = sb("cs", [P, NT, 2, 2, 16])
            tmp = sb("tmp3", [P, 4, 512])
            dup = sb("dup", [P, NT, N_KV, 2, HD])
            qT = sb("qT", [P, NM, T])
            kT = sb("kT", [P, N_KV, T])
            m_in = p.dma(G, "gqa", [
                (gain[:, 0, :], ins["at_q_norm_g_2"].broadcast_to((P, HD))),
                (gain[:, 1, :], ins["at_k_norm_g_2"].broadcast_to((P, HD))),
                (cs[:, :, :, :, :], self.c["axial"])])
            PE(*self.turned(self.xn, self.xT, self.gains("mix_norm_g_2", 1), *self.m_xn))
            w = ins["at_w_in_2"][0]
            V(m_in)

            def rows(c0, heads, k):
                width = heads * HD
                x = qkv[:, :, c0:c0 + width]
                x4 = x.rearrange("p t (h e) -> p t h e", e=HD)
                sq = tmp[:, 0:2, :].rearrange("p a b -> p (a b)")[:, 0:NT * width].rearrange("p (t n) -> p t n", t=NT)
                ss, rs = (self.st[:, o:o + NT * heads] for o in (32, 48))
                V(self.m_copy, V.last)
                V.done(V.eng.tensor_tensor(sq, x, x, ALU.mult))
                V(V.last)
                m = V.done(V.eng.tensor_reduce(ss.rearrange("p (t h) -> p t h", t=NT),
                                               sq.rearrange("p t (h e) -> p t h e", e=HD), AX, ALU.add))
                V(self.rstd(ss, HD, rs, m))
                V.done(V.eng.tensor_tensor(x4, x4, rs.rearrange("p (t h) -> p t h", t=NT).unsqueeze(3)
                                           .broadcast_to((P, NT, heads, HD)), ALU.mult))
                V(V.last)
                n = NT * heads
                for tt in range(NT):
                    x3 = x4[:, tt]
                    V.done(V.eng.tensor_tensor(x3, x3, gain[:, k, :].unsqueeze(1).broadcast_to((P, heads, HD)), ALU.mult))
                V(V.last)
                half = heads * HD // 2
                for tt in range(NT):
                    v = x[:, tt].rearrange("p (h a s f) -> p s h a f", a=2, s=2, f=16)
                    t = [tmp[:, j, tt * half:(tt + 1) * half].rearrange("p (h a f) -> p h a f", a=2, f=16) for j in range(4)]
                    c, s = (cs[:, tt, j].unsqueeze(1).broadcast_to((P, heads, 2, 16)) for j in range(2))
                    for j, (at, by) in enumerate(((0, c), (1, s), (0, s), (1, c))):
                        V.done(V.eng.tensor_tensor(t[j], v[:, at], by, ALU.mult))
                V(V.last)
                for tt in range(NT):
                    v = x[:, tt].rearrange("p (h a s f) -> p s h a f", a=2, s=2, f=16)
                    t = [tmp[:, j, tt * half:(tt + 1) * half].rearrange("p (h a f) -> p h a f", a=2, f=16) for j in range(4)]
                    V.done(V.eng.tensor_tensor(v[:, 0], t[0], t[1], ALU.subtract))
                    V.done(V.eng.tensor_tensor(v[:, 1], t[2], t[3], ALU.add))
                if k:
                    V(V.last)
                    for tt in range(NT):
                        V.done(V.eng.tensor_copy(dup[:, tt], x4[:, tt].unsqueeze(2).broadcast_to((P, N_KV, 2, HD))))
            for c, heads, k in ((N_QH * HD, N_KV, 1), (0, 6, 0), (384, 6, 0), (N_QH * HD + 384, 0, 0)):
                n = min(384, W - c)
                self.project(w[:, c:c + n], self.xT, n, lambda ps, m, c=c, n=n: [self.copy(qkv[:, :, c:c + n], ps, m)])
                if heads:
                    rows(c, heads, k)
            marks = [V.last]
            self.project_T(w[:, W:W + 256], self.xT, 256, self.copy_to(self.cqT))
            PE(self.m_copy)
            m_cross = self.attend(self.cross_jobs(1))
            PE(*marks)
            srcs = [lambda tt, c=c: qkv[:, tt, c * P:(c + 1) * P] for c in range(NM)]
            srcs += [lambda tt, c=c: dup[:, tt, c].rearrange("p a b -> p (a b)") for c in range(N_KV)]
            dst = [qT[:, c, :] for c in range(NM)] + [kT[:, c, :] for c in range(N_KV)]
            for g, n in ((0, 4), (4, 2), (6, 4)):
                i, ps = p.take()
                for q in range(n):
                    for tt in range(NT):
                        last = PE.eng.transpose(ps[:, q // 2, (q % 2) * T + tt * P:(q % 2) * T + tt * P + P], srcs[g + q](tt), self.ident[:, :])
                m = PE.done(last)
                o = qT[:, g:g + n, :] if g < NM else kT[:, g - NM:g - NM + n, :]
                m = self.copy(o, ps.rearrange("p a (b t) -> p (a b) t", t=T)[:, 0:n, :], m)
                p.give(i, m)
            PE(m)
            per = N_QH // N_KV
            jobs = [(tt, lambda h, g=g: qT[self.half(h), 2 * g + h // 2, :],
                     lambda h, g=g: kT[self.half(h), (4 * g + h) // per, :],
                     lambda kt, h, g=g: qkv[:, kt, (NH + (4 * g + h) // per) * HD:(NH + (4 * g + h) // per + 1) * HD],
                     self.mainT[:, 2 * g:2 * g + 2, :]) for g in range(3) for tt in range(NT)]
            m = self.attend(jobs)
            self.m_xs = self.accumulate(self.row_panels(ins["w_out_2"][1], ND), self.mainT, self.x, lambda n: m + m_cross)
            self.m_xn = self.normed_rows(self.x, self.xn, *self.m_xs)

    def experts(self, i):
        p, ins, sb = self.prog, self.ins, self.sb
        PE, A, V, G = self.PE, self.A, self.V, self.G
        NG = N_EXP // 4
        with self.scope():
            aff = sb("aff", [P, NT, N_EXP])
            affT, work = (self.cqT[0:N_EXP, k, :] for k in range(2))
            main, xT = self.flat(self.mainT), self.flat(self.xT)
            W = N_EXP * CAP
            pick = main[:, 0:NT * W].rearrange("p (a w) -> p a w", a=NT)
            share = main[:, NT * W:2 * NT * W].rearrange("p (a w) -> p a w", a=NT)
            shareT = xT[:, 0:NG * T].rearrange("p (a t) -> p a t", a=NG)
            xgT = xT[:, NG * T:NG * T + ND * P].rearrange("p (a t) -> p a t", a=ND)
            slot = sb("slot", [N_EXP, T])
            ones = sb("ones3", [N_EXP, T])
            top8 = sb("top8b", [N_EXP, 8])
            slots = sb("slots", [P, NT, N_EXP])
            pick_g = sb("pick_g", [P, NT, P])
            share_g = sb("share_g", [P, T])
            sig = sb("sig", [P, 2, 256])
            hid = sb("hid", [P, 2, 256])
            hidT = sb("hidT", [P, 2, 2, 96])
            y = sb("y", [P, 2, 512])
            p.grow(sb("more_ring", [P, MORE, SLOT]))
            m_ones = V.done(V.eng.memset(ones[:, :], 1.0))
            gain = self.gains("ffn_norm_g_2", i)
            PE(*self.turned(self.xn, self.xT, gain, *self.m_xn), self.m_c2)
            k, ps = p.take()
            for tt in range(NT):
                for d in range(ND):
                    last = PE.eng.matmul(ps[:, 0, tt * N_EXP:(tt + 1) * N_EXP], self.xT[:, d, tt * P:(tt + 1) * P],
                                         self.router[:, i, d, :], start=d == 0, stop=d == ND - 1)
            m = PE.done(last)
            s = self.st
            V(m)
            af = aff[:, :, :]
            lg = ps[:, 0, 0:NT * N_EXP].rearrange("p (a e) -> p a e", a=NT)
            V.done(V.eng.tensor_reduce(s[:, 0:NT], lg, AX, ALU.max))
            V(V.last)
            m = V.done(V.eng.tensor_tensor(af, lg, s[:, 0:NT].unsqueeze(2).broadcast_to((P, NT, N_EXP)), ALU.subtract))
            p.give(k, m)
            A(m)
            m = A.done(A.eng.activation(af, af, ACT.Exp))
            V(m)
            V.done(V.eng.tensor_reduce(s[:, 4:4 + NT], af, AX, ALU.add))
            V(V.last)
            V.done(V.eng.reciprocal(s[:, 4:4 + NT], s[:, 4:4 + NT]))
            V(V.last)
            m = V.done(V.eng.tensor_tensor(af, af, s[:, 4:4 + NT].unsqueeze(2).broadcast_to((P, NT, N_EXP)), ALU.mult))
            PE(m)
            k, ps = p.take()
            for tt in range(NT):
                last = PE.eng.transpose(ps[0:N_EXP, 0, tt * P:(tt + 1) * P], aff[:, tt, :], self.ident[:, :])
            m = PE.done(last)
            V(m)
            m = V.done(V.eng.tensor_copy(affT, ps[0:N_EXP, 0, 0:T]))
            p.give(k, m)
            for r in range(CAP // 8):
                src = affT if r == 0 else work
                V(V.last)
                V.done(V.eng.max(out=top8[:, :], in_=src))
                V(V.last)
                V.done(V.eng.match_replace(out=work, in_to_replace=top8[:, :], in_values=src, imm_value=TINY))
            V(V.last)
            V.done(V.eng.tensor_scalar(work, work, 2 * NEG, None, ALU.is_lt))
            V(V.last, m_ones)
            V.done(V.eng.tensor_tensor_scan(slot[:, :], ones[:, :], work, 0.0, ALU.mult, ALU.add))
            V(V.last)
            m = V.done(V.eng.tensor_tensor(slot[:, :], slot[:, :], work, ALU.mult))
            PE(m)
            k, ps = p.take()
            for tt in range(NT):
                last = PE.eng.transpose(ps[:, 0, tt * N_EXP:(tt + 1) * N_EXP], slot[:, tt * P:(tt + 1) * P], self.ident[0:N_EXP, 0:N_EXP])
            m = PE.done(last)
            V(m)
            m = V.done(V.eng.tensor_copy(slots[:, :, :], ps[:, 0, 0:NT * N_EXP].rearrange("p (a e) -> p a e", a=NT)))
            p.give(k, m)
            V(m, self.m_c2)
            for tt in range(NT):
                pk = pick[:, tt].rearrange("p (e r) -> p e r", r=CAP)
                V.done(V.eng.tensor_tensor(pk, slots[:, tt, :].unsqueeze(2).broadcast_to((P, N_EXP, CAP)),
                                           self.iota[:, :].unsqueeze(1).broadcast_to((P, N_EXP, CAP)), ALU.is_equal))
            V(V.last)
            for tt in range(NT):
                pk, sh = (t[:, tt].rearrange("p (e r) -> p e r", r=CAP) for t in (pick, share))
                m = V.done(V.eng.tensor_tensor(sh, pk, aff[:, tt, :].unsqueeze(2).broadcast_to((P, N_EXP, CAP)), ALU.mult))
            PE(m)
            k, ps = p.take()
            for g in range(NG):
                for tt in range(NT):
                    last = PE.eng.transpose(ps[:, g // 2, (g % 2) * T + tt * P:(g % 2) * T + tt * P + P],
                                            share[:, tt, g * P:(g + 1) * P], self.ident[:, :])
            m = PE.done(last)
            m = self.copy(shareT[:, :, :], ps.rearrange("p a (b t) -> p (a b) t", t=T), m)
            p.give(k, m)

            ds = bass.ds
            with p.loop_of(f"experts{i}", NG) as g:
                self.expert_group(i, g, ds, pick, pick_g, shareT, share_g, xgT, sig, hid, hidT, y, gain)
            p.shrink()
            self.m_xn = self.normed_rows(self.x, self.xn, *self.m_xs)

    def expert_group(self, i, g, ds, pick, pick_g, shareT, share_g, xgT, sig, hid, hidT, y, gain):
        p, ins = self.prog, self.ins
        PE, A, V = self.PE, self.A, self.V
        V.done(V.eng.tensor_copy(pick_g[:, :, :], pick[:, :, ds(g * P, P)]))
        m_sh = V.done(V.eng.tensor_copy(share_g[:, :], shareT[:, ds(g, 1), :].rearrange("p a t -> p (a t)")))
        PE(m_sh)
        k, ps = p.take()
        for d in range(ND):
            for tt in range(NT):
                last = PE.eng.matmul(ps[:, d // 4, (d % 4) * P:(d % 4 + 1) * P], self.xn[:, tt, d * P:(d + 1) * P],
                                     pick_g[:, tt, :], start=tt == 0, stop=tt == 1)
        m = PE.done(last)
        A(m)
        V(m)
        for d in range(ND):
            o, s, gn = xgT[:, d, :], ps[:, d // 4, (d % 4) * P:(d % 4 + 1) * P], gain[:, d:d + 1]
            if d < 4:
                a = A.done(A.eng.activation(o, s, ACT.Copy, scale=gn))
            else:
                v = V.done(V.eng.tensor_scalar(o, s, gn, None, ALU.mult))
        p.give(k, a, v)
        PE(a, v)
        ky, py = p.take()
        state = {}

        def up(e):
            k, ps = p.take()
            for b, name in enumerate(("exp_w_gate_2", "exp_w_up_2")):
                w = ins[name][i, ds(g * 4 + e, 1), :, :].rearrange("a d n -> (a d) n")
                for r0 in range(0, ND, 4):
                    u = self.unit(w[r0 * P:(r0 + 4) * P, :], 4, E_FF)
                    for r in range(4):
                        for j in range(3):
                            last = PE.eng.matmul(ps[32 * j:32 * j + 32, b, 0:256], xgT[:, r0 + r, 32 * e:32 * e + 32],
                                                 u[:, r, j * 256:(j + 1) * 256],
                                                 start=r0 + r == 0, stop=r0 + r == ND - 1)
                    m = PE.done(last, p.used)
                if b == 0:
                    A(m, state.get(("free", e % 2)))
                    m_sig = A.done(A.eng.activation(sig[0:96, e % 2, :], ps[0:96, 0, 0:256], ACT.Sigmoid))
                    V(m_sig)
                    V.done(V.eng.tensor_tensor(sig[0:96, e % 2, :], ps[0:96, 0, 0:256], sig[0:96, e % 2, :], ALU.mult))
            V(m, V.last, state.get(("free", e % 2)))
            m = V.done(V.eng.tensor_tensor(hid[0:96, e % 2, :], ps[0:96, 1, 0:256], sig[0:96, e % 2, :], ALU.mult))
            p.give(k, m)
            state[e] = m

        def down(e):
            PE(state[e])
            k, ps = p.take()
            for c in range(2):
                last = PE.eng.transpose(ps[:, 0, c * 96:(c + 1) * 96], hid[0:96, e % 2, c * P:(c + 1) * P], self.ident[0:96, 0:96])
            m = PE.done(last)
            state["free", e % 2] = m
            A(state.get(("t", e % 2)))
            m = self.copy(hidT[:, e % 2].rearrange("p a b -> p (a b)"), ps[:, 0, 0:192], m, A)
            p.give(k, m)
            PE(m)
            w = ins["exp_w_down_2"][i, ds(g * 4 + e, 1), :, :].rearrange("a d n -> (a d) n")
            for r0 in range(0, NM, 3):
                u = self.unit(w[r0 * P:(r0 + 3) * P, :], 3, D)
                for r in range(3):
                    j, c = (r0 + r) // 2, (r0 + r) % 2
                    for b in range(2):
                        last = PE.eng.matmul(py[32 * e:32 * e + 32, b, :], hidT[:, e % 2, c, 32 * j:32 * j + 32],
                                             u[:, r, b * 512:(b + 1) * 512], start=r0 + r == 0, stop=r0 + r == NM - 1)
                m = PE.done(last, p.used)
            state["t", e % 2] = m
            return m
        up(0)
        for e in range(1, 4):
            up(e)
            down(e - 1)
        m = down(3)
        ma = self.copy(y[:, 0, :], py[:, 0, :], m, A)
        mv = self.copy(y[:, 1, :], py[:, 1, :], m, V)
        p.give(ky, ma, mv)
        PE(ma, mv)
        self.m_xs = []
        for tt in range(NT):
            k, ps = p.take()
            for b in range(2):
                last = PE.eng.matmul(ps[:, b, :], share_g[:, tt * P:(tt + 1) * P], y[:, b, :], start=True, stop=True)
            m = PE.done(last)
            V(m)
            m = V.done(V.eng.tensor_tensor(self.x[:, tt, :], self.x[:, tt, :], ps.rearrange("p a b -> p (a b)"), ALU.add))
            p.give(k, m)
            self.m_xs.append(m)

    def block2(self):
        self.block2_memory()
        self.hyena()
        self.experts(0)
        self.gqa()
        self.experts(1)

    def finish(self):
        p, V, A = self.prog, self.V, self.A
        with self.scope():
            g = self.sb("final_gain", [P, D])
            m = p.dma(self.G, "final", [(g[:, :], self.ins["final_norm_g_2"].unsqueeze(0).broadcast_to((P, D)))])
            V(m, *self.m_xn)
            stored = Counter(p, "stored")
            out = self.out[0].rearrange("(a p) d -> p a d", p=P)
            for tt in range(NT):
                m = V.done(V.eng.tensor_tensor(self.xn[:, tt, :], self.xn[:, tt, :], g[:, :], ALU.mult))
                self.prog.sp(m)
                self.nc.sync.dma_start(out[:, tt, :], self.xn[:, tt, :]).then_inc(stored.sem, 16)
                stored.count += 16
            self.prog.sp(stored.mark())

    def run(self):
        self.setup()
        with self.scope():
            self.block1()
        self.block2()
        self.finish()
        self.room.close()


_DRAM_CONSTS = ("ident", "negu", "strict", "levels", "dsa_cos", "dsa_sin")


def constants():
    f = np.float32
    out = {"ident": np.eye(P, dtype=f)}
    s = np.arange(P)
    out["negu"] = -(s[:, None] >= s[None, :]).astype(f)
    out["strict"] = (s[:, None] < s[None, :]).astype(f)
    r = s % 32
    lv = []
    for m in MASKED:
        t = np.arange(32)
        if m:
            same = (r[:, None] // (2 * m)) == (t[None, :] // (2 * m))
            lv.append(same & (r[:, None] % (2 * m) < m) & (t[None, :] % (2 * m) >= m))
        else:
            lv.append(r[:, None] == t[None, :])
    out["levels"] = np.stack(lv, 1).astype(f)
    half = ROT // 2
    inv = f(500000.0) ** (-(np.arange(half, dtype=f) * f(2.0)) / f(ROT))
    ang = np.arange(T, dtype=f)[:, None] * inv[None, :].astype(f)
    cos, sin = (np.tile(g(ang.astype(np.float64))[:, None, :], (1, NBLK, 1)) for g in (np.cos, np.sin))
    cos[:, 7], sin[:, 7] = 1.0, 0.0
    for n, a in (("dsa_cos", cos), ("dsa_sin", sin)):
        out[n] = np.ascontiguousarray(a.reshape(NT, P, NBLK * half).transpose(1, 0, 2)).astype(f)
    out["iota"] = np.broadcast_to(np.arange(1, CAP + 1, dtype=f), (P, CAP)).copy()
    t, k = np.arange(T)[:, None], np.arange(T)[None, :]
    ph = np.pi * ((t * k) % (2 * T)) / T
    fwd = np.concatenate([np.cos(ph), -np.sin(ph)], 1)
    fwd[:, T] = (-1.0) ** np.arange(T)
    out["dft"] = np.ascontiguousarray(fwd.reshape(NT, P, 2 * T).transpose(1, 0, 2)).astype(f)
    scale = np.full(2 * T, 2.0)
    scale[0] = scale[T] = 1.0
    inv_ = (fwd * scale / (2 * T)).T
    out["idft"] = np.ascontiguousarray(inv_.reshape(4, P, T).transpose(1, 0, 2)).astype(f)
    tl = np.linspace(0.0, 1.0, T, dtype=f)[:, None]
    wl = (f(2.0 * math.pi) * np.arange(T, dtype=f)[:, None] / f(T)).astype(f)
    bands = np.linspace(1e-4, 15, 16, dtype=f)[None, :]
    bw = (bands * wl).astype(np.float64)
    out["featsT"] = np.ascontiguousarray(np.concatenate([tl, np.cos(bw), -np.sin(bw)], 1).T).astype(f)
    lo, hi = math.log(1e-2) / 1.5, math.log(1e-2) / 0.3
    dec = np.exp(-tl.astype(np.float64) * np.abs(np.linspace(lo, hi, D_MAIN, dtype=f)))
    out["decay"] = np.ascontiguousarray(dec.reshape(NT, P, D_MAIN).transpose(1, 0, 2)).astype(f)
    pos = np.stack([np.repeat(np.arange(T // 64), 64), np.tile(np.arange(64), T // 64)], 1).astype(f)
    inv2 = f(1.0) / (f(10000.0) ** (np.arange(0, 32, 2, dtype=f) / f(32)))
    an = (pos[:, :, None] * inv2).astype(f).astype(np.float64)
    ax = np.stack([np.cos(an), np.sin(an)], 1).reshape(NT, P, 2, 2, 16).transpose(1, 0, 2, 3, 4)
    out["axial"] = np.ascontiguousarray(ax).astype(f)
    return out


OUT = "out_0_dram"


def build(new_bass, arrays):
    per_iteration = {}
    for _ in range(2):
        nc = new_bass()
        aps = {n: nc.dram_tensor(n, a.shape, F32, kind="ExternalInput").ap() for n, a in arrays.items()}
        ins = {n[3:]: a for n, a in aps.items() if n.startswith("in_")}
        consts = {n[6:]: a for n, a in aps.items() if n.startswith("const_")}
        out = nc.dram_tensor(OUT, (1, T, D), F32, kind="ExternalOutput").ap()
        Kernel(nc, per_iteration, ins, consts, out).run()
    return nc


def kernel(**inputs):
    import concourse.bacc as bacc
    from concourse.bass_utils import run_bass_kernel_spmd

    arrays = {f"in_{n}": np.ascontiguousarray(a) for n, a in inputs.items()}
    arrays |= {f"const_{n}": a for n, a in constants().items()}
    nc = build(lambda: bacc.Bacc("TRN2", target_bir_lowering=False, num_devices=1), arrays)
    r = run_bass_kernel_spmd(nc, [arrays], core_ids=[0])
    return r.results[0][OUT]
```

```python
import math
from contextlib import ExitStack, contextmanager

import numpy as np

import concourse.bass as bass
from concourse import mybir

F32R = mybir.dt.float32r
F32 = mybir.dt.float32
I32 = mybir.dt.int32
ALU = mybir.AluOpType
ACT = mybir.ActivationFunctionType
AX = mybir.AxisListType.X

P = 128
T = 256
NT = T // P
D = 1024
ND = D // P
DEPTH = 2
HD = 64
EPS = 1e-6
NEG = -1e30
N_SB = N_DSA = 6
N_IDX = 8
K_TOP = min(256, T // 4)
N_HG = 4
HG_DK = 128
D_FF = 4 * D
ROT = HD // 4
F_MIN = 1e-12
IDX_SCALE = (HD * N_IDX) ** -0.5
C_SQ, C_SK, C_SV = 0, 384, 768
C_DSA = 1152
W_DSA = 384 + 64 + 64 + 512 + 64 + 8
C_HQ = C_DSA + W_DSA
C_HI = C_HQ + 1024
C_GATE = C_HI + 512
D_IN = C_GATE + 3 * D
NBLK = 17
HG_LEVELS = (128, 64, 32, 16, 8, 4, 2, 1)
MASKED = (16, 8, 4, 2, 1, 0)
D_MAIN = 768
NM = D_MAIN // P
N_QH, N_KV, N_MEM = 12, 4, 4
N_EXP = 16
CAP = 2 * T // N_EXP
E_FF = 768
N_FEAT = 33
FILT = 64
ORD = 2
NC2 = ORD * D_MAIN
SLOTS = 4
PIECES = 3
MORE = 8
SLOT = 3072
TINY = -3.0e38


class Counter:

    def __init__(self, prog, name, start=0):
        self.prog, self.name, self.count = prog, name, start
        self.sem = prog.nc.alloc_semaphore(name)
        prog.counters.append(self)

    def mark(self):
        return Mark(self, self.count, self.prog.loop)


class Mark:

    def __init__(self, counter, count, loop):
        self.counter, self.count, self.loop = counter, count, loop

    def value(self):
        loop = self.loop
        if loop is None:
            return self.count
        per = loop.per.get(self.counter.name, 0)
        if loop.closed:
            return self.count + (loop.n - 1) * per
        return loop.reg * per + self.count if per else self.count


class Loop:
    def __init__(self, name, n, per):
        self.name, self.n, self.per, self.closed, self.reg = name, n, per, False, None


class Engine:

    def __init__(self, prog, eng, name):
        self.prog, self.eng, self.name = prog, eng, name
        self.sig = Counter(prog, "s_" + name)
        self.seen = {}

    def __call__(self, *marks):
        for m in marks:
            if m is None:
                continue
            key = m.counter.name
            if m.loop is not None and m.loop.closed:
                m = Mark(m.counter, m.value(), None)
            got = self.seen.get((key, m.loop), -1)
            if got >= m.count:
                continue
            self.seen[(key, m.loop)] = m.count
            self.eng.wait_ge(m.counter.sem, m.value())
        return self.eng

    def done(self, inst, counter=None):
        s = counter or self.sig
        inst.then_inc(s.sem, 1)
        s.count += 1
        return s.mark()

    @property
    def last(self):
        return self.sig.mark()


class Program:

    def __init__(self, nc, per_iteration):
        self.nc, self.loop, self.counters = nc, None, []
        self.per_iteration = per_iteration
        self.pe = Engine(self, nc.tensor, "pe")
        self.act = Engine(self, nc.scalar, "act")
        self.dve = Engine(self, nc.vector, "dve")
        self.pool = Engine(self, nc.gpsimd, "pool")
        self.sp = Engine(self, nc.sync, "sp")
        self.engines = (self.pe, self.act, self.dve, self.pool)
        self.used = Counter(self, "used", SLOTS)
        nc.tensor.sem_inc(self.used.sem, SLOTS)
        self.landed = [Counter(self, f"landed{i}") for i in range(SLOTS + MORE)]
        self.ring = nc.alloc_sbuf_tensor("ring", [P, SLOTS, SLOT], F32)
        self.order = [(self.ring, i) for i in range(SLOTS)]
        self.units_used = 0
        self.psum = nc.alloc_psum_tensor("psum", [P, 4, 2, 512], F32)
        self.free_marks = [[] for _ in range(4)]
        self.free_order = [0, 1, 2, 3]

    def meet(self):
        marks = [e.sig.mark() for e in self.engines] + [self.used.mark()]
        for e in self.engines:
            e(*[m for m in marks if m.count])
        self.free_marks = [[] for _ in range(4)]

    @contextmanager
    def loop_of(self, name, n):
        loop = Loop(name, n, self.per_iteration.get(name, {}))
        start = {s.name: s.count for s in self.counters}
        with self.nc.Fori(0, n) as i:
            loop.reg = i
            self.loop = loop
            self.meet()
            yield i
        self.loop = None
        gave = {s.name: s.count - start.get(s.name, 0) for s in self.counters}
        gave = {k: v for k, v in gave.items() if v}
        if name in self.per_iteration:
            assert gave == self.per_iteration[name]
        self.per_iteration[name] = gave
        loop.per, loop.closed = gave, True
        for s in self.counters:
            s.count += (n - 1) * gave.get(s.name, 0)
        self.units_used += (n - 1) * gave.get("used", 0)

    def dma(self, engine, name, pairs, *after):
        s = Counter(self, f"in_{name}")
        engine(*after)
        for to, of in pairs:
            engine.eng.dma_start(to, of).then_inc(s.sem, 16)
            s.count += 16
        return s.mark()

    def unit(self, src, rows, cols):
        slot = self.order.pop(0)
        self.order.append(slot)
        ring, at = slot
        need = Mark(self.used, self.units_used + 1, self.loop)
        self.sp(need)
        s = self.landed[at if ring is self.ring else SLOTS + at]
        view = ring[:, at, 0:rows * cols].rearrange("p (c n) -> p c n", c=rows)
        self.nc.sync.dma_start(view, src.rearrange("(c p) n -> p c n", p=P)).then_inc(s.sem, 16)
        s.count += 16
        self.units_used += 1
        return view, s.mark()

    def grow(self, more):
        self.pe.eng.sem_inc(self.used.sem, MORE)
        self.used.count += MORE
        self.order += [(more, i) for i in range(MORE)]

    def shrink(self):
        self.units_used += MORE
        self.order = [s for s in self.order if s[0] is self.ring]

    def take(self):
        i = self.free_order.pop(0)
        self.pe(*self.free_marks[i])
        return i, self.psum[:, i, :, :]

    def give(self, i, *marks):
        self.free_marks[i] = list(marks)
        self.free_order.append(i)


class Kernel:

    def __init__(self, nc, per_iteration, ins, consts, out):
        self.nc, self.ins, self.c, self.out = nc, ins, consts, out
        self.prog = Program(nc, per_iteration)
        p = self.prog
        self.PE, self.A, self.V, self.G = p.pe, p.act, p.dve, p.pool
        self.room, self.names, self.fillers = ExitStack(), {}, []

    def sb(self, name, shape, dt=F32):
        self.names[name] = self.names.get(name, 0) + 1
        name += f"_{self.names[name]}" if self.names[name] > 1 else ""
        return self.room.enter_context(self.nc.sbuf_tensor(name, shape, dt))

    def flat(self, t):
        return t[:, :, :].rearrange("p a b -> p (a b)")

    @contextmanager
    def scope(self, meet=True):
        outer = self.room
        with ExitStack() as self.room:
            yield
            if meet:
                self.prog.meet()
        self.room = outer

    def grow_ring(self):
        p = self.prog
        p.pe(*[e.last for e in p.engines], p.used.mark())
        p.grow(self.sb("more_ring", [P, MORE, SLOT]))


    def rstd(self, ss, n, out, after):
        V, A = self.V, self.A
        V(after)
        m = V.done(V.eng.tensor_scalar(out, ss, 1.0 / n, EPS, ALU.mult, ALU.add))
        A(m)
        m = A.done(A.eng.activation(out, out, ACT.Sqrt))
        V(m)
        return V.done(V.eng.reciprocal(out, out))

    def sqrt_table(self):
        self.A(self.m_one)
        self.A.done(self.A.eng.activation(self.one[:, :], self.one[:, :], ACT.Sqrt))

    def normed_rows(self, x, xn, *after):
        V, A = self.V, self.A
        self.sqrt_table()
        V(*after)
        for tt in range(NT):
            A(*after[tt:tt + 1])
            m = A.done(A.eng.activation(xn[:, tt, :], x[:, tt, :], ACT.Square,
                                        accum_out=self.ss[:, tt:tt + 1]))
        m = self.rstd(self.ss[:, 0:NT], D, self.rs[:, 0:NT], m)
        A(m)
        V(m)
        for tt in range(NT):
            rs = self.rs[:, tt:tt + 1]
            mv = V.done(V.eng.tensor_scalar(xn[:, tt, 0:D // 2], x[:, tt, 0:D // 2], rs, None, ALU.mult))
            ma = A.done(A.eng.activation(xn[:, tt, D // 2:], x[:, tt, D // 2:], ACT.Copy, scale=rs))
        return mv, ma

    def turned(self, xn, xT, gain, *after):
        PE, A, V, p = self.PE, self.A, self.V, self.prog
        PE(self.m_ident)
        marks = []
        for c, m in ((0, after[0]), (4, after[1])):
            PE(m)
            i, ps = p.take()
            for k in range(4):
                for tt in range(NT):
                    o = ps[:, k // 2, (k % 2) * T + tt * P:(k % 2) * T + tt * P + P]
                    last = PE.eng.transpose(o, xn[:, tt, (c + k) * P:(c + k + 1) * P], self.ident[:, :])
            m = PE.done(last)
            A(m)
            V(m)
            for k in range(4):
                o, s = xT[:, c + k, :], ps[:, k // 2, (k % 2) * T:(k % 2) * T + T]
                g = gain[:, c + k:c + k + 1]
                if k // 2:
                    a = A.done(A.eng.activation(o, s, ACT.Copy, scale=g))
                else:
                    v = V.done(V.eng.tensor_scalar(o, s, g, None, ALU.mult))
            p.give(i, a, v)
            marks.append([a, v])
        self.xT_late = marks[1]
        return marks[0]

    def fill(self, n=1):
        for _ in range(n):
            if self.fillers:
                self.fillers.pop(0)()

    def unit(self, src, rows, cols):
        u, m = self.prog.unit(src, rows, cols)
        self.PE(m)
        return u

    def project_T(self, src, xT, cols, evacuate):
        PE, p = self.PE, self.prog
        u = self.unit(src, ND, cols)
        n = cols // P
        i, ps = p.take()
        for c in range(n):
            o = ps[:, c // 2, (c % 2) * T:(c % 2) * T + T]
            for d in range(ND):
                if d == ND // 2:
                    PE(*self.xT_late)
                last = PE.eng.matmul(o, u[:, d, c * P:(c + 1) * P], xT[:, d, :],
                                     start=d == 0, stop=d == ND - 1)
        m = PE.done(last, p.used)
        flat = ps.rearrange("p a (b t) -> p (a b) t", t=T)[:, 0:n, :]
        p.give(i, *evacuate(n, flat, m))

    def project(self, src, xT, cols, evacuate):
        PE, p = self.PE, self.prog
        u = self.unit(src, ND, cols)
        i, ps = p.take()
        for tt in range(NT):
            for d in range(ND):
                if d == ND // 2:
                    PE(*self.xT_late)
                last = PE.eng.matmul(ps[:, tt, 0:cols], xT[:, d, tt * P:(tt + 1) * P], u[:, d, :],
                                     start=d == 0, stop=d == ND - 1)
        m = PE.done(last, p.used)
        p.give(i, *evacuate(ps[:, :, 0:cols], m))

    def copy_to(self, dst, engine=None, scale=None):
        at = [0]

        def evacuate(n, ps, m):
            o = dst[:, at[0]:at[0] + n, :]
            at[0] += n
            return [self.copy(o, ps, m, engine, scale)]
        return evacuate

    def copy(self, o, i, m, engine=None, scale=None):
        engine = engine or self.A
        engine(m)
        if engine is self.A:
            r = engine.done(engine.eng.activation(o, i, ACT.Copy, scale=1.0 if scale is None else scale))
        elif scale is None:
            r = engine.done(engine.eng.tensor_copy(o, i))
        else:
            r = engine.done(engine.eng.tensor_scalar(o, i, scale, None, ALU.mult))
        self.m_copy = r
        return r

    def accumulate(self, srcs, lhsT, x, ready):
        PE, V, p = self.PE, self.V, self.prog
        PE(*ready(0))
        i, pa = p.take()
        j, pb = p.take()
        pair = (pa, pb)
        for n, (src, at, rows) in enumerate(srcs):
            PE(*(ready(n) if n else ()))
            u = self.unit(src, rows, D)
            end = n == len(srcs) - 1
            steps = [(r, tt) for r in range(rows) for tt in range(NT)]
            if end:
                steps.sort(key=lambda s: s[1])
            for r, tt in steps:
                for h in range(2):
                    last = PE.eng.matmul(pair[tt][:, h, :], lhsT[:, at + r, tt * P:(tt + 1) * P],
                                         u[:, r, h * 512:(h + 1) * 512],
                                         start=n == 0 and r == 0, stop=end and r == rows - 1)
                if end and (r, tt) == (rows - 1, 0):
                    m0 = PE.done(last)
            m1 = PE.done(last, p.used)
        marks = []
        for tt, m in ((0, m0), (1, m1)):
            V(m)
            marks.append(V.done(V.eng.tensor_tensor(x[:, tt, :], x[:, tt, :],
                                                    pair[tt].rearrange("p a b -> p (a b)"), ALU.add)))
        p.give(i, marks[0])
        p.give(j, marks[1])
        return marks

    def row_panels(self, w, n, first=0):
        out, at = [], first
        while at < n:
            r = min(3, n - at)
            out.append((w[at * P:(at + r) * P, :], at, r))
            at += r
        return out


    def setup(self):
        p, c, ins, sb = self.prog, self.c, self.ins, self.sb
        PE, A, V, G = self.PE, self.A, self.V, self.G
        self.ident = sb("ident", [P, P])
        self.x = sb("x", [P, NT, D])
        self.xT = sb("xT", [P, ND, T])
        self.xn = sb("xn", [P, NT, D])
        self.ss = sb("ss", [P, 32])
        self.rs = sb("rs", [P, 32])
        self.one = sb("one", [P, 1])
        self.m_one = V.done(V.eng.memset(self.one[:, :], 1.0))
        m_x = p.dma(A, "x", [(self.x[:, :, :], ins["x"][0].rearrange("(a p) d -> p a d", p=P))])
        self.m_ident = p.dma(A, "ident", [(self.ident[:, :], c["ident"])])
        rows, at = [], 0
        self.col = {}
        for name in ("norm_mix", "norm_mlp", "hgrn_lb", "mix_norm_g_2", "ffn_norm_g_2", "mem_norm_g_2"):
            a = ins[name]
            n = math.prod(a.shape) // P
            flat = a.rearrange("a (b p) -> (a b) p", p=P) if len(a.shape) == 2 else a.rearrange("(b p) -> b p", p=P)
            rows.append((at, n, flat))
            self.col[name] = at
            at += n
        n_short = 3 * 3 * NM
        rowbuf = self.xn[:, 0, 0:2 * P].rearrange("p (a b) -> p a b", a=2)
        self.par = sb("par", [P, 2, P])
        pairs = [(rowbuf[a:a + n, 0, :], f) for a, n, f in rows]
        pairs.append((rowbuf[0:n_short, 1, :], ins["hy_short_w_2"][0].rearrange("a (b p) -> (a b) p", p=P)))
        m = p.dma(p.sp, "rows", pairs)
        PE(m, self.m_ident)
        i, ps = p.take()
        PE.eng.transpose(ps[:, 0, 0:at], rowbuf[0:at, 0, :], self.ident[0:at, 0:at])
        m = PE.done(PE.eng.transpose(ps[:, 0, P:P + n_short], rowbuf[0:n_short, 1, :],
                                     self.ident[0:n_short, 0:n_short]))
        V(m)
        V.done(V.eng.tensor_copy(self.par[:, 0, 0:at], ps[:, 0, 0:at]))
        m_par = V.done(V.eng.tensor_copy(self.par[:, 1, 0:n_short], ps[:, 0, P:P + n_short]))
        p.give(i, m_par)
        self.m_par = m_par
        self.m_x = m_x

    def gains(self, name, l=0):
        at = self.col[name] + l * ND
        return self.par[:, 0, at:at + ND]


    def mixer_memory(self):
        sb = self.sb
        self.gate = sb("gate", [P, 4 * ND, T])
        self.mixT = self.xT
        self.sqT = sb("sqT", [P, 3, T])
        self.skT = sb("skT", [P, 3, T])
        self.hvg = sb("hvg", [P, NT, 512])
        self.sv = self.hvg[:, :, 0:384]
        self.oT = sb("oT", [P, 3, T])
        self.dsa = sb("dsa", [P, NT, W_DSA])
        self.dT = sb("dT", [P, 9, T])
        self.rot = self.dT[:, 0:4, 0:NBLK * 8]
        self.att = sb("att", [P, N_HG, 384])
        early = self.flat(self.att)[:, 0:2 * NT * T].rearrange("p (k a t) -> p k a t", k=2, a=NT)
        self.score, self.work = early[:, 0], early[:, 1]
        self.top8 = sb("top8", [P, NT, 8])
        self.big1 = self.xn[:, :, :].rearrange("p a (b t) -> p (a b) t", t=T)[:, 0:6, :]
        self.big2 = sb("big2", [P, 6, T])
        self.hqT = sb("hqT", [P, N_HG, T])
        self.hkT = sb("hkT", [P, N_HG, T])
        self.hbT = sb("hbT", [P, N_HG, T])
        self.hw = self.gate[:, 3 * ND:3 * ND + N_HG, :]
        self.hw2 = self.gate[:, 3 * ND + N_HG:4 * ND, :]
        self.ones = sb("ones", [P, T])
        self.held_back(self.idle[:, :])
        self.m_set1 = self.G.done(self.G.eng.memset(self.ones[:, :], 1.0))
        self.gatebuf = self.big2[:, :, :]
        self.hg_oT = self.skT[:, 0:2, :]
        self.dsa_oT = self.sqT[:, :, :]

    def mlp_memory(self):
        sb = self.sb
        self.hid_hi, self.hid_lo = (sb(n, [P, D_FF // P, T], F32R) for n in ("hid_hi", "hid_lo"))
        self.units = self.flat(self.xn)[:, 0:2 * 3 * T].rearrange("p (k c t) -> p k c t", k=2, c=3)

    def block1_memory(self):
        sb, p, c, A, G = self.sb, self.prog, self.c, self.A, self.G
        self.small = sb("small", [P, 64])
        self.xT_hi, self.xT_lo = (sb(n, [P, ND, T], F32R) for n in ("xT_hi", "xT_lo"))
        self.w_hi, self.w_lo = (sb(n, [P, PIECES, D], F32R) for n in ("w_hi", "w_lo"))
        self.negu = sb("negu", [P, P])
        self.negone = sb("negone", [P, P])
        self.strict = sb("strict", [P, P])
        self.lvl = sb("lvl", [P, len(MASKED), 32])
        self.rc = sb("rc", [P, NT, NBLK * 8])
        self.rsn = sb("rsn", [P, NT, NBLK * 8])
        self.m_c1 = p.dma(G, "consts1", [
            (self.negu[:, :], c["negu"]), (self.strict[:, :], c["strict"]),
            (self.lvl[:, :, :], c["levels"]), (self.rc[:, :, :], c["dsa_cos"]),
            (self.rsn[:, :, :], c["dsa_sin"])])
        V = self.V
        V.done(V.eng.memset(self.negone[:, :], -1.0))
        self.gcur = sb("gcur", [P, 2 * ND])
        self.lb = sb("lb", [P, DEPTH, N_HG])
        self.lbc = sb("lbc", [P, 2, N_HG])
        self.qkg = sb("qkg", [P, 2, HD])
        self.og = sb("og", [P, 1])
        self.idle = sb("idle", [P, 1])
        self.idle_v = sb("idle_v", [P, 1])
        self.m_idle = G.done(G.eng.memset(self.idle[:, :], 0.0))
        at = self.col["hgrn_lb"]
        a = [self.par[:, 0, at + l * N_HG:at + (l + 1) * N_HG] for l in range(DEPTH)]
        s = self.small
        V(self.m_par)
        V.done(V.eng.tensor_tensor(s[:, 0:4], a[0], a[1], ALU.max))
        V(V.last)
        V.done(V.eng.tensor_tensor(s[:, 4:8], a[0], s[:, 0:4], ALU.subtract))
        m = V.done(V.eng.tensor_tensor(s[:, 8:12], a[1], s[:, 0:4], ALU.subtract))
        A(m)
        m = A.done(A.eng.activation(s[:, 4:12], s[:, 4:12], ACT.Exp))
        V(m)
        V.done(V.eng.tensor_tensor(s[:, 12:16], s[:, 4:8], s[:, 8:12], ALU.add))
        V(V.last)
        V.done(V.eng.reciprocal(s[:, 12:16], s[:, 12:16]))
        V(V.last)
        V.done(V.eng.tensor_tensor(s[:, 4:8], s[:, 4:8], s[:, 12:16], ALU.mult))
        V.done(V.eng.tensor_tensor(s[:, 8:12], s[:, 8:12], s[:, 12:16], ALU.mult))
        V(V.last)
        V.done(V.eng.tensor_tensor(s[:, 16:20], s[:, 4:8], s[:, 8:12], ALU.add))
        V.done(V.eng.tensor_tensor(self.lb[:, 0, :], s[:, 4:8], s[:, 4:8], ALU.subtract))
        V(V.last)
        V.done(V.eng.tensor_tensor(self.lb[:, 1, :], s[:, 16:20], s[:, 4:8], ALU.subtract))

    def layer_vectors(self, l):
        p, V, G, ins = self.prog, self.V, self.G, self.ins
        par, ds = self.par, bass.ds
        qk = [(self.qkg[:, k, :], ins[n][ds(l, 1), :].broadcast_to((P, HD)))
              for k, n in enumerate(("qn_dsa", "kn_dsa"))]
        og = [(self.og[h * HD:(h + 1) * HD, :], ins["hgrn_onorm"][ds(l, 1), :].rearrange("a d -> d a"))
              for h in range(2)]
        self.m_lv = p.dma(G, "layer_vectors", qk + og)
        V.done(V.eng.tensor_copy(self.gcur[:, 0:ND], par[:, 0, ds(self.col["norm_mix"] + l * ND, ND)]))
        V.done(V.eng.tensor_copy(self.gcur[:, ND:], par[:, 0, ds(self.col["norm_mlp"] + l * ND, ND)]))
        V.done(V.eng.tensor_copy(self.lbc[:, 0, :], self.lb[:, ds(l, 1), :].rearrange("p a b -> p (a b)")))
        V(V.last)
        self.m_cur = V.done(V.eng.tensor_scalar(self.lbc[:, 1, :], self.lbc[:, 0, :], -1.0, 1.0, ALU.mult, ALU.add))

    def held_back(self, t, *marks):
        G = self.G
        G(*marks, self.m_idle)
        self.m_idle = G.done(G.eng.tensor_tensor(t, t, t, ALU.add))


    def sb_scores(self, c):
        PE, A, V, p = self.PE, self.A, self.V, self.prog
        PE(self.m_sqk)
        i, ps = p.take()
        for h in range(2):
            r = slice(h * HD, (h + 1) * HD)
            PE.eng.matmul(ps[:, h, 0:T], self.skT[r, c, 0:P], self.sqT[r, c, :], start=True,
                          stop=False, skip_group_check=True)
            last = PE.eng.matmul(ps[:, h, T:T + P], self.skT[r, c, P:T], self.sqT[r, c, P:T],
                                 start=False, stop=False, skip_group_check=True)
        m = PE.done(last)
        z = ps[:, :, 0:384]
        e = self.big1[:, 3 * (c % 2):3 * (c % 2) + 3, :].rearrange("p a b -> p (a b)").rearrange("p (h n) -> p h n", h=2)
        A(m, self.sb_free[c % 2])
        for f, src, kw in ((ACT.Abs, z, {}), (ACT.Exp, e, {"scale": -1.0}), (ACT.Ln, e, {"bias": 1.0})):
            m = A.done(A.eng.activation(e, src, f, **kw))
            A(m)
        V(m, self.m_c1)
        V.done(V.eng.scalar_tensor_tensor(out=e, in0=z, scalar=0.0, in1=e, op0=ALU.max, op1=ALU.add))
        V(V.last)
        for h in range(2):
            d = e[:, h, :].rearrange("p (a b) -> p a b", a=3)[:, 0:3:2, :]
            m = V.done(V.eng.tensor_tensor(d, d, self.strict[:, :].unsqueeze(1).broadcast_to((P, 2, P)),
                                           ALU.mult))
        self.sb_state[c] = (i, ps, e, m)

    def sb_weights(self, c):
        PE, A, G = self.PE, self.A, self.G
        i, ps, e, m = self.sb_state[c]
        PE(m, self.m_set1)
        for h in range(2):
            PE.eng.matmul(ps[:, h, 0:384], self.negu[:, :], e[:, h, :], start=False, stop=False,
                          skip_group_check=True)
            last = PE.eng.matmul(ps[:, h, P:T], self.negone[:, :], e[:, h, T:384], start=False,
                                 stop=True, skip_group_check=True)
        m = PE.done(last)
        A(m)
        m = A.done(A.eng.activation(e, ps[:, :, 0:384], ACT.Exp))
        self.prog.give(i, m)
        self.held_back(self.idle[:, :], m)
        for h in range(2):
            d = e[:, h, :].rearrange("p (a b) -> p a b", a=3)[:, 0:3:2, :]
            m = G.done(G.eng.affine_select(out=d, in_=d, compare_op=ALU.is_gt, fill=0.0, base=0,
                                           pattern=[[0, 2], [1, P]], channel_multiplier=-1))
        self.sb_state[c] = (e, m)

    def sb_values(self, c, sb_oT):
        PE, p = self.PE, self.prog
        e, m = self.sb_state[c]
        PE(m, self.m_sv)
        i, ps = p.take()
        for h in range(2):
            o, f = slice(h * HD, (h + 1) * HD), slice((2 * c + h) * HD, (2 * c + h + 1) * HD)
            PE.eng.matmul(ps[o, h, 0:T], self.sv[:, 0, f], e[:, h, 0:T], start=True, stop=False,
                          skip_group_check=True)
            last = PE.eng.matmul(ps[o, h, P:T], self.sv[:, 1, f], e[:, h, T:384], start=False,
                                 stop=True, skip_group_check=True)
        m = PE.done(last)
        self.sb_free[c % 2] = m
        for h in range(2):
            o = slice(h * HD, (h + 1) * HD)
            m = self.copy(sb_oT[o, c, :], ps[o, h, 0:T], m, self.V)
        p.give(i, m)
        return m

    def branch(self, k, w, nrow, oT, after):
        PE, V, G, p = self.PE, self.V, self.G, self.prog
        u = None
        if k == 2:
            u = self.unit(w, nrow, D)
            yield
        for f in range(0, ND, 4):
            if f:
                yield
            if f == 0:
                PE(*after())
                u = u or self.unit(w, nrow, D)
            i, ps = p.take()
            for q in range(4):
                for r in range(nrow):
                    last = PE.eng.matmul(ps[:, q // 2, (q % 2) * T:(q % 2) * T + T],
                                         u[:, r, (f + q) * P:(f + q + 1) * P], oT[:, r, :],
                                         start=r == 0, stop=r == nrow - 1)
            m = PE.done(last, p.used if f + 4 == ND else None)
            V(m, self.m_gate)
            y = ps.rearrange("p a (b t) -> p (a b) t", t=T)
            g = self.gate[:, k * ND + f:k * ND + f + 4, :]
            if k == 0:
                m = V.done(V.eng.tensor_tensor(self.mixT[:, f:f + 4, :], y, g, ALU.mult))
            else:
                m = V.done(V.eng.tensor_tensor(g, y, g, ALU.mult))
                E = G if k == 1 else V
                E(m, self.m_mix.get(f))
                m2 = self.m_mix[f] = E.done(E.eng.tensor_tensor(self.mixT[:, f:f + 4, :], self.mixT[:, f:f + 4, :], g, ALU.add))
            p.give(i, m)
        yield m if k == 0 else m2


    def dsa_rows(self):
        V, G = self.V, self.G
        d = self.dsa
        qk = d[:, :, 0:448].rearrange("p a (h e) -> p a h e", e=HD)
        sq = self.big2[:, 0:4, :].rearrange("p a b -> p (a b)")[:, 0:896]
        sq4 = sq.rearrange("p (a h e) -> p a h e", a=2, e=HD)
        V(self.m_dsa, self.m_lv)
        V.done(V.eng.tensor_tensor(sq4, qk, qk, ALU.mult))
        V(V.last)
        m = V.done(V.eng.tensor_reduce(self.small[:, 0:14], sq.rearrange("p (x e) -> p x e", e=HD), AX, ALU.add))
        m = self.rstd(self.small[:, 0:14], HD, self.small[:, 16:30], m)
        V(m)
        r = self.small[:, 16:30].rearrange("p (a h) -> p a h", a=2)
        for tt in range(NT):
            V.done(V.eng.tensor_tensor(qk[:, tt], qk[:, tt], r[:, tt].unsqueeze(2).broadcast_to((P, 7, HD)), ALU.mult))
        V(V.last)
        for tt in range(NT):
            V.done(V.eng.tensor_tensor(qk[:, tt, 0:6], qk[:, tt, 0:6],
                                       self.qkg[:, 0, :].unsqueeze(1).broadcast_to((P, 6, HD)), ALU.mult))
            V.done(V.eng.tensor_tensor(qk[:, tt, 6], qk[:, tt, 6], self.qkg[:, 1, :], ALU.mult))
        V.done(V.eng.tensor_scalar(d[:, :, 1088:1096], d[:, :, 1088:1096], IDX_SCALE, None, ALU.mult))
        V(V.last)
        blocks = d[:, :, 0:NBLK * HD].rearrange("p a (k e) -> p a k e", e=HD)
        n = NBLK * 8
        for tt in range(NT):
            x1, x2 = blocks[:, tt, :, 0:8], blocks[:, tt, :, 8:16]
            cs, sn = (t[:, tt, :].rearrange("p (k e) -> p k e", e=8) for t in (self.rc, self.rsn))
            t = [self.rot[:, k, 0:n].rearrange("p (k e) -> p k e", e=8) for k in range(4)]
            V.done(V.eng.tensor_tensor(t[0], x1, cs, ALU.mult))
            V.done(V.eng.tensor_tensor(t[1], x2, sn, ALU.mult))
            V.done(V.eng.tensor_tensor(t[2], x2, cs, ALU.mult))
            V.done(V.eng.tensor_tensor(t[3], x1, sn, ALU.mult))
            V(V.last)
            V.done(V.eng.tensor_tensor(x1, t[0], t[1], ALU.subtract))
            m = V.done(V.eng.tensor_tensor(x2, t[2], t[3], ALU.add))
            V(m)
        dup = sq[:, 0:512].rearrange("p (a k h e) -> p a k h e", a=2, k=2, h=2)
        for tt in range(NT):
            for k, at in ((0, 384), (1, 1024)):
                m = V.done(V.eng.tensor_copy(dup[:, tt, k], d[:, tt, at:at + HD].unsqueeze(1).broadcast_to((P, 2, HD))))
        self.dup = dup
        self.m_rows = m

    def dsa_turn(self):
        PE, p, d = self.PE, self.prog, self.dsa
        PE(self.m_rows)
        dup = self.dup

        def src(j, tt):
            if j < 3:
                return d[:, tt, j * P:(j + 1) * P]
            if j in (3, 8):
                return dup[:, tt, 0 if j == 3 else 1].rearrange("p h e -> p (h e)")
            return d[:, tt, 512 + (j - 4) * P:512 + (j - 3) * P]
        order = [4, 5, 6, 7, 8, 0, 1, 2, 3]
        for g in range(0, 9, 4):
            js = order[g:g + 4]
            i, ps = p.take()
            for q, j in enumerate(js):
                for tt in range(NT):
                    last = PE.eng.transpose(ps[:, q // 2, (q % 2) * T + tt * P:(q % 2) * T + tt * P + P],
                                            src(j, tt), self.ident[:, :])
            m = PE.done(last)
            flat = ps.rearrange("p a (b t) -> p (a b) t", t=T)
            done = []
            q = 0
            while q < len(js):
                n = 1
                while q + n < len(js) and js[q + n] == js[q] + n:
                    n += 1
                done.append(self.copy(self.dT[:, js[q]:js[q] + n, :], flat[:, q:q + n, :], m))
                q += n
            p.give(i, *done)
        self.m_dT = done[-1]

    def dsa_index(self, tt):
        PE, A, V, G, p = self.PE, self.A, self.V, self.G, self.prog
        n = (tt + 1) * P
        PE(self.m_dT)
        sc = self.score[:, tt, 0:n]
        hs = 4 if tt else 8
        first = True
        for h0 in range(0, N_IDX, hs):
            i, ps = p.take()
            for j in range(h0, h0 + hs):
                r = slice((j % 2) * HD, (j % 2 + 1) * HD)
                k = (j - h0) // 2
                last = PE.eng.matmul(ps[:, j % 2, k * n:(k + 1) * n],
                                     self.dT[r, 4 + j // 2, tt * P:(tt + 1) * P], self.dT[r, 8, 0:n],
                                     start=True, stop=True)
            m = PE.done(last)
            rel = self.big1[:, 0:4, :].rearrange("p a b -> p (a b)")
            A(m, self.m_rel)
            m = A.done(A.eng.activation(rel, ps.rearrange("p a b -> p (a b)"), ACT.Relu))
            p.give(i, m)
            V(m)
            for j in range(h0, h0 + hs):
                k = (j % 2) * (hs // 2) + (j - h0) // 2
                w = self.dsa[:, tt, 1088 + j:1089 + j]
                if first:
                    m = V.done(V.eng.tensor_scalar(sc, rel[:, k * n:(k + 1) * n], w, None, ALU.mult))
                else:
                    V(m)
                    m = V.done(V.eng.scalar_tensor_tensor(out=sc, in0=rel[:, k * n:(k + 1) * n], scalar=w, in1=sc,
                                                          op0=ALU.mult, op1=ALU.add))
                first = False
            self.m_rel = m
        self.held_back(self.idle[:, :], m)
        self.m_sc[tt] = G.done(G.eng.affine_select(out=sc, in_=sc, compare_op=ALU.is_ge, fill=NEG, base=tt * P,
                                                   pattern=[[-1, n]], channel_multiplier=1))

    def dsa_select(self):
        V = self.V
        step = self.topk_step
        V.eng.sem_clear(step)
        V(*self.m_sc)
        V.done(V.eng.tensor_copy(self.idle_v[:, :], self.score[:, 0, 0:1]))
        n_step = 0
        for r in range(K_TOP // 8):
            src = self.score if r == 0 else self.work
            for tt in range(NT):
                if r:
                    V.eng.wait_ge(step, n_step - 1)
                V.eng.max(out=self.top8[:, tt, :], in_=src[:, tt, 0:(tt + 1) * P]).then_inc(step, 1)
                n_step += 1
            for tt in range(NT):
                n = (tt + 1) * P
                V.eng.wait_ge(step, n_step - 1)
                V.eng.match_replace(out=self.work[:, tt, 0:n], in_to_replace=self.top8[:, tt, :],
                                    in_values=src[:, tt, 0:n], imm_value=TINY).then_inc(step, 1)
                n_step += 1
        V.eng.wait_ge(step, n_step)
        for tt in range(NT):
            n = (tt + 1) * P
            w, s = self.work[:, tt, 0:n], self.score[:, tt, 0:n]
            V.done(V.eng.tensor_scalar(w, w, 2 * NEG, None, ALU.is_lt))
            V(V.last)
            V.done(V.eng.scalar_tensor_tensor(out=w, in0=s, scalar=0.5 * NEG, in1=w, op0=ALU.is_gt, op1=ALU.mult))
            V(V.last)
            m = V.done(V.eng.tensor_scalar(w, w, -NEG, NEG, ALU.mult, ALU.add))
        self.m_bias = m

    def dsa_attend(self, tt):
        PE, A, V, p = self.PE, self.A, self.V, self.prog
        n = (tt + 1) * P
        bias = self.work[:, tt, 0:n]
        lg = self.big1[:, :, 0:n] if tt else self.big1[:, 0:3, :].rearrange("p a (b n) -> p (a b) n", n=P)
        slots = [0, 2, 1, 3, 4, 5] if tt else [0, 2, 4, 1, 3, 5]
        PE(self.m_dT)
        V(self.m_bias, self.m_lg)
        for group in ([[0, 2, 1, 3], [4, 5]] if tt else [[0, 2, 4, 1, 3, 5]]):
            i, ps = p.take()
            k = len(group) // 2
            for q, h in enumerate(group):
                r = slice((h % 2) * HD, (h % 2 + 1) * HD)
                last = PE.eng.matmul(ps[:, h % 2, (q % k) * n:(q % k + 1) * n],
                                     self.dT[r, h // 2, tt * P:(tt + 1) * P], self.dT[r, 3, 0:n], start=True, stop=True)
            m = PE.done(last)
            V(m)
            for b in range(2):
                s0 = slots.index(group[b * k])
                m = V.done(V.eng.scalar_tensor_tensor(
                    out=lg[:, s0:s0 + k, :], in0=ps[:, b, 0:k * n].rearrange("p (a n) -> p a n", n=n),
                    scalar=HD ** -0.5, in1=bias.unsqueeze(1).broadcast_to((P, k, n)), op0=ALU.mult, op1=ALU.add))
            p.give(i, m)
        V(V.last)
        s = self.small
        V.done(V.eng.tensor_reduce(s[:, 32:38], lg, AX, ALU.max))
        V(V.last)
        m = V.done(V.eng.tensor_scalar(s[:, 32:38], s[:, 32:38], -1.0, None, ALU.mult))
        A(m)
        for h in range(6):
            m = A.done(A.eng.activation(lg[:, h, :], lg[:, h, :], ACT.Exp, bias=s[:, 32 + h:33 + h],
                                        accum_out=s[:, 40 + h:41 + h]))
        V(m)
        V.done(V.eng.reciprocal(s[:, 40:46], s[:, 40:46]))
        V(V.last)
        m = V.done(V.eng.tensor_tensor(lg, lg, s[:, 40:46].unsqueeze(2).broadcast_to((P, 6, n)), ALU.mult))
        self.fill()
        PE(m)
        for kt in range(tt + 1):
            i, ps = p.take()
            for h in range(6):
                last = PE.eng.transpose(ps[:, h % 2, (h // 2) * P:(h // 2 + 1) * P],
                                        lg[:, slots.index(h), kt * P:(kt + 1) * P], self.ident[:, :])
            m = PE.done(last)
            A(self.m_pt)
            m = self.copy(self.ptv(kt), ps[:, :, 0:384], m)
            p.give(i, m)
        self.m_lg = m
        PE(m)
        i, ps = p.take()
        for b in range(2):
            for kt in range(tt + 1):
                last = PE.eng.matmul(ps[b * HD:(b + 1) * HD, b, 0:384], self.dsa[:, kt, 448:512], self.ptv(kt)[:, b, :],
                                     start=kt == 0, stop=kt == tt)
        m = PE.done(last)
        self.m_pt = m
        for b in range(2):
            m = self.copy(self.dsa_oT[b * HD:(b + 1) * HD, :, tt * P:(tt + 1) * P],
                          ps[b * HD:(b + 1) * HD, b, 0:384].rearrange("p (a n) -> p a n", n=P), m, self.V)
        p.give(i, m)
        return m

    def ptv(self, kt):
        return self.big2[:, 3 * kt:3 * kt + 3, :].rearrange("p a b -> p (a b)").rearrange("p (h n) -> p h n", h=2)


    def hg_gates(self):
        A, V = self.A, self.V
        q, k, b = self.hqT, self.hkT, self.hbT
        V(self.m_hf)
        for h in range(N_HG):
            m = V.done(V.eng.tensor_scalar(b[:, h, :], k[:, h, :], self.lbc[:, 1, h:h + 1], self.lbc[:, 0, h:h + 1],
                                           ALU.mult, ALU.add))
        V(m)
        V.done(V.eng.tensor_scalar(k[:, :, :], b[:, :, :], -1.0, 1.0, ALU.mult, ALU.add))
        m = V.done(V.eng.tensor_scalar(self.hw[:, :, :], b[:, :, :], F_MIN, None, ALU.max))
        A(m)
        m = A.done(A.eng.activation(self.hw[:, :, :], self.hw[:, :, :], ACT.Ln))
        V(m, self.m_set1)
        for h in range(N_HG):
            m = V.done(V.eng.tensor_tensor_scan(b[:, h, :], self.ones[:, :], self.hw[:, h, :], 0.0, ALU.mult, ALU.add))
        self.m_b = m

    def hg_level(self, m_, w, free):
        A, V = self.A, self.V

        def halves(t):
            v = t[:, :, :].rearrange("p h t -> p (h t)").rearrange("p (n a m) -> p n a m", a=2, m=m_)
            return v[:, :, 0, :], v[:, :, 1, :]
        b1, b2 = halves(self.hbT)
        e1, e2 = halves(w)
        n = N_HG * T // (2 * m_)
        ref = b1[:, :, m_ - 1:m_].broadcast_to((P, n, m_))
        V(self.m_b, free)
        V.done(V.eng.tensor_tensor(e2, b2, ref, ALU.subtract))
        m = V.done(V.eng.tensor_tensor(e1, ref, b1, ALU.subtract))
        A(m)
        m = A.done(A.eng.activation(w[:, :, :], w[:, :, :], ACT.Exp))
        V(m)
        V.done(V.eng.tensor_tensor(e2, e2, halves(self.hqT)[1], ALU.mult))
        return V.done(V.eng.tensor_tensor(e1, e1, halves(self.hkT)[0], ALU.mult))

    def hg_big(self):
        PE, V, p = self.PE, self.V, self.prog
        for m_ in HG_LEVELS[:3]:
            w = (self.hw, self.hw2)[m_ == 64]
            m = self.hg_level(m_, w, self.hw_free[m_ == 64])
            self.fill()
            PE(m)
            i, ps = p.take()
            outs = []
            for s0 in range(0, T, 2 * m_):
                st, r = s0 // P, s0 % P
                t0 = s0 + m_
                col = t0 if st == 0 else T + t0 - P
                for h in range(N_HG):
                    last = PE.eng.matmul(ps[r:r + m_, st, h * P:h * P + m_], w[:, h, s0:s0 + m_], w[:, h, t0:t0 + m_],
                                         start=True, stop=True)
                outs.append((st, r, col))
            m = PE.done(last)
            self.hw_free[m_ == 64] = m
            V(m, self.m_att0)
            for st, r, col in outs:
                m = V.done(V.eng.tensor_copy(self.att[r:r + m_, :, col:col + m_],
                                             ps[r:r + m_, st, :].rearrange("p (h n) -> p h n", n=P)[:, :, 0:m_]))
            p.give(i, m)

    def hg_small(self):
        PE, V, p = self.PE, self.V, self.prog
        part = self.gatebuf
        for g in range(0, len(MASKED), 3):
            i, ps = p.take()
            j = None
            for q, m_ in enumerate(MASKED[g:g + 3]):
                if m_:
                    k = q % 2
                    w = (self.hw, self.hw2)[k]
                    m = self.hg_level(m_, w, self.hw_free[k])
                    self.fill()
                    PE(m)
                    lw = rw = w
                else:
                    lw, rw = self.hkT, self.hqT
                    PE(self.m_b, self.m_hq)
                if q == 2:
                    j, ps2 = p.take()
                bank = ps[:, q, :] if q < 2 else ps2[:, 0, :]
                for h in range(N_HG):
                    for blk in range(T // 32):
                        r = 32 * (blk % 4)
                        col = h * 64 + (blk // 4) * 32
                        t = slice(blk * 32, blk * 32 + 32)
                        last = PE.eng.matmul(bank[r:r + 32, col:col + 32], lw[:, h, t], rw[:, h, t], start=True, stop=True)
                m = PE.done(last)
                if m_:
                    self.hw_free[k] = m
                V(m)
                lv = g + q
                m = V.done(V.eng.tensor_tensor(
                    part[:, lv, 0:256].rearrange("p (x t) -> p x t", t=32),
                    bank[:, 0:256].rearrange("p (x t) -> p x t", t=32),
                    self.lvl[:, lv, :].unsqueeze(1).broadcast_to((P, 8, 32)), ALU.mult))
            p.give(i, m)
            p.give(j, m)
        V(V.last)
        for lv in range(1, len(MASKED)):
            V.done(V.eng.tensor_tensor(part[:, 0, 0:256], part[:, 0, 0:256], part[:, lv, 0:256], ALU.add))
            V(V.last)
        for r in range(4):
            q = slice(32 * r, 32 * r + 32)
            for st in range(2):
                col = 32 * r + (T if st else 0)
                m = V.done(V.eng.tensor_copy(self.att[q, :, col:col + 32],
                                             part[q, 0, 0:256].rearrange("p (h a t) -> p h a t", a=2, t=32)[:, :, st, :]))
        self.m_att = m

    def hg_out(self):
        PE, A, V, p = self.PE, self.A, self.V, self.prog
        self.fill()
        PE(self.m_att, self.m_hvg)
        i, ps = p.take()
        for tt in range(NT):
            for h in range(N_HG):
                for kt in range(tt + 1):
                    col = tt * P if kt == 0 else T
                    last = PE.eng.matmul(ps[:, tt, h * HD:(h + 1) * HD], self.att[:, h, col:col + P],
                                         self.hvg[:, kt, h * HD:(h + 1) * HD], start=kt == 0, stop=kt == tt)
        m = PE.done(last)
        o, sq = self.hw[:, 0:2, :], self.hw2[:, 0:2, :]
        A(m, self.hw_free[0], self.hw_free[1])
        m2 = A.done(A.eng.activation(o, ps[:, :, 0:256], ACT.Copy))
        m = A.done(A.eng.activation(sq, ps[:, :, 0:256], ACT.Square))
        p.give(i, m)
        V(m)
        s = self.small
        m = V.done(V.eng.tensor_reduce(s[:, 48:56], sq.rearrange("p a (h e) -> p (a h) e", e=HD), AX, ALU.add))
        m = self.rstd(s[:, 48:56], HD, s[:, 56:64], m)
        V(m)
        o3 = o.rearrange("p a (h e) -> p (a h) e", e=HD)
        V.done(V.eng.tensor_tensor(o3, o3, s[:, 56:64].unsqueeze(2).broadcast_to((P, 8, HD)), ALU.mult))
        V(V.last)
        m = V.done(V.eng.tensor_tensor(o, o, self.hvg[:, :, 256:512], ALU.mult))
        self.fill()
        PE(m)
        i, ps = p.take()
        for c in range(2):
            for tt in range(NT):
                last = PE.eng.transpose(ps[:, 0, c * T + tt * P:c * T + tt * P + P], o[:, tt, c * P:(c + 1) * P], self.ident[:, :])
        m = PE.done(last)
        m = self.copy(self.hg_oT[:, :, :].rearrange("p a b -> p (a b)"), ps[:, 0, :], m, self.A, scale=self.og[:, 0:1])
        p.give(i, m)
        return m

    def split(self, src, hi, lo, *after, engine=None):
        A, V = self.A, engine or self.V
        A(*after)
        a = A.done(A.eng.activation(hi, src, ACT.Copy))
        V(*after, a)
        v = V.done(V.eng.tensor_tensor(lo, src, hi.bitcast(F32), ALU.subtract))
        return a, v

    def piece(self, src, m, end):
        k = self.n_piece % PIECES
        self.n_piece += 1
        _, a, b = src.shape
        hi, lo = (t[:, k, 0:a * b].rearrange("p (a b) -> p a b", a=a) for t in (self.w_hi, self.w_lo))
        return hi, lo, self.split(src, hi, lo, m, self.piece_free[k], engine=self.lo_engine), k, end

    def dense_pieces(self, l, ds):
        for name, chunks, rows in (("w_out", ND, True), ("w_up", D_FF // P, False), ("w_down", D_FF // P, True)):
            w = self.ins[name][ds(l, 1), :, :].rearrange("a d n -> (a d) n")
            for c0 in range(0, chunks, 3):
                n = min(3, chunks - c0)
                cols = slice(c0 * P, (c0 + n) * P)
                u, m = self.prog.unit(w[cols, :], n, D) if rows else self.prog.unit(w[:, cols], ND, n * P)
                for c in range(n):
                    yield self.piece(u[:, c:c + 1, :] if rows else u[:, :, c * P:(c + 1) * P], m, c == n - 1)

    def in_pieces(self, w):
        for c0, n, rows in self.panels:
            u, m = self.prog.unit(w[:, c0:c0 + n], ND, n)
            if rows:
                for d in range(0, ND, 2):
                    yield self.piece(u[:, d:d + 2, :], m, d + 2 == ND)
            else:
                for c in range(0, n, P):
                    yield self.piece(u[:, :, c:c + P], m, c + P == n)

    def next_piece(self, panel=None):
        if panel and self.noting and panel not in self.panels:
            self.panels.append(panel)
        if not self.in_hand:
            self.in_hand.append(next(self.more_pieces))
        piece = self.in_hand.pop(0)
        self.PE(*piece[2])
        return piece

    def release(self, piece, last, refill=True):
        m = self.PE.done(last, self.prog.used if piece[4] else None)
        self.piece_free[piece[3]] = m
        if refill:
            self.refill()
        return m

    def refill(self):
        if not self.noting:
            self.in_hand += [q for q in (next(self.more_pieces, None),) if q]

    def start_pieces(self):
        self.in_hand = [] if self.noting else [next(self.more_pieces) for _ in range(PIECES)]

    def split_half(self, xT, k, marks):
        at = slice(k * ND // 2, (k + 1) * ND // 2)
        return self.split(xT[:, at, :], self.xT_hi[:, at, :], self.xT_lo[:, at, :], *marks)

    def split_x(self, xT, early):
        self.m_halves = [self.split_half(xT, 0, early), self.split_half(xT, 1, self.xT_late)]

    def split_T(self, c0, cols, evacuate):
        PE, p = self.PE, self.prog
        n = cols // P
        i, ps = p.take()
        for c in range(n):
            piece = self.next_piece((c0, cols, False))
            o = ps[:, c // 2, (c % 2) * T:(c % 2) * T + T]
            for d in range(ND):
                PE(*self.m_halves[d // (ND // 2)])
                last = self.passes(o, [t[:, d, :] for t in piece[:2]], (self.xT_hi[:, d, :], self.xT_lo[:, d, :]),
                                   d == 0, d == ND - 1)
            m = self.release(piece, last)
        p.give(i, *evacuate(n, ps.rearrange("p a (b t) -> p (a b) t", t=T)[:, 0:n, :], m))

    def split_rows(self, c0, cols, evacuate):
        PE, p = self.PE, self.prog
        i, ps = p.take()
        for d0 in range(0, ND, 2):
            piece = self.next_piece((c0, cols, True))
            PE(*self.m_halves[d0 // (ND // 2)])
            for d in range(2):
                for tt in range(NT):
                    x = [t[:, d0 + d, tt * P:(tt + 1) * P] for t in (self.xT_hi, self.xT_lo)]
                    last = self.passes(ps[:, tt, 0:cols], x, [t[:, d, :] for t in piece[:2]],
                                       d0 + d == 0, d0 + d == ND - 1)
            m = self.release(piece, last)
        p.give(i, *evacuate(ps[:, :, 0:cols], m))

    def passes(self, out, w, x, start, stop):
        mm = self.PE.eng.matmul
        mm(out, w[0], x[0], start=start, stop=False)
        mm(out, w[0], x[1], start=False, stop=False)
        return mm(out, w[1], x[0], start=False, stop=stop)

    def mlp(self):
        PE, A, V, p = self.PE, self.A, self.V, self.prog
        xn = self.normed_rows(self.x, self.xn, *self.m_xs)
        self.refill()
        early = self.turned(self.xn, self.xT, self.gcur[:, ND:], *xn)
        self.split_x(self.xT, early)
        hid_marks, held, free = [], [], [None, None]

        def release(piece, last):
            m = self.release(piece, last)
            for f in held:
                f()
            held.clear()
            return m
        for n, c0 in enumerate(range(0, D_FF // P, 3)):
            w = min(3, D_FF // P - c0)
            i, ps = p.take()
            for c in range(w):
                piece = self.next_piece()
                o = ps[:, c // 2, (c % 2) * T:(c % 2) * T + T]
                for d in range(ND):
                    PE(*self.m_halves[d // (ND // 2)])
                    last = self.passes(o, [t[:, d, :] for t in piece[:2]], (self.xT_hi[:, d, :], self.xT_lo[:, d, :]),
                                       d == 0, d == ND - 1)
                m = release(piece, last)
            t = self.units[:, n % 2, 0:w, :]
            A(m, free[n % 2])
            a = A.done(A.eng.activation(t, ps.rearrange("p a (b t) -> p (a b) t", t=T)[:, 0:w, :], ACT.Relu))
            p.give(i, a)
            V(a)
            v = V.done(V.eng.tensor_tensor(t, t, t, ALU.mult))

            def rest(n=n, t=t, at=slice(c0, c0 + w), v=v):
                ms = self.split(t, self.hid_hi[:, at, :], self.hid_lo[:, at, :], v)
                free[n % 2] = ms[1]
                hid_marks.append(ms)
            held.append(rest)
        for f in held:
            f()
        held.clear()
        self.sum_parts(D_FF // P, self.hid_hi, self.hid_lo, lambda k: hid_marks[k // 3])
        self.sqrt_table()

    def sum_parts(self, n, lhs_hi, lhs_lo, ready):
        PE, V, p = self.PE, self.V, self.prog
        i, pa = p.take()
        j, pb = p.take()
        pair = (pa, pb)
        for k in range(n):
            piece = self.next_piece()
            PE(*ready(k))
            for tt in range(NT):
                x = [t[:, k, tt * P:(tt + 1) * P] for t in (lhs_hi, lhs_lo)]
                for b in range(2):
                    last = self.passes(pair[tt][:, b, :], x, [t[:, 0, b * 512:(b + 1) * 512] for t in piece[:2]],
                                       k == 0, k == n - 1)
                if tt == 0 and k == n - 1:
                    m0 = PE.done(last)
            m1 = self.release(piece, last, refill=k < n - 1)
        self.m_xs = []
        for tt, (slot, m) in enumerate(((i, m0), (j, m1))):
            V(m)
            m = V.done(V.eng.tensor_tensor(self.x[:, tt, :], self.x[:, tt, :],
                                           pair[tt].rearrange("p a b -> p (a b)"), ALU.add))
            p.give(slot, m)
            self.m_xs.append(m)

    def block1(self):
        p, ins, A, V, PE = self.prog, self.ins, self.A, self.V, self.PE
        self.block1_memory()
        A(self.m_x, self.m_par)
        V(self.m_x)
        p.sp(self.m_x)
        ds = bass.ds
        self.noting = "panels" not in p.per_iteration
        self.panels = p.per_iteration.setdefault("panels", [])
        self.topk_step = p.nc.alloc_semaphore("topk_step")
        with p.loop_of("layers", DEPTH) as l:
            noting = self.noting
            with self.scope(meet=False):
                self.mixer_memory()
                self.mixers(l, ds)
            with self.scope(meet=False):
                self.mlp_memory()
                self.sum_parts(ND, self.xT_hi, self.xT_lo, lambda k: self.m_halves[k // (ND // 2)])
                self.mlp()
                self.noting = noting

    def mixers(self, l, ds):
        p, ins, A, V, PE = self.prog, self.ins, self.A, self.V, self.PE
        self.sb_state, self.sb_free = {}, [None, None]
        self.hw_free = [None, None]
        self.m_sc = [None] * NT
        self.m_rel = self.m_lg = self.m_pt = None
        self.m_mix = {}
        xn = self.normed_rows(self.x, self.xn)
        self.layer_vectors(l)
        w = ins["w_in"][ds(l, 1), :, :].rearrange("a d n -> (a d) n")
        self.n_piece, self.piece_free = 0, [None] * PIECES
        self.lo_engine = self.G
        self.more_pieces = self.in_pieces(w)
        self.start_pieces()
        V(self.m_cur)
        A(self.m_cur)
        ready = self.turned(self.xn, self.xT, self.gcur[:, 0:ND], *xn)
        self.split_x(self.xT, ready)
        self.split_T(C_SQ, 384, self.copy_to(self.sqT, scale=HD ** -0.5))
        self.split_T(C_SK, 384, self.copy_to(self.skT))
        self.m_sqk = self.m_copy

        def evac(dst):
            def f(ps, m):
                self.m_ev = self.copy(dst, ps, m)
                return [self.m_ev]
            return f
        self.split_rows(C_SV, 384, evac(self.sv[:, :, :]))
        self.m_sv = self.m_ev
        self.sb_scores(0)
        for c in range(0, W_DSA, 384):
            n = min(384, W_DSA - c)
            self.split_rows(C_DSA + c, n, evac(self.dsa[:, :, c:c + n]))
            if c == 0:
                self.sb_weights(0)
                self.sb_scores(1)
            elif c == 384:
                self.sb_values(0, self.oT)
                self.sb_weights(1)
        self.m_dsa = self.m_ev
        self.sb_scores(2)
        self.sb_values(1, self.oT)
        self.dsa_rows()
        at = [0]

        def hqf(n, ps, m):
            A(m)
            out = []
            js = range(at[0], at[0] + n)
            at[0] += n
            for k, j in enumerate(js):
                dst = (self.hqT if j < N_HG else self.hkT)[:, j % N_HG, :]
                self.m_hf = A.done(A.eng.activation(dst, ps[:, k, :], ACT.Sigmoid))
            for k, j in enumerate(js):
                if j < N_HG:
                    V(self.m_hf)
                    dst = self.hqT[:, j, :]
                    self.m_hq = V.done(V.eng.tensor_tensor(dst, ps[:, k, :], dst, ALU.mult))
                    out = [self.m_hq]
            return out + [self.m_hf]
        for k, (c, n) in enumerate(((0, 384), (384, 384), (768, 256))):
            self.split_T(C_HQ + c, n, hqf)
            if k == 0:
                self.sb_weights(2)
            if k == 1:
                self.m_oT = self.sb_values(2, self.oT)
        self.dsa_turn()
        self.dsa_index(0)
        self.hg_gates()

        def silu_hg(ps, m):
            A(m)
            V(m)
            a = A.done(A.eng.activation(self.hvg[:, :, 256:512], ps, ACT.Sigmoid))
            V(a)
            self.m_hvg = V.done(V.eng.tensor_tensor(self.hvg[:, :, 256:512], ps, self.hvg[:, :, 256:512], ALU.mult))
            return [self.m_hvg]
        gate_at = [0]

        def gates(n, ps, m):
            A(m)
            o = self.gate[:, gate_at[0]:gate_at[0] + n, :]
            gate_at[0] += n
            self.m_gate = A.done(A.eng.activation(o, ps, ACT.Sigmoid))
            return [self.m_gate]

        def gate_unit(k):
            c, n = ((0, 384), (384, 384), (768, 256))[k % 3]
            c += C_GATE + (k // 3) * D
            self.split_T(c, n, gates)
        br = {n: ins[n][ds(l, 1), :, :].rearrange("a d n -> (a d) n") for n in ("w_br_sb", "w_br_dsa", "w_br_hgrn")}
        b_sb = self.branch(0, br["w_br_sb"], 3, self.oT, lambda: [self.m_oT])
        b_dsa = self.branch(1, br["w_br_dsa"], 3, self.dsa_oT, lambda: [self.m_dsa_oT])
        self.fillers = [lambda k=k: gate_unit(k) for k in range(9)]
        self.fillers[4:4] = [
            lambda: self.split_rows(C_HI, 256, evac(self.hvg[:, :, 0:256])),
            lambda: self.split_rows(C_HI + 256, 256, silu_hg)]
        self.fillers += [lambda: next(b_sb), lambda: next(b_sb), lambda: next(b_dsa), lambda: next(b_dsa)]
        self.fill()
        self.dsa_index(1)
        self.dsa_select()
        self.fill(2)
        self.dsa_attend(0)
        self.m_dsa_oT = self.dsa_attend(1)
        G = self.G
        self.held_back(self.idle[:, :], *[e.last for e in (PE, A, V)])
        self.m_att0 = G.done(G.eng.memset(self.att[:, :, :], 0.0))
        self.hg_big()
        self.hg_small()
        m_hg = self.hg_out()
        self.fill(len(self.fillers))
        b_hg = self.branch(2, br["w_br_hgrn"], 2, self.hg_oT, lambda: [m_hg])
        next(b_hg)
        self.more_pieces, self.noting = self.dense_pieces(l, ds), False
        self.start_pieces()
        self.lo_engine = V
        next(b_hg)
        self.m_halves = [self.split_half(self.mixT, 0, [self.m_mix[0]])]
        next(b_hg)
        self.m_halves.append(self.split_half(self.mixT, 1, [self.m_mix[4]]))


    def block2_memory(self):
        sb, p, ins, c = self.sb, self.prog, self.ins, self.c
        G, V, PE = self.G, self.V, self.PE
        self.mkT, self.mv = [None, sb("mkT1", [P, 2, T])], [None, sb("mv1", [P, NT, N_MEM * HD])]
        self.router = sb("router", [P, DEPTH, ND, N_EXP])
        self.iota = sb("iota", [P, CAP])
        self.mainT = sb("mainT", [P, ND, T])
        self.low = sb("low", [P, 3 * NM + 4, T])
        self.prob = self.flat(self.xn).rearrange("p (k h t) -> p k h t", k=2, h=4)
        self.probT = self.flat(self.xT).rearrange("p (k a h q) -> p k a h q", k=2, a=NT, h=4)
        self.st = sb("st", [P, 64])
        pairs = [(self.router[:, i], ins["router_w_2"][i].rearrange("(c p) e -> p c e", p=P)) for i in range(DEPTH)]
        self.m_c2 = p.dma(G, "consts2", pairs + [(self.iota[:, :], c["iota"])])
        self.att_free = [None, None]

    def memory_units(self):
        units = []
        for i in range(DEPTH):
            w = self.ins["w_mem_kv_2"][i]
            units.append(lambda w=w, i=i: self.project_T(w[:, 0:256], self.xT, 256, self.copy_to(self.mkT[i])))
            units.append(lambda w=w, i=i: self.project(w[:, 256:512], self.xT, 256,
                                                       lambda ps, m: [self.copy(self.mv[i][:, :, :], ps, m)]))
        return units

    def attend_steps(self, jobs):
        PE, A, V, p, scale = self.PE, self.A, self.V, self.prog, HD ** -0.5
        out, last_job = [], None
        for n, job in enumerate(jobs + [None]):
            k, was = n % 2, (n - 1) % 2
            if job:
                tt, qT, kT, v, oT = job
                i, ps = p.take()
                for h in range(4):
                    last = PE.eng.matmul(ps[:, h % 2, (h // 2) * T:(h // 2 + 1) * T], qT(h)[:, tt * P:(tt + 1) * P],
                                         kT(h), start=True, stop=True)
                m = PE.done(last)
                pr, s = self.prob[:, k], self.st
                mx, sm = s[:, 8 * k:8 * k + 4], s[:, 16 + 8 * k:20 + 8 * k]
                V(m, self.att_free[k])
                V.done(V.eng.tensor_reduce(mx, ps.rearrange("p a (b n) -> p (a b) n", n=T), AX, ALU.max))
                V(V.last)
                m_max = V.done(V.eng.tensor_scalar(mx, mx, -scale, None, ALU.mult))
            if last_job:
                tt1, v1, oT1, m = last_job
                pr1, pt = self.prob[:, was], self.probT[:, was]
                PE(m)
                j, pt_ps = p.take()
                for kt in range(NT):
                    for q in range(4):
                        last = PE.eng.transpose(pt_ps[:, kt, q * P:(q + 1) * P], pr1[:, q, kt * P:(kt + 1) * P],
                                                self.ident[:, :])
                m = self.att_free[was] = PE.done(last)
                ma = self.copy(pt[:, 0].rearrange("p h q -> p (h q)"), pt_ps[:, 0, :], m, A)
                mv = self.copy(pt[:, 1].rearrange("p h q -> p (h q)"), pt_ps[:, 1, :], m, V)
                p.give(j, ma, mv)
            if job:
                A(m_max, self.att_free[k])
                for q in range(4):
                    m = A.done(A.eng.activation(pr[:, q, :], ps[:, q // 2, (q % 2) * T:(q % 2 + 1) * T], ACT.Exp,
                                                scale=scale, bias=mx[:, q:q + 1], accum_out=sm[:, q:q + 1]))
                p.give(i, m)
                V(m)
                V.done(V.eng.reciprocal(sm, sm))
                V(V.last)
                m_prob = V.done(V.eng.tensor_tensor(pr, pr, sm.unsqueeze(2).broadcast_to((P, 4, T)), ALU.mult))
            if last_job:
                PE(ma, mv)
                j, o_ps = p.take()
                for h in range(4):
                    o = slice((h % 2) * HD, (h % 2 + 1) * HD)
                    q = (h % 2) * 2 + h // 2
                    for kt in range(NT):
                        last = PE.eng.matmul(o_ps[o, h % 2, (h // 2) * P:(h // 2 + 1) * P], v1(kt, h), pt[:, kt, q, :],
                                             start=kt == 0, stop=kt == NT - 1)
                m = PE.done(last)
                out = []
                for b, e in ((0, A), (1, V)):
                    o = slice(b * HD, (b + 1) * HD)
                    out.append(self.copy(oT1[o, :, tt1 * P:(tt1 + 1) * P],
                                         o_ps[o, b, 0:2 * P].rearrange("p (a n) -> p a n", n=P), m, e))
                p.give(j, *out)
            last_job = (tt, v, oT, m_prob) if job else None
            yield out

    def half(self, h):
        return slice((h % 2) * HD, (h % 2 + 1) * HD)

    def cross_jobs(self, i):
        return [(tt, lambda h: self.cqT[self.half(h), h // 2, :],
                 lambda h: self.mkT[i][self.half(h), h // 2, :],
                 lambda kt, h: self.mv[i][:, kt, h * HD:(h + 1) * HD], self.mainT[:, NM:NM + 2, :])
                for tt in range(NT)]

    def sine(self, ps, bias, freq, h, tmp, m):
        A, V = self.A, self.V
        big = 1.5 * 2.0 ** 23
        hi = 6.28125
        V(m)
        V.done(V.eng.tensor_scalar(h, ps, bias, freq, ALU.add, ALU.mult))
        V(V.last)
        V.done(V.eng.tensor_scalar(tmp, h, 1 / (2 * math.pi), big, ALU.mult, ALU.add))
        V(V.last)
        V.done(V.eng.tensor_scalar(tmp, tmp, big, None, ALU.subtract))
        for part in (hi, 2 * math.pi - hi):
            V(V.last)
            V.done(V.eng.scalar_tensor_tensor(out=h, in0=tmp, scalar=-part, in1=h, op0=ALU.mult, op1=ALU.add))
        V(V.last)
        lim = 3.1415925
        m = V.done(V.eng.tensor_scalar(h, h, lim, -lim, ALU.min, ALU.max))
        A(m)
        return A.done(A.eng.activation(h, h, ACT.Sin))

    def hyena_filters(self):
        p, ins, c, sb = self.prog, self.ins, self.c, self.sb
        PE, A, V, G = self.PE, self.A, self.V, self.G
        with self.scope():
            featsT = sb("featsT", [N_FEAT, T])
            w1 = sb("w1", [N_FEAT, FILT])
            w2 = sb("w2", [FILT, FILT])
            w3 = sb("w3", [FILT, 4 * D_MAIN])
            vec = sb("vec", [FILT, 3])
            streams = self.low[:, 0:3 * NM, :].rearrange("p a b -> p (a b)")
            hs = streams[:, 0:NT * NC2].rearrange("p (a n) -> p a n", a=NT)
            decay = streams[:, NT * NC2:].rearrange("p (a n) -> p a n", a=NT)
            hd = sb("hd", [P, NT, NC2])
            h1, h2 = self.cqT[0:FILT, 0, :], self.cqT[0:FILT, 1, :]
            tmp = self.mainT[0:FILT, 6, :]
            ones = self.mainT[:, 7, 0:P]
            mem = sb("mem", [P, NT, D])
            n = NT * 2 * 384
            taps, mag = (self.flat(t)[:, 0:n].rearrange("p (a d n) -> p a d n", a=NT, d=2) for t in (self.xn, mem))
            rn = self.flat(self.mainT)[:, 0:384]
            skip = self.spec_i0[0:1, :]
            left = [e.last for e in p.engines]
            m_mem = p.dma(p.sp, "mem", [(mem[:, :, :], ins["mem_2"][0].rearrange("(a p) d -> p a d", p=P))], *left)
            m = p.dma(p.sp, "filt", [
                (featsT[:, :], c["featsT"]), (w1[:, :], ins["hy_filt_w1_2"][0]), (w2[:, :], ins["hy_filt_w2_2"][0]),
                (w3[:, :], ins["hy_filt_w3_2"][0]),
                (skip, ins["hy_skip_2"].rearrange("a o c -> a (o c)"))]
                + [(vec[:, k:k + 1], ins[n].rearrange("a f -> f a")) for k, n in
                   enumerate(("hy_filt_b1_2", "hy_filt_b2_2", "hy_filt_freq_2"))])
            m_decay = p.dma(p.sp, "decay", [(decay, c["decay"])])
            self.m_dft = p.dma(p.sp, "dft", [(self.dft[:, :, :], c["dft"]), (self.idft[:, :, :], c["idft"])])
            m_ones = V.done(V.eng.memset(ones, 1.0))
            A(m_mem)
            V(m_mem)
            xn = self.normed_rows(mem, self.xn)
            A(*xn)
            PE(*self.turned(self.xn, self.xT, self.gains("mem_norm_g_2"), *xn))
            self.fillers = self.memory_units()
            PE(m)
            V(m)
            for w, src, b, dst in ((w1, featsT[:, :], 0, h1), (w2, h1, 1, h2)):
                i, ps = p.take()
                m = PE.done(PE.eng.matmul(ps[0:FILT, 0, 0:T], w[:, :], src, start=True, stop=True))
                m = self.sine(ps[0:FILT, 0, 0:T], vec[:, b:b + 1], vec[:, 2:3], dst, tmp, m)
                p.give(i, m)
                PE(m)
            PE(m_ones, self.m_dft)
            V(m_decay)
            m_mag = m_taps = None
            m_filt = []
            for o in range(ORD):
                for q in range(2):
                    blk = slice(o * D_MAIN + q * 384, o * D_MAIN + (q + 1) * 384)
                    for tt in range(NT):
                        i, ps = p.take()
                        for d in range(2):
                            at = (2 * o + d) * D_MAIN + q * 384
                            last = PE.eng.matmul(ps[:, d, 0:384], h2[:, tt * P:(tt + 1) * P], w3[:, at:at + 384],
                                                 start=True, stop=True)
                        m = PE.done(last)
                        V(m, m_taps)
                        m = V.done(V.eng.tensor_tensor(taps[:, tt], ps[:, :, 0:384],
                                                       decay[:, tt, q * 384:(q + 1) * 384].unsqueeze(1)
                                                       .broadcast_to((P, 2, 384)), ALU.mult))
                        p.give(i, m)
                        A(m, m_mag)
                        m = A.done(A.eng.activation(mag[:, tt], taps[:, tt], ACT.Abs))
                    self.fill()
                    PE(m)
                    i, ps = p.take()
                    for n in range(4):
                        last = PE.eng.matmul(ps[:, 0, 0:384], ones, mag[:, n // 2, n % 2, :], start=n == 0, stop=n == 3)
                    m = m_mag = PE.done(last)
                    V(m)
                    m = V.done(V.eng.tensor_scalar(rn, ps[:, 0, 0:384], 1e-6, None, ALU.add))
                    p.give(i, m)
                    V(m)
                    V.done(V.eng.reciprocal(rn, rn))
                    V.done(V.eng.tensor_tensor(hs[:, :, blk], taps[:, :, 0, :], taps[:, :, 1, :], ALU.add))
                    m_taps = V.done(V.eng.tensor_tensor(hd[:, :, blk], taps[:, :, 0, :], taps[:, :, 1, :], ALU.subtract))
                    V(m_taps)
                    r = rn.unsqueeze(1).broadcast_to((P, NT, 384))
                    V.done(V.eng.tensor_tensor(hs[:, :, blk], hs[:, :, blk], r, ALU.mult))
                    m = V.done(V.eng.tensor_tensor(hd[:, :, blk], hd[:, :, blk], r, ALU.mult))
                V(m)
                row = slice(o * D_MAIN, (o + 1) * D_MAIN)
                m_filt.append(V.done(V.eng.tensor_tensor(hs[0:1, 0, row], hs[0:1, 0, row], skip[:, row], ALU.add)))
            for q in range(0, 4, 2):
                PE(m_filt[q // 2])
                for fc in range(4):
                    src = hs if fc < 2 else hd
                    i, ps = p.take()
                    for b in range(2):
                        for tt in range(NT):
                            last = PE.eng.matmul(ps[:, b, 0:384], self.dft[:, tt, fc * P:(fc + 1) * P],
                                                 src[:, tt, (q + b) * 384:(q + b + 1) * 384], start=tt == 0, stop=tt == 1)
                    m = PE.done(last)
                    o = self.spec[:, fc, q * 384:(q + 2) * 384].rearrange("p (b n) -> p b n", b=2)
                    m = self.copy(o, ps[:, :, 0:384], m, A)
                    p.give(i, m)
                if q == 0:
                    A(m_taps)
                    self.m_xn = self.normed_rows(self.x, self.xn, *self.m_xs)
            V(*[e.last for e in (A, V)])
            V.done(V.eng.tensor_copy(self.spec_i0[:, :], self.spec[:, 0, :]))
            V.done(V.eng.memset(self.spec[0:1, 2, :], 0.0))
            for q in range(0, 4, 2):
                i, ps = p.take()
                for b in range(2):
                    for tt in range(NT):
                        last = PE.eng.matmul(ps[0:1, b, 0:384], self.dft[:, tt, T:T + 1],
                                             hs[:, tt, (q + b) * 384:(q + b + 1) * 384], start=tt == 0, stop=tt == 1)
                m = PE.done(last)
                V(m, V.last)
                m = V.done(V.eng.tensor_copy(self.spec_i0[0:1, q * 384:(q + 2) * 384].rearrange("p (b n) -> p b n", b=2),
                                             ps[0:1, :, 0:384]))
                p.give(i, m)

    def spectrum(self, z, zf, m):
        PE, A, V, p = self.PE, self.A, self.V, self.prog
        PE(*m)
        marks = []
        for fc in range(4):
            i, ps = p.take()
            for b in range(2):
                for tt in range(NT):
                    last = PE.eng.matmul(ps[:, b, 0:384], self.dft[:, tt, fc * P:(fc + 1) * P],
                                         z[:, tt, b * 384:(b + 1) * 384], start=tt == 0, stop=tt == 1)
            m = PE.done(last)
            m = self.copy(zf[:, fc, :].rearrange("p (b n) -> p b n", b=2), ps[:, :, 0:384], m, A)
            p.give(i, m)
            marks.append(m)
        return marks

    def filtered(self, o, zf, pf, tmp, marks):
        V, G = self.V, self.G
        sp = self.spec
        V(*marks)
        G(*marks, V.last)
        for b in range(2):
            c = slice(b * 384, (b + 1) * 384)
            k = slice(o * D_MAIN + b * 384, o * D_MAIN + (b + 1) * 384)
            for f in range(2):
                mg = G.done(G.eng.tensor_tensor(tmp[:, f, c], zf[:, 2 + f, c], sp[:, 2 + f, k], ALU.mult))
            V.done(V.eng.tensor_tensor(pf[0][:, :, c], zf[:, 0:2, c], sp[:, 0:2, k], ALU.mult))
            V.done(V.eng.tensor_tensor(pf[1][:, :, c], zf[:, 0:2, c], sp[:, 2:4, k], ALU.mult))
            V(V.last, mg)
            V.done(V.eng.tensor_tensor(pf[0][:, :, c], pf[0][:, :, c], tmp[:, :, c], ALU.subtract))
            V(V.last)
            V.done(V.eng.tensor_tensor(tmp[:, 0, c], zf[:, 2, c], self.spec_i0[:, k], ALU.mult))
            V.done(V.eng.tensor_tensor(tmp[:, 1, c], zf[:, 3, c], sp[:, 1, k], ALU.mult))
            V(V.last)
            yield V.done(V.eng.tensor_tensor(pf[1][:, :, c], pf[1][:, :, c], tmp[:, :, c], ALU.add))

    def hyena(self):
        p, ins, sb = self.prog, self.ins, self.sb
        PE, A, V, G = self.PE, self.A, self.V, self.G
        NU = 3 * NM
        ucT, self.idft = self.low[:, 0:NU, :], self.low[:, NU:NU + 4, :]
        with self.scope(meet=False):
            self.cqT = sb("cqT", [P, 2, T])
            self.mkT[0], self.mv[0] = sb("mkT0", [P, 2, T]), sb("mv0", [P, NT, N_MEM * HD])
            self.dft = sb("dft", [P, NT, 2 * T])
            self.spec = sb("spec", [P, 4, NC2])
            self.spec_i0 = sb("spec_i0", [P, NC2])
            self.hyena_filters()
            uT = sb("uT", [P, NU, T + 2])
            xv = sb("xv", [P, NT, 2 * D_MAIN])
            V.done(V.eng.memset(uT[:, :, 0:1], 0.0))
            V.done(V.eng.memset(uT[:, :, T + 1:T + 2], 0.0))
            PE(*self.turned(self.xn, self.xT, self.gains("mix_norm_g_2", 0), *self.m_xn))
            w = ins["hy_w_in_2"][0]
            sw = self.par[:, 1, :]
            uc_marks = {}

            def streams(c0):
                def f(n, ps, m):
                    m = self.copy(uT[:, c0:c0 + n, 1:T + 1], ps, m, A)
                    V(m)
                    for k in range(c0, c0 + n):
                        o = ucT[:, k, :]
                        V.done(V.eng.tensor_scalar(o, uT[:, k, 0:T], sw[:, k:k + 1], None, ALU.mult))
                    for j in (1, 2):
                        for k in range(c0, c0 + n):
                            V(V.last)
                            uc_marks[k] = V.done(V.eng.scalar_tensor_tensor(
                                out=ucT[:, k, :], in0=uT[:, k, j:j + T], scalar=sw[:, j * NU + k:j * NU + k + 1],
                                in1=ucT[:, k, :], op0=ALU.mult, op1=ALU.add))
                    return [m]
                return f
            order = [12, 15, 0, 3, 6, 9]
            for c0 in order:
                self.project_T(w[:, c0 * P:(c0 + 3) * P], self.xT, 384, streams(c0))
            chunks = list(range(NM)) + list(range(2 * NM, 3 * NM))
            xv_marks = []
            for g in (8, 4, 0):
                i, ps = p.take()
                for q in range(4):
                    k = chunks[g + q]
                    PE(uc_marks[k])
                    for tt in range(NT):
                        last = PE.eng.transpose(ps[:, tt, q * P:(q + 1) * P], ucT[:, k, tt * P:(tt + 1) * P], self.ident[:, :])
                m = PE.done(last)
                ms = [self.copy(xv[:, tt, g * P:(g + 4) * P], ps[:, tt, :], m, (A, V)[tt]) for tt in range(NT)]
                p.give(i, *ms)
                xv_marks += ms
            room = self.flat(uT)
            zf = room[:, 0:4 * D_MAIN].rearrange("p (a b) -> p a b", a=4)
            tmp = room[:, 4 * D_MAIN:6 * D_MAIN].rearrange("p (a b) -> p a b", a=2)
            pf = [ucT[:, k:k + NM, :].rearrange("p a b -> p (a b)").rearrange("p (a b) -> p a b", a=2) for k in (0, 2 * NM)]
            z = xv[:, :, D_MAIN:]
            A(*uc_marks.values())
            halves = list(self.filtered(0, zf, pf, tmp, self.spectrum(z, zf, xv_marks)))
            self.project_T(w[:, NU * P:NU * P + 256], self.xT, 256, self.copy_to(self.cqT))
            PE(self.m_copy)
            xz = []
            for b in range(2):
                PE(halves[b])
                i, ps = p.take()
                for tt in range(NT):
                    for fc in range(4):
                        last = PE.eng.matmul(ps[:, tt, 0:384], self.idft[:, fc, tt * P:(tt + 1) * P],
                                             pf[fc // 2][:, fc % 2, b * 384:(b + 1) * 384], start=fc == 0, stop=fc == 3)
                m = PE.done(last)
                V(m)
                m = V.done(V.eng.tensor_tensor(z[:, :, b * 384:(b + 1) * 384], ps[:, :, 0:384],
                                               xv[:, :, b * 384:(b + 1) * 384], ALU.mult))
                p.give(i, m)
                xz.append(m)
            cross = self.attend_steps(self.cross_jobs(0))
            next(cross)
            marks = self.spectrum(z, zf, xz)
            next(cross)
            m_cross = next(cross)
            halves = list(self.filtered(1, zf, pf, tmp, marks))

        def ready(n):
            if n == 0:
                return m_cross
            b = n - 1
            PE(halves[b])
            if b == 1:
                self.grow_ring()
            i, ps = p.take()
            for q in range(3):
                for fc in range(4):
                    last = PE.eng.matmul(ps[:, q // 2, (q % 2) * T:(q % 2) * T + T],
                                         pf[fc // 2][:, fc % 2, (3 * b + q) * P:(3 * b + q + 1) * P],
                                         self.idft[:, fc, :], start=fc == 0, stop=fc == 3)
            m = PE.done(last)
            V(m)
            m = V.done(V.eng.tensor_tensor(self.mainT[:, 3 * b:3 * b + 3, :],
                                           ps.rearrange("p a (b t) -> p (a b) t", t=T)[:, 0:3, :],
                                           ucT[:, NM + 3 * b:NM + 3 * b + 3, :], ALU.mult))
            p.give(i, m)
            return [m]
        w = ins["w_out_2"][0]
        panels = self.row_panels(w, ND, NM) + self.row_panels(w, NM)
        self.m_xs = self.accumulate(panels, self.mainT, self.x, ready)
        self.m_xn = self.normed_rows(self.x, self.xn, *self.m_xs)

    def gqa(self):
        p, ins, sb = self.prog, self.ins, self.sb
        PE, A, V, G = self.PE, self.A, self.V, self.G
        NH = N_QH + N_KV
        W = (NH + N_KV) * HD
        with self.scope(meet=False):
            self.cqT = sb("cqT", [P, 2, T])
            qkv = sb("qkv", [P, NT, W])
            gain = sb("gain", [P, 2, HD])
            cs = sb("cs", [P, NT, 2, 2, 16])
            tmp = sb("tmp3", [P, 4, 512])
            dup = sb("dup", [P, NT, N_KV, 2, HD])
            qT = sb("qT", [P, NM, T])
            kT = sb("kT", [P, N_KV, T])
            m_in = p.dma(G, "gqa", [
                (gain[:, 0, :], ins["at_q_norm_g_2"].broadcast_to((P, HD))),
                (gain[:, 1, :], ins["at_k_norm_g_2"].broadcast_to((P, HD))),
                (cs[:, :, :, :, :], self.c["axial"])])
            PE(*self.turned(self.xn, self.xT, self.gains("mix_norm_g_2", 1), *self.m_xn))
            w = ins["at_w_in_2"][0]
            V(m_in)

            def rows(c0, heads, k):
                width = heads * HD
                x = qkv[:, :, c0:c0 + width]
                x4 = x.rearrange("p t (h e) -> p t h e", e=HD)
                sq = tmp[:, 0:2, :].rearrange("p a b -> p (a b)")[:, 0:NT * width].rearrange("p (t n) -> p t n", t=NT)
                ss, rs = (self.st[:, o:o + NT * heads] for o in (32, 48))
                V(self.m_copy, V.last)
                V.done(V.eng.tensor_tensor(sq, x, x, ALU.mult))
                V(V.last)
                m = V.done(V.eng.tensor_reduce(ss.rearrange("p (t h) -> p t h", t=NT),
                                               sq.rearrange("p t (h e) -> p t h e", e=HD), AX, ALU.add))
                V(self.rstd(ss, HD, rs, m))
                V.done(V.eng.tensor_tensor(x4, x4, rs.rearrange("p (t h) -> p t h", t=NT).unsqueeze(3)
                                           .broadcast_to((P, NT, heads, HD)), ALU.mult))
                V(V.last)
                n = NT * heads
                for tt in range(NT):
                    x3 = x4[:, tt]
                    V.done(V.eng.tensor_tensor(x3, x3, gain[:, k, :].unsqueeze(1).broadcast_to((P, heads, HD)), ALU.mult))
                V(V.last)
                half = heads * HD // 2
                for tt in range(NT):
                    v = x[:, tt].rearrange("p (h a s f) -> p s h a f", a=2, s=2, f=16)
                    t = [tmp[:, j, tt * half:(tt + 1) * half].rearrange("p (h a f) -> p h a f", a=2, f=16) for j in range(4)]
                    c, s = (cs[:, tt, j].unsqueeze(1).broadcast_to((P, heads, 2, 16)) for j in range(2))
                    for j, (at, by) in enumerate(((0, c), (1, s), (0, s), (1, c))):
                        V.done(V.eng.tensor_tensor(t[j], v[:, at], by, ALU.mult))
                V(V.last)
                for tt in range(NT):
                    v = x[:, tt].rearrange("p (h a s f) -> p s h a f", a=2, s=2, f=16)
                    t = [tmp[:, j, tt * half:(tt + 1) * half].rearrange("p (h a f) -> p h a f", a=2, f=16) for j in range(4)]
                    V.done(V.eng.tensor_tensor(v[:, 0], t[0], t[1], ALU.subtract))
                    V.done(V.eng.tensor_tensor(v[:, 1], t[2], t[3], ALU.add))
                if k:
                    V(V.last)
                    for tt in range(NT):
                        V.done(V.eng.tensor_copy(dup[:, tt], x4[:, tt].unsqueeze(2).broadcast_to((P, N_KV, 2, HD))))
            for c, heads, k in ((N_QH * HD, N_KV, 1), (0, 6, 0), (384, 6, 0), (N_QH * HD + 384, 0, 0)):
                n = min(384, W - c)
                self.project(w[:, c:c + n], self.xT, n, lambda ps, m, c=c, n=n: [self.copy(qkv[:, :, c:c + n], ps, m)])
                if heads:
                    rows(c, heads, k)
            marks = [V.last]
            self.project_T(w[:, W:W + 256], self.xT, 256, self.copy_to(self.cqT))
            PE(self.m_copy)
            cross = self.attend_steps(self.cross_jobs(1))
            next(cross)
            PE(*marks)
            srcs = [lambda tt, c=c: qkv[:, tt, c * P:(c + 1) * P] for c in range(NM)]
            srcs += [lambda tt, c=c: dup[:, tt, c].rearrange("p a b -> p (a b)") for c in range(N_KV)]
            for g, n in ((0, 4), (4, 2), (6, 4)):
                i, ps = p.take()
                for q in range(n):
                    for tt in range(NT):
                        last = PE.eng.transpose(ps[:, q // 2, (q % 2) * T + tt * P:(q % 2) * T + tt * P + P], srcs[g + q](tt), self.ident[:, :])
                m = PE.done(last)
                o = qT[:, g:g + n, :] if g < NM else kT[:, g - NM:g - NM + n, :]
                m = self.copy(o, ps.rearrange("p a (b t) -> p (a b) t", t=T)[:, 0:n, :], m)
                p.give(i, m)
            next(cross)
            m_cross = next(cross)
            PE(m)
            per = N_QH // N_KV
            jobs = [(tt, lambda h, g=g: qT[self.half(h), 2 * g + h // 2, :],
                     lambda h, g=g: kT[self.half(h), (4 * g + h) // per, :],
                     lambda kt, h, g=g: qkv[:, kt, (NH + (4 * g + h) // per) * HD:(NH + (4 * g + h) // per + 1) * HD],
                     self.mainT[:, 2 * g:2 * g + 2, :]) for g in range(3) for tt in range(NT)]
        steps = self.attend_steps(jobs)
        done = []

        def ready(n):
            if n == 0:
                PE(*m_cross)
            for _ in range(2 if n == 2 else n < 6):
                done.append(next(steps))
            if n == 6:
                self.grow_ring()
            return done[2 * (n // 2)] if n > 1 else []
        w = ins["w_out_2"][1]
        panels = [p1 for c in (NM, NM + 1, 0, 1, 2, 3) for p1 in self.row_panels(w, c + 1, c)] + self.row_panels(w, NM, 4)
        self.m_xs = self.accumulate(panels, self.mainT, self.x, ready)
        self.m_xn = self.normed_rows(self.x, self.xn, *self.m_xs)

    def experts(self, i):
        p, ins, sb = self.prog, self.ins, self.sb
        PE, A, V, G = self.PE, self.A, self.V, self.G
        NG = N_EXP // 4
        self.prog.meet()
        with self.scope():
            aff = sb("aff", [P, NT, N_EXP])
            top8 = sb("top8b", [N_EXP, 8])
            slots = sb("slots", [P, NT, N_EXP])
            low, main, xT = (self.flat(t) for t in (self.low, self.mainT, self.xT))
            at = [0]

            def part(*shape):
                n = math.prod(shape)
                at[0] += n
                v = low[:, at[0] - n:at[0]]
                if len(shape) == 1:
                    return v
                names = "abc"[:len(shape)]
                return v.rearrange(f"p ({' '.join(names)}) -> p {' '.join(names)}", **dict(zip(names[:-1], shape)))
            affT, work, slot, ones = (part(T)[0:N_EXP, :] for _ in range(4))
            pick_g, share_g = part(NT, P), part(T)
            sig, hid, y, hidT = part(2, 256), part(2, 256), part(2, 512), part(2, 2, 96)
            W = N_EXP * CAP
            pick = main[:, 0:NT * W].rearrange("p (a w) -> p a w", a=NT)
            share = main[:, NT * W:2 * NT * W].rearrange("p (a w) -> p a w", a=NT)
            shareT = xT[:, 0:NG * T].rearrange("p (a t) -> p a t", a=NG)
            xgT = xT[:, NG * T:NG * T + ND * P].rearrange("p (a t) -> p a t", a=ND)
            m_ones = V.done(V.eng.memset(ones, 1.0))
            gain = self.gains("ffn_norm_g_2", i)
            PE(*self.turned(self.xn, self.xT, gain, *self.m_xn), self.m_c2)
            k, ps = p.take()
            for tt in range(NT):
                for d in range(ND):
                    if d == ND // 2:
                        PE(*self.xT_late)
                    last = PE.eng.matmul(ps[:, 0, tt * N_EXP:(tt + 1) * N_EXP], self.xT[:, d, tt * P:(tt + 1) * P],
                                         self.router[:, i, d, :], start=d == 0, stop=d == ND - 1)
            m = PE.done(last)
            s = self.st
            V(m)
            af = aff[:, :, :]
            lg = ps[:, 0, 0:NT * N_EXP].rearrange("p (a e) -> p a e", a=NT)
            V.done(V.eng.tensor_reduce(s[:, 0:NT], lg, AX, ALU.max))
            V(V.last)
            m = V.done(V.eng.tensor_tensor(af, lg, s[:, 0:NT].unsqueeze(2).broadcast_to((P, NT, N_EXP)), ALU.subtract))
            p.give(k, m)
            A(m)
            m = A.done(A.eng.activation(af, af, ACT.Exp))
            V(m)
            V.done(V.eng.tensor_reduce(s[:, 4:4 + NT], af, AX, ALU.add))
            V(V.last)
            V.done(V.eng.reciprocal(s[:, 4:4 + NT], s[:, 4:4 + NT]))
            V(V.last)
            m = V.done(V.eng.tensor_tensor(af, af, s[:, 4:4 + NT].unsqueeze(2).broadcast_to((P, NT, N_EXP)), ALU.mult))
            PE(m)
            k, ps = p.take()
            for tt in range(NT):
                last = PE.eng.transpose(ps[0:N_EXP, 0, tt * P:(tt + 1) * P], aff[:, tt, :], self.ident[:, :])
            m = PE.done(last)
            V(m)
            m = V.done(V.eng.tensor_copy(affT, ps[0:N_EXP, 0, 0:T]))
            p.give(k, m)
            for r in range(CAP // 8):
                src = affT if r == 0 else work
                V(V.last)
                V.done(V.eng.max(out=top8[:, :], in_=src))
                V(V.last)
                V.done(V.eng.match_replace(out=work, in_to_replace=top8[:, :], in_values=src, imm_value=TINY))
            V(V.last)
            V.done(V.eng.tensor_scalar(work, work, 2 * NEG, None, ALU.is_lt))
            V(V.last, m_ones)
            V.done(V.eng.tensor_tensor_scan(slot, ones, work, 0.0, ALU.mult, ALU.add))
            V(V.last)
            m = V.done(V.eng.tensor_tensor(slot, slot, work, ALU.mult))
            PE(m)
            k, ps = p.take()
            for tt in range(NT):
                last = PE.eng.transpose(ps[:, 0, tt * N_EXP:(tt + 1) * N_EXP], slot[:, tt * P:(tt + 1) * P], self.ident[0:N_EXP, 0:N_EXP])
            m = PE.done(last)
            V(m)
            m = V.done(V.eng.tensor_copy(slots[:, :, :], ps[:, 0, 0:NT * N_EXP].rearrange("p (a e) -> p a e", a=NT)))
            p.give(k, m)
            V(m, self.m_c2)
            for tt in range(NT):
                pk = pick[:, tt].rearrange("p (e r) -> p e r", r=CAP)
                V.done(V.eng.tensor_tensor(pk, slots[:, tt, :].unsqueeze(2).broadcast_to((P, N_EXP, CAP)),
                                           self.iota[:, :].unsqueeze(1).broadcast_to((P, N_EXP, CAP)), ALU.is_equal))
            V(V.last)
            for tt in range(NT):
                pk, sh = (t[:, tt].rearrange("p (e r) -> p e r", r=CAP) for t in (pick, share))
                m = V.done(V.eng.tensor_tensor(sh, pk, aff[:, tt, :].unsqueeze(2).broadcast_to((P, N_EXP, CAP)), ALU.mult))
            PE(m)
            k, ps = p.take()
            for g in range(NG):
                for tt in range(NT):
                    last = PE.eng.transpose(ps[:, g // 2, (g % 2) * T + tt * P:(g % 2) * T + tt * P + P],
                                            share[:, tt, g * P:(g + 1) * P], self.ident[:, :])
            m = PE.done(last)
            m = self.copy(shareT[:, :, :], ps.rearrange("p a (b t) -> p (a b) t", t=T), m)
            p.give(k, m)

            ds = bass.ds
            with p.loop_of(f"experts{i}", NG) as g:
                self.expert_group(i, g, ds, pick, pick_g, shareT, share_g, xgT, sig, hid, hidT, y, gain)
            p.shrink()
            self.m_xn = self.normed_rows(self.x, self.xn, *self.m_xs)

    def expert_group(self, i, g, ds, pick, pick_g, shareT, share_g, xgT, sig, hid, hidT, y, gain):
        p, ins = self.prog, self.ins
        PE, A, V = self.PE, self.A, self.V
        V.done(V.eng.tensor_copy(pick_g[:, :, :], pick[:, :, ds(g * P, P)]))
        m_sh = V.done(V.eng.tensor_copy(share_g[:, :], shareT[:, ds(g, 1), :].rearrange("p a t -> p (a t)")))
        PE(m_sh)
        k, ps = p.take()
        for d in range(ND):
            for tt in range(NT):
                last = PE.eng.matmul(ps[:, d // 4, (d % 4) * P:(d % 4 + 1) * P], self.xn[:, tt, d * P:(d + 1) * P],
                                     pick_g[:, tt, :], start=tt == 0, stop=tt == 1)
        m = PE.done(last)
        A(m)
        V(m)
        for d in range(ND):
            o, s, gn = xgT[:, d, :], ps[:, d // 4, (d % 4) * P:(d % 4 + 1) * P], gain[:, d:d + 1]
            if d < 4:
                a = A.done(A.eng.activation(o, s, ACT.Copy, scale=gn))
            else:
                v = V.done(V.eng.tensor_scalar(o, s, gn, None, ALU.mult))
        p.give(k, a, v)
        PE(a, v)
        ky, py = p.take()
        state = {}

        def up(e):
            k, ps = p.take()
            for b, name in enumerate(("exp_w_gate_2", "exp_w_up_2")):
                w = ins[name][i, ds(g * 4 + e, 1), :, :].rearrange("a d n -> (a d) n")
                for r0 in range(0, ND, 4):
                    u = self.unit(w[r0 * P:(r0 + 4) * P, :], 4, E_FF)
                    for r in range(4):
                        for j in range(3):
                            last = PE.eng.matmul(ps[32 * j:32 * j + 32, b, 0:256], xgT[:, r0 + r, 32 * e:32 * e + 32],
                                                 u[:, r, j * 256:(j + 1) * 256],
                                                 start=r0 + r == 0, stop=r0 + r == ND - 1)
                    m = PE.done(last, p.used)
                if b == 0:
                    A(m, state.get(("free", e % 2)))
                    m_sig = A.done(A.eng.activation(sig[0:96, e % 2, :], ps[0:96, 0, 0:256], ACT.Sigmoid))
                    V(m_sig)
                    V.done(V.eng.tensor_tensor(sig[0:96, e % 2, :], ps[0:96, 0, 0:256], sig[0:96, e % 2, :], ALU.mult))
            V(m, V.last, state.get(("free", e % 2)))
            m = V.done(V.eng.tensor_tensor(hid[0:96, e % 2, :], ps[0:96, 1, 0:256], sig[0:96, e % 2, :], ALU.mult))
            p.give(k, m)
            state[e] = m

        def down(e):
            PE(state[e])
            k, ps = p.take()
            for c in range(2):
                last = PE.eng.transpose(ps[:, 0, c * 96:(c + 1) * 96], hid[0:96, e % 2, c * P:(c + 1) * P], self.ident[0:96, 0:96])
            m = PE.done(last)
            state["free", e % 2] = m
            A(state.get(("t", e % 2)))
            m = self.copy(hidT[:, e % 2].rearrange("p a b -> p (a b)"), ps[:, 0, 0:192], m, A)
            p.give(k, m)
            PE(m)
            w = ins["exp_w_down_2"][i, ds(g * 4 + e, 1), :, :].rearrange("a d n -> (a d) n")
            for r0 in range(0, NM, 3):
                u = self.unit(w[r0 * P:(r0 + 3) * P, :], 3, D)
                for r in range(3):
                    j, c = (r0 + r) // 2, (r0 + r) % 2
                    for b in range(2):
                        last = PE.eng.matmul(py[32 * e:32 * e + 32, b, :], hidT[:, e % 2, c, 32 * j:32 * j + 32],
                                             u[:, r, b * 512:(b + 1) * 512], start=r0 + r == 0, stop=r0 + r == NM - 1)
                m = PE.done(last, p.used)
            state["t", e % 2] = m
            return m
        up(0)
        for e in range(1, 4):
            up(e)
            down(e - 1)
        m = down(3)
        ma = self.copy(y[:, 0, :], py[:, 0, :], m, A)
        mv = self.copy(y[:, 1, :], py[:, 1, :], m, V)
        p.give(ky, ma, mv)
        PE(ma, mv)
        self.m_xs = []
        for tt in range(NT):
            k, ps = p.take()
            for b in range(2):
                last = PE.eng.matmul(ps[:, b, :], share_g[:, tt * P:(tt + 1) * P], y[:, b, :], start=True, stop=True)
            m = PE.done(last)
            V(m)
            m = V.done(V.eng.tensor_tensor(self.x[:, tt, :], self.x[:, tt, :], ps.rearrange("p a b -> p (a b)"), ALU.add))
            p.give(k, m)
            self.m_xs.append(m)

    def block2(self):
        self.block2_memory()
        for i, mixer in enumerate((self.hyena, self.gqa)):
            with self.scope():
                mixer()
                self.experts(i)

    def finish(self):
        p, V, A = self.prog, self.V, self.A
        with self.scope():
            g = self.sb("final_gain", [P, D])
            m = p.dma(self.G, "final", [(g[:, :], self.ins["final_norm_g_2"].unsqueeze(0).broadcast_to((P, D)))])
            V(m, *self.m_xn)
            stored = Counter(p, "stored")
            out = self.out[0].rearrange("(a p) d -> p a d", p=P)
            for tt in range(NT):
                m = V.done(V.eng.tensor_tensor(self.xn[:, tt, :], self.xn[:, tt, :], g[:, :], ALU.mult))
                self.prog.sp(m)
                self.nc.sync.dma_start(out[:, tt, :], self.xn[:, tt, :]).then_inc(stored.sem, 16)
                stored.count += 16
            self.prog.sp(stored.mark())

    def run(self):
        self.setup()
        with self.scope():
            self.block1()
        self.block2()
        self.finish()
        self.room.close()


_DRAM_CONSTS = ("ident", "negu", "strict", "levels", "dsa_cos", "dsa_sin")


def constants():
    f = np.float32
    out = {"ident": np.eye(P, dtype=f)}
    s = np.arange(P)
    out["negu"] = -(s[:, None] >= s[None, :]).astype(f)
    out["strict"] = (s[:, None] < s[None, :]).astype(f)
    r = s % 32
    lv = []
    for m in MASKED:
        t = np.arange(32)
        if m:
            same = (r[:, None] // (2 * m)) == (t[None, :] // (2 * m))
            lv.append(same & (r[:, None] % (2 * m) < m) & (t[None, :] % (2 * m) >= m))
        else:
            lv.append(r[:, None] == t[None, :])
    out["levels"] = np.stack(lv, 1).astype(f)
    half = ROT // 2
    inv = f(500000.0) ** (-(np.arange(half, dtype=f) * f(2.0)) / f(ROT))
    ang = np.arange(T, dtype=f)[:, None] * inv[None, :].astype(f)
    cos, sin = (np.tile(g(ang.astype(np.float64))[:, None, :], (1, NBLK, 1)) for g in (np.cos, np.sin))
    cos[:, 7], sin[:, 7] = 1.0, 0.0
    for n, a in (("dsa_cos", cos), ("dsa_sin", sin)):
        out[n] = np.ascontiguousarray(a.reshape(NT, P, NBLK * half).transpose(1, 0, 2)).astype(f)
    out["iota"] = np.broadcast_to(np.arange(1, CAP + 1, dtype=f), (P, CAP)).copy()
    t, k = np.arange(T)[:, None], np.arange(T)[None, :]
    ph = np.pi * ((t * k) % (2 * T)) / T
    fwd = np.concatenate([np.cos(ph), -np.sin(ph)], 1)
    fwd[:, T] = (-1.0) ** np.arange(T)
    out["dft"] = np.ascontiguousarray(fwd.reshape(NT, P, 2 * T).transpose(1, 0, 2)).astype(f)
    scale = np.full(2 * T, 2.0)
    scale[0] = scale[T] = 1.0
    inv_ = (fwd * scale / (2 * T)).T
    out["idft"] = np.ascontiguousarray(inv_.reshape(4, P, T).transpose(1, 0, 2)).astype(f)
    tl = np.linspace(0.0, 1.0, T, dtype=f)[:, None]
    wl = (f(2.0 * math.pi) * np.arange(T, dtype=f)[:, None] / f(T)).astype(f)
    bands = np.linspace(1e-4, 15, 16, dtype=f)[None, :]
    bw = (bands * wl).astype(np.float64)
    out["featsT"] = np.ascontiguousarray(np.concatenate([tl, np.cos(bw), -np.sin(bw)], 1).T).astype(f)
    lo, hi = math.log(1e-2) / 1.5, math.log(1e-2) / 0.3
    dec = np.exp(-tl.astype(np.float64) * np.abs(np.linspace(lo, hi, D_MAIN, dtype=f)))
    out["decay"] = np.ascontiguousarray(dec.reshape(NT, P, D_MAIN).transpose(1, 0, 2)).astype(f)
    pos = np.stack([np.repeat(np.arange(T // 64), 64), np.tile(np.arange(64), T // 64)], 1).astype(f)
    inv2 = f(1.0) / (f(10000.0) ** (np.arange(0, 32, 2, dtype=f) / f(32)))
    an = (pos[:, :, None] * inv2).astype(f).astype(np.float64)
    ax = np.stack([np.cos(an), np.sin(an)], 1).reshape(NT, P, 2, 2, 16).transpose(1, 0, 2, 3, 4)
    out["axial"] = np.ascontiguousarray(ax).astype(f)
    return out


OUT = "out_0_dram"


def build(new_bass, arrays):
    per_iteration = {}
    for _ in range(2):
        nc = new_bass()
        aps = {n: nc.dram_tensor(n, a.shape, F32, kind="ExternalInput").ap() for n, a in arrays.items()}
        ins = {n[3:]: a for n, a in aps.items() if n.startswith("in_")}
        consts = {n[6:]: a for n, a in aps.items() if n.startswith("const_")}
        out = nc.dram_tensor(OUT, (1, T, D), F32, kind="ExternalOutput").ap()
        Kernel(nc, per_iteration, ins, consts, out).run()
    return nc


def kernel(**inputs):
    import concourse.bacc as bacc
    from concourse.bass_utils import run_bass_kernel_spmd

    arrays = {f"in_{n}": np.ascontiguousarray(a) for n, a in inputs.items()}
    arrays |= {f"const_{n}": a for n, a in constants().items()}
    nc = build(lambda: bacc.Bacc("TRN2", target_bir_lowering=False, num_devices=1), arrays)
    r = run_bass_kernel_spmd(nc, [arrays], core_ids=[0])
    return r.results[0][OUT]
```
